# Optimizing a Trainium2 kernel written in Bass

```python
import jax, jax.numpy as jnp
from jax import lax
import numpy as np

D_MODEL = 1024
BATCH = 1
SEQ = 512
DEPTH = 2
DEC_BATCH = 1
DEC_SEQ = 32
PAST_LEN = 256

CHUNK = 64
MIX_WIDTH = D_MODEL
N_SB_HEADS = 8
SB_HEAD_DIM = 64
SB_WIDTH = N_SB_HEADS * SB_HEAD_DIM
SB_QBLOCK = 128
N_A_GROUPS = 8
A_GROUP_DIM = 64
A_WIDTH = N_A_GROUPS * A_GROUP_DIM
GMLP_CHUNK = 128
IN_WIDTH = 3 * SB_WIDTH + 2 * A_WIDTH
PEER_HEADS = 8
PEER_NKEYS = 128
PEER_EXPERTS = PEER_NKEYS * PEER_NKEYS
PEER_TOPK = 16
PEER_DKEY = 128
PEER_DKEY_HALF = PEER_DKEY // 2
PEER_BLOCK = 256
PLE_DIM = 256
RMS_EPS = 1e-6

kernel_name = "stickbreak_chunkmlp_peer_streaming_step"

def rmsnorm(x, g):
    xf = x.astype(jnp.float32)
    y = xf * lax.rsqrt(jnp.mean(xf * xf, axis=-1, keepdims=True) + RMS_EPS)
    return (y * g.astype(jnp.float32)).astype(x.dtype)

def stick_breaking_block(q, k, v, q_pos, k_pos):
    z = jnp.einsum('bqhd,bkhd->bhqk', q, k).astype(jnp.float32)
    mask = k_pos[None, :] < q_pos[:, None]
    log_beta = jax.nn.log_sigmoid(z)
    log_1m = jnp.where(mask, jax.nn.log_sigmoid(-z), 0.0)
    rest = lax.cumsum(log_1m, axis=3, reverse=True) - log_1m
    w = jnp.where(mask, jnp.exp(log_beta + rest), 0.0)
    return jnp.einsum('bhqk,bkhd->bqhd', w.astype(v.dtype), v)

def spatial_gate(u, v, w_s, b_s):
    B, T, G, Dg = v.shape
    L = min(T, GMLP_CHUNK)
    mask = jnp.tril(jnp.ones((L, L), dtype=bool))
    w = jnp.where(mask[None], w_s[:, :L, :L], 0.0)
    vc = v.reshape(B, T // L, L, G, Dg)
    mix = jnp.einsum('gts,bcsgd->bctgd', w, vc) + jnp.transpose(b_s[:, :L])[None, None, :, :, None]
    return u * mix.reshape(B, T, G, Dg)

def token_mixers(xn, past_k, past_v, w_in, g_sb_out, w_s, b_s, g_a_v, g_a_out, w_out):
    B, T, _ = xn.shape
    proj = xn @ w_in
    q, k, v, u_a, v_a = jnp.split(
        proj, [SB_WIDTH, 2 * SB_WIDTH, 3 * SB_WIDTH, 3 * SB_WIDTH + A_WIDTH], axis=-1)
    q = q.reshape(B, T, N_SB_HEADS, SB_HEAD_DIM) * (SB_HEAD_DIM ** -0.5)
    k = k.reshape(B, T, N_SB_HEADS, SB_HEAD_DIM)
    v = v.reshape(B, T, N_SB_HEADS, SB_HEAD_DIM)
    if past_k is None:
        k_all, v_all, P = k, v, 0
    else:
        k_all = jnp.concatenate([past_k.astype(k.dtype), k], axis=1)
        v_all = jnp.concatenate([past_v.astype(v.dtype), v], axis=1)
        P = past_k.shape[1]
    k_pos = jnp.arange(P + T)
    q_pos = P + jnp.arange(T)
    outs = []
    for qs in range(0, T, SB_QBLOCK):
        qe = min(qs + SB_QBLOCK, T)
        outs.append(stick_breaking_block(q[:, qs:qe], k_all[:, :P + qe], v_all[:, :P + qe],
                                         q_pos[qs:qe], k_pos[:P + qe]))
    o_sb = rmsnorm(jnp.concatenate(outs, axis=1), g_sb_out)
    u_a = jax.nn.gelu(u_a, approximate=False).reshape(B, T, N_A_GROUPS, A_GROUP_DIM)
    v_a = rmsnorm(jax.nn.gelu(v_a, approximate=False).reshape(B, T, N_A_GROUPS, A_GROUP_DIM), g_a_v)
    o_a = rmsnorm(spatial_gate(u_a, v_a, w_s, b_s), g_a_out)
    o = jnp.concatenate([o_sb.reshape(B, T, SB_WIDTH), o_a.reshape(B, T, A_WIDTH)], axis=-1) @ w_out
    return o, k, v, v_a

def peer_tokens(xb, w_q, sub_keys, u_tab, v_tab):
    t = xb.shape[0]
    q = (xb @ w_q).reshape(t, PEER_HEADS, 2, PEER_DKEY_HALF)
    s = jnp.einsum('thpd,hpnd->thpn', q, sub_keys).astype(jnp.float32)
    s1, i1 = lax.top_k(s[:, :, 0], PEER_TOPK)
    s2, i2 = lax.top_k(s[:, :, 1], PEER_TOPK)
    cand = (s1[..., :, None] + s2[..., None, :]).reshape(t, PEER_HEADS, PEER_TOPK * PEER_TOPK)
    cidx = (i1[..., :, None] * PEER_NKEYS + i2[..., None, :]).reshape(t, PEER_HEADS, PEER_TOPK * PEER_TOPK)
    sc, sel = lax.top_k(cand, PEER_TOPK)
    idx = jnp.take_along_axis(cidx, sel, axis=-1)
    g = jax.nn.softmax(sc, axis=-1)
    u_sel = jnp.take(u_tab, idx, axis=0)
    hid = jnp.einsum('td,thkd->thk', xb, u_sel).astype(jnp.float32)
    a = (g * jax.nn.gelu(hid, approximate=False)).astype(xb.dtype)
    return jnp.einsum('thk,thkd->td', a, jnp.take(v_tab, idx, axis=0))

def peer(x, w_q, sub_keys, u_tab, v_tab):
    B, T, D = x.shape
    n = B * T
    blk = min(PEER_BLOCK, n)
    nb = -(-n // blk)
    xf = jnp.pad(x.reshape(n, D), ((0, nb * blk - n), (0, 0))).reshape(nb, blk, D)
    out = lax.map(lambda xb: peer_tokens(xb, w_q, sub_keys, u_tab, v_tab), xf)
    return out.reshape(nb * blk, D)[:n].reshape(B, T, D)

def trunk_layer(h, p_l, past_k, past_v, g_mix, w_in, g_sb_out, w_s, b_s, g_a_v, g_a_out, w_out,
                g_ffn, w_peer_q, sub_keys, u_tab, v_tab, g_ple, w_ple_gate, b_ple_gate, w_ple):
    mix, k, v, v_a = token_mixers(rmsnorm(h, g_mix), past_k, past_v, w_in, g_sb_out,
                                  w_s, b_s, g_a_v, g_a_out, w_out)
    h = h + mix
    h = h + peer(rmsnorm(h, g_ffn), w_peer_q, sub_keys, u_tab, v_tab)
    gate = jax.nn.sigmoid(rmsnorm(h, g_ple) @ w_ple_gate + b_ple_gate)
    h = h + (p_l @ w_ple) * gate
    return h, k, v, v_a

def setup_inputs(seed: int = 0) -> dict:
    key = jax.random.key(seed)
    ks = jax.random.split(key, 26)
    nrm = lambda k, shape, scale: jax.random.normal(k, shape, jnp.float32) * scale
    gain = lambda k, shape: 1.0 + 0.05 * jax.random.normal(k, shape, jnp.float32)
    D = D_MODEL
    return {
        "x_prompt": nrm(ks[0], (BATCH, SEQ, D), 1.0),
        "x_sample": nrm(ks[1], (DEC_BATCH, DEC_SEQ, D), 1.0),
        "cache_k": nrm(ks[2], (DEPTH, DEC_BATCH, PAST_LEN, N_SB_HEADS, SB_HEAD_DIM), 1.0),
        "cache_v": nrm(ks[3], (DEPTH, DEC_BATCH, PAST_LEN, N_SB_HEADS, SB_HEAD_DIM), 1.0),
        "p_prompt": nrm(ks[4], (DEPTH, BATCH, SEQ, PLE_DIM), 1.0),
        "p_sample": nrm(ks[5], (DEPTH, DEC_BATCH, DEC_SEQ, PLE_DIM), 1.0),
        "g_mix": gain(ks[6], (DEPTH, D)),
        "w_in": nrm(ks[7], (DEPTH, D, IN_WIDTH), D ** -0.5),
        "g_sb_out": gain(ks[8], (DEPTH, N_SB_HEADS, SB_HEAD_DIM)),
        "w_spatial": nrm(ks[9], (DEPTH, N_A_GROUPS, GMLP_CHUNK, GMLP_CHUNK), GMLP_CHUNK ** -0.5),
        "b_spatial": gain(ks[10], (DEPTH, N_A_GROUPS, GMLP_CHUNK)),
        "g_a_v": gain(ks[11], (DEPTH, N_A_GROUPS, A_GROUP_DIM)),
        "g_a_out": gain(ks[12], (DEPTH, N_A_GROUPS, A_GROUP_DIM)),
        "w_out": nrm(ks[13], (DEPTH, MIX_WIDTH, D), MIX_WIDTH ** -0.5),
        "g_ffn": gain(ks[14], (DEPTH, D)),
        "w_peer_q": nrm(ks[15], (DEPTH, D, PEER_HEADS * PEER_DKEY), D ** -0.5),
        "peer_sub_keys": nrm(ks[16], (DEPTH, PEER_HEADS, 2, PEER_NKEYS, PEER_DKEY_HALF), PEER_DKEY_HALF ** -0.5),
        "peer_u": nrm(ks[17], (DEPTH, PEER_EXPERTS, D), D ** -0.5),
        "peer_v": nrm(ks[18], (DEPTH, PEER_EXPERTS, D), 0.5),
        "g_ple": gain(ks[19], (DEPTH, D)),
        "w_ple_gate": nrm(ks[20], (DEPTH, D, D), D ** -0.5),
        "b_ple_gate": nrm(ks[21], (DEPTH, D), 0.02),
        "w_ple": nrm(ks[22], (DEPTH, PLE_DIM, D), PLE_DIM ** -0.5),
        "g_final": gain(ks[23], (D,)),
    }

def reference(x_prompt, x_sample, cache_k, cache_v, p_prompt, p_sample, g_mix, w_in, g_sb_out,
              w_spatial, b_spatial, g_a_v, g_a_out, w_out, g_ffn, w_peer_q, peer_sub_keys,
              peer_u, peer_v, g_ple, w_ple_gate, b_ple_gate, w_ple, g_final):
    h_p, h_s = x_prompt, x_sample
    kp_l, vp_l, ks_l, vs_l, vas_l = [], [], [], [], []
    for l in range(DEPTH):
        lp = (g_mix[l], w_in[l], g_sb_out[l], w_spatial[l], b_spatial[l], g_a_v[l], g_a_out[l],
              w_out[l], g_ffn[l], w_peer_q[l], peer_sub_keys[l], peer_u[l], peer_v[l],
              g_ple[l], w_ple_gate[l], b_ple_gate[l], w_ple[l])
        h_p, kp, vp, _ = trunk_layer(h_p, p_prompt[l], None, None, *lp)
        h_s, ks, vs, vas = trunk_layer(h_s, p_sample[l], cache_k[l], cache_v[l], *lp)
        kp_l.append(kp); vp_l.append(vp); ks_l.append(ks); vs_l.append(vs); vas_l.append(vas)
    y_prompt = rmsnorm(h_p, g_final)
    y_sample = rmsnorm(h_s, g_final)
    new_k_prompt = jnp.stack(kp_l)
    new_v_prompt = jnp.stack(vp_l)
    new_k_sample = jnp.stack(ks_l)
    new_v_sample = jnp.stack(vs_l)
    new_chunkmlp_v_sample = jnp.stack(vas_l)
    return (y_prompt, y_sample, new_k_prompt, new_v_prompt, new_k_sample, new_v_sample, new_chunkmlp_v_sample)


_drawn_inputs = setup_inputs


def setup_inputs(seed=0):
    import zlib

    import numpy as np

    out = dict(_drawn_inputs(seed))
    spreads = {}
    factors = {'g_ple': 3.71, 'b_ple_gate': 17.479}
    for name, (base, spread) in spreads.items():
        noise = np.random.default_rng([zlib.crc32(name.encode()), seed]).standard_normal(out[name].shape)
        drawn = base * np.exp(spread * noise) if base else spread * noise
        out[name] = __import__('jax').numpy.asarray(drawn.astype(out[name].dtype))
    for name, factor in factors.items():
        out[name] = (out[name] * factor).astype(out[name].dtype)
    return out
```

```python
from contextlib import ExitStack

import concourse.bass as bass
import numpy as np
from concourse import mybir

F32 = mybir.dt.float32
U32 = mybir.dt.uint32
ALU = mybir.AluOpType
ACT = mybir.ActivationFunctionType
AX_X = mybir.AxisListType.X

P = 128
D = 1024
KD = D // P
L = 2
SEQ, DEC, PAST = 512, 32, 256
NT = SEQ // P + 1
SAMPLE = NT - 1
ROWS = [P] * SAMPLE + [DEC]
GROUPS = [[0, 1], [2, 3, 4]]
GCOLS = [sum(ROWS[t] for t in g) for g in GROUPS]
H, DH = 8, 64
W = H * DH
NKEYS, EXPERTS, TOPK = 128, 128 * 128, 16
PLE = 256
EPS = 1e-6
MASKED = -1e30
BELOW = -3.0e38
RSQRT_SEED = 0x5F3759DF
NEWTON_STEPS = 3
NU, NV = 4, 4
NW = 2
NB = 4
QUARTER = 4

IN_PARTS = ["q", "k", "v", "ua", "va"]


def group_of(t):
    return 0 if t in GROUPS[0] else 1


def place(t):
    g = GROUPS[group_of(t)]
    i = g.index(t)
    return i, P * i


def attention_stages(l, g):
    tiles = GROUPS[g]
    out = [("params", l)] if g == 0 else []
    out += [("norm", l, t, "mix") for t in tiles]
    out += [("q", l, g, b) for b in range(4)]
    late = None
    for t in tiles:
        out.append(("k", l, t))
        if late is not None:
            out.append(("kt", l, late))
        late = t
    out.append(("v", l, tiles[0]))
    out.append(("kt", l, late))
    out += [("v", l, t) for t in tiles[1:]]
    out += [("ua", l, t) for t in tiles]
    out += [("va", l, t) for t in tiles]
    units = [(l, t, h) for t in tiles if t != SAMPLE for h in range(H)]
    n = len(units)
    for i in range(n + 2):
        if i < n:
            out.append(("attZ",) + units[i])
        if 1 <= i <= n:
            out.append(("attE",) + units[i - 1])
        if i >= 2:
            out.append(("attP",) + units[i - 2])
            if units[i - 2][2] == H - 1:
                out.append(("attN", l, units[i - 2][1]))
    if SAMPLE in tiles:
        out += [("samZ", l), ("samE", l), ("samP", l), ("attN", l, SAMPLE)]
    out += [("mix", l, t) for t in tiles]
    out += [("wout", l, t, c) for c in range(2) for t in tiles]
    out += [("norm", l, t, "ffn") for t in tiles]
    out += [("pq", l, g, h) for h in range(H)]
    order = ([SAMPLE] if SAMPLE in tiles else []) + [t for t in tiles if t != SAMPLE]
    for t in order:
        out += [("topk", l, t, h) for h in range(H)]
        if t == SAMPLE:
            out.append(("pack", l))
    return out


def embedding_stages(l, g):
    tiles = GROUPS[g]
    out = [("pleparams", l, g)]
    out += [("ple", l, t, c) for t in tiles for c in range(2)]
    out += [("norm", l, t, "ple") for t in tiles]
    out += [("gate", l, t, c) for c in range(2) for t in tiles]
    if l == L - 1:
        out += ([("finalparams",)] if g == 0 else []) + [("final", t) for t in tiles]
    return out


ITEMS = []
FIRST_ITEM = {}
for l_ in range(L):
    for g_ in range(2):
        FIRST_ITEM[l_, g_] = len(ITEMS)
        for t_ in GROUPS[g_]:
            ITEMS += [(l_, t_, h_) for h_ in range(2 if t_ == SAMPLE else H)]
ITEM_COUNT = len(ITEMS)


def items_in_tile(t):
    return 2 if t == SAMPLE else H


def beside(gathers, work, weight):
    total = sum(weight(s) for s in work)
    out, done, n = [], 0.0, 0
    for i, s in enumerate(gathers):
        out.append(s)
        while n < len(work) and done + weight(work[n]) / 2 <= total * (i + 1) / len(gathers):
            done += weight(work[n])
            out.append(work[n])
            n += 1
    return out + work[n:]


COST = {"norm": 3, "q": 4, "k": 7, "kt": 1, "v": 7, "ua": 7, "va": 7, "attZ": 2, "attE": 2,
        "attP": 2, "attN": 3, "samZ": 11, "samE": 6, "samP": 10, "mix": 5, "wout": 7, "pq": 4,
        "topk": 9, "ple": 2, "gate": 8, "final": 3}


def schedule(overlap=True):
    weight = lambda s: COST.get(s[0], 0)
    gathers = lambda a, b: [("peer", j, q) for j in range(a, b) for q in range(4)]
    last = ITEM_COUNT
    b = [FIRST_ITEM[0, 0], FIRST_ITEM[0, 1], FIRST_ITEM[1, 0], FIRST_ITEM[1, 1], last]
    out = attention_stages(0, 0)
    out += beside(gathers(b[0], b[1]), attention_stages(0, 1), weight)
    out += gathers(b[1], b[1] + 1)
    out += beside(gathers(b[1] + 1, b[2]), embedding_stages(0, 0) + attention_stages(1, 0), weight)
    out += gathers(b[2], b[2] + 1)
    out += beside(gathers(b[2] + 1, b[3]), embedding_stages(0, 1) + attention_stages(1, 1), weight)
    out += gathers(b[3], b[3] + 1)
    out += beside(gathers(b[3] + 1, b[4]), embedding_stages(1, 0), weight)
    out += gathers(last, last + 1)
    out += embedding_stages(1, 1)
    return out


SCHEDULE = schedule()


class Signal:

    def __init__(self, sem, events):
        self.sem = sem
        self.count = {e: n + 1 for n, e in enumerate(events)}

    def after(self, event):
        return self.sem, self.count[event]


def bank_uses(s):
    k = s[0]
    if k == "norm":
        return [("tr",) + s[1:] + (half,) for half in range(2)]
    if k in ("q", "k", "kt", "v", "ua", "va", "attZ", "wout", "pq", "topk", "ple", "gate"):
        return [s]
    if k == "attN":
        return [("otr",) + s[1:]]
    if k == "samZ":
        return [("samZ", s[1], 0), ("samZ", s[1], 1)]
    if k == "samE":
        return [("samE", s[1], 0), ("samE", s[1], 1)]
    if k == "mix":
        return [s, ("mtr",) + s[1:]]
    return []


def releases(s):
    k = s[0]
    if k == "attZ":
        return []
    if k == "attE":
        return [("act", ("attZ",) + s[1:])]
    if k in ("kt", "wout"):
        return [("dve", u) for u in bank_uses(s)]
    if k == "samE":
        return [("dve", u) for u in bank_uses(s)]
    if k == "samZ":
        return [("dve", u) for u in bank_uses(s)]
    if k == "mix":
        return [("dve", s), ("act", ("mtr",) + s[1:])]
    return [("act", u) for u in bank_uses(s)]


USES = [u for s in SCHEDULE for u in bank_uses(s)]
BANK = {u: n % NB for n, u in enumerate(USES)}
TAKEN_BEFORE = {u: USES[n - NB] for n, u in enumerate(USES) if n >= NB}
RELEASES = [r for s in SCHEDULE for r in releases(s)]
RELEASED_BY = {u: who for who, u in RELEASES}


def weight_unit(s):
    k = s[0]
    if k in IN_PARTS:
        return ("in", s[1], s[2] if k == "q" else group_of(s[2]), IN_PARTS.index(k))
    if k in ("wout", "gate"):
        return (k, s[1], group_of(s[2]), s[3])
    if k == "ple":
        return (k, s[1], group_of(s[2]), 0)
    if k == "pq":
        return (k, s[1], s[2], s[3] // 4)
    if k == "topk":
        return (k, s[1], group_of(s[2]), 0)
    return None


UNITS = []
LAST_STAGE = {}
for s_ in SCHEDULE:
    u_ = weight_unit(s_)
    if u_ is not None:
        if u_ not in LAST_STAGE:
            UNITS.append(u_)
        LAST_STAGE[u_] = s_
UNIT_NUMBER = {u: n for n, u in enumerate(UNITS)}
NORMS = [s for s in SCHEDULE if s[0] in ("norm", "final")]
NORM_NUMBER = {s: n for n, s in enumerate(NORMS)}
TOPKS = [s for s in SCHEDULE if s[0] == "topk"]
TOPK_NUMBER = {s: n for n, s in enumerate(TOPKS)}
KS = [s for s in SCHEDULE if s[0] == "k"]
K_NUMBER = {s: n for n, s in enumerate(KS)}
UNIT_OF_ATT = {s: n for n, s in enumerate([s for s in SCHEDULE if s[0] == "attZ"])}
ATTNS = [s for s in SCHEDULE if s[0] == "attN"]


def encoder(nc, i, o):
    with ExitStack() as ctx:
        def sb(name, shape, dt=F32):
            return ctx.enter_context(nc.sbuf_tensor(name, shape, dt))

        def sem(name):
            return ctx.enter_context(nc.semaphore(name))

        h = sb("h", [P, NT, D])
        xn2 = sb("xn2", [P, NT, D])
        kT = sb("kT", [P, 4, SEQ + DEC])
        v = sb("v", [P, NT, W])
        ident = sb("ident", [P, P])
        spread = sb("spread", [P, DEC])
        neg_tri = sb("neg_tri", [P, P])
        neg_ones = sb("neg_ones", [P, P])
        mask = sb("mask", [P, P])
        ones_row = sb("ones_row", [1, P])
        iota16 = sb("iota16", [P, TOPK])
        gains = sb("gains", [P, L, 3, KD])
        kcT = sb("kcT", [P, 4, PAST])
        vc = sb("vc", [P, PAST // P, W])
        wsT = sb("wsT", [P, H, P])
        b_sp = sb("b_sp", [P, H])
        g_av = sb("g_av", [P, W])
        g_row = sb("g_row", [P, D])
        pT = sb("pT", [P, 2, GCOLS[1]])
        weights = sb("weights", [P, NW, KD * 512])
        xT = sb("xT", [P, KD, GCOLS[1]])
        xs = sb("xs", [P, 2, D])
        routing = sb("routing", [P, H * GCOLS[1]])
        qT = routing[:, 0:4 * GCOLS[1]].rearrange("p (a n) -> p a n", a=4)
        ktok = routing[:, 4 * GCOLS[1]:4 * GCOLS[1] + 2 * W].rearrange("p (a n) -> p a n", a=2)
        qpT = routing[:, :].rearrange("p (a n) -> p a n", a=H)
        mlp = sb("mlp", [P, 3, D])
        norm_work = sb("norm_work", [P, 2 * W])
        osb = norm_work[:, 0:W]
        sq = norm_work[:, W:2 * W]
        b_gate = norm_work[0:1, :]
        work = sb("work", [P, 4 * 512])
        sp = work[:, 0:1024].rearrange("p (a n) -> p a n", a=2)
        att = work[:, 1024:2048].rearrange("p (a n) -> p a n", a=2)
        ss = sb("ss", [P, 2])
        rs = sb("rs", [P, 2])
        ss8 = sb("ss8", [P, H])
        newton = sb("newton", [P, 2, H])
        square = TOPK * TOPK
        rep = work[:, 0:square].rearrange("p (a n) -> p a n", a=2)
        cand = work[:, square:2 * square].rearrange("p (a b) -> p a b", a=TOPK)
        cand2 = work[:, 2 * square:3 * square].rearrange("p (a b) -> p a b", a=TOPK)
        hot = work[:, 3 * square:5 * square].rearrange("p (a n) -> p a n", a=2)
        st = work[:, 5 * square:5 * square + 4 * NKEYS].rearrange("p (a n) -> p a n", a=2)
        top = sb("top", [P, 2, TOPK])
        topi = sb("topi", [P, 2, TOPK], U32)
        best = sb("best", [P, TOPK])
        pos = sb("pos", [P, TOPK], U32)
        pos2 = sb("pos2", [P, 2, TOPK], U32)
        part = sb("part", [P, 2, TOPK])
        negm = sb("negm", [P, 1])
        ex = sb("ex", [P, TOPK])
        esum = sb("esum", [P, 2])
        idx = sb("idx", [P, NT, H * TOPK], U32)
        gate = sb("gate", [P, NT, H * TOPK])
        idx_sam = sb("idx_sam", [P, 2 * TOPK], U32)
        gate_sam = sb("gate_sam", [P, 2 * TOPK])
        urows = sb("urows", [P, NU, D])
        vrows = sb("vrows", [P, NV, D])
        hid = sb("hid", [P, 2, TOPK])
        act_hid = sb("act_hid", [P, 2, TOPK])
        amount = sb("amount", [P, 2, TOPK])
        diag = sb("diag", [P, 2, QUARTER, P])

        def bank(name):
            return ctx.enter_context(nc.psum_tensor(name, [P, 512], F32))

        experts = [bank("experts0"), bank("experts1")]
        banks = [bank(f"bank{n}") for n in range(NB)]
        att_out = bank("att_out")

        const_made = sem("const_made")
        h_in = [sem(f"h_in{t}") for t in range(NT)]
        gains_in = sem("gains_in")
        params_in = sem("params_in")
        tril_made = sem("tril_made")
        ple_in = sem("ple_in")
        final_in = sem("final_in")
        w_in = [sem(f"w_in{n}") for n in range(NW)]
        k_out = [sem("k_out0"), sem("k_out1")]
        v_out = sem("v_out")
        va_out = sem("va_out")
        y_out = [sem("y_out0"), sem("y_out1")]
        packed = sem("packed")
        u_in = [sem(f"u_in{n}") for n in range(NU)]
        v_in = [sem(f"v_in{n}") for n in range(NV)]
        dve_chain, act_chain, pool_chain, pe_chain = (sem(n) for n in ("dve_chain", "act_chain",
                                                                       "pool_chain", "pe_chain"))

        def of(kinds):
            return [s for s in SCHEDULE if s[0] in kinds]

        products_done = Signal(sem("products_done"), USES)
        act_read = Signal(sem("act_read"), [u for who, u in RELEASES if who == "act"])
        dve_read = Signal(sem("dve_read"), [u for who, u in RELEASES if who == "dve"])
        bank_read = {"act": act_read, "dve": dve_read}
        squares_summed = Signal(sem("squares_summed"), NORMS)
        normed = Signal(sem("normed"), NORMS)
        va_normed = Signal(sem("va_normed"), of(["va"]))
        log_done = Signal(sem("log_done"), of(["attZ", "samZ"]))
        softplus_done = Signal(sem("softplus_done"), of(["attE", "samE"]))
        decay_done = Signal(sem("decay_done"), of(["attE"]))
        exponent_done = Signal(sem("exponent_done"), of(["samE"]))
        att_done = Signal(sem("att_done"), of(["samE"]))
        heads_done = Signal(sem("heads_done"), of(["attP", "samP"]))
        att_moved = Signal(sem("att_moved"), ATTNS)
        att_normed = Signal(sem("att_normed"), ATTNS)
        mix_done = Signal(sem("mix_done"), of(["mix"]))
        best_found = Signal(sem("best_found"), TOPKS)
        exps_done = Signal(sem("exps_done"), TOPKS)
        routed = Signal(sem("routed"), TOPKS)
        gated = Signal(sem("gated"), of(["gate"]))
        steps = [(j, s) for j in range(ITEM_COUNT) for s in range(TOPK)]
        dotted = Signal(sem("dotted"), steps)
        gelu_done = Signal(sem("gelu_done"), range(ITEM_COUNT))
        amounts_done = Signal(sem("amounts_done"), range(ITEM_COUNT))
        diag_made = Signal(sem("diag_made"), [(j, q) for j in range(ITEM_COUNT) for q in range(4)])
        added = Signal(sem("added"), steps)
        tiles_in_order = [(l, t) for l, t, e in ITEMS if e == 0]
        experts_added = Signal(sem("experts_added"), tiles_in_order)

        def h_ready(eng, l, t, kind):
            if kind == "mix" and l == 0:
                eng.wait_ge(h_in[t], 16)
            elif kind == "mix" or kind == "final":
                eng.wait_ge(*gated.after(("gate", l - 1, t, 1)))
            elif kind == "ffn":
                eng.wait_ge(*dve_read.after(("wout", l, t, 1)))
            else:
                eng.wait_ge(*experts_added.after((l, t)))

        def norm_source(s):
            return (L, s[1], "final") if s[0] == "final" else s[1:]

        PARAMS, PACKED = 16 * 6, 16 * 11

        block = ctx.enter_context(nc.Block())

        @block.sync
        def _(sp_eng):
            eng = sp_eng

            def load_unit(n):
                kind, l, g, c = UNITS[n]
                if n >= NW:
                    eng.wait_ge(*products_done.after(LAST_STAGE[UNITS[n - NW]]))
                src = {"in": i["w_in"], "wout": i["w_out"], "pq": i["w_peer_q"],
                       "gate": i["w_ple_gate"], "ple": i["w_ple"], "topk": i["sub_keysT"]}[kind][l, c]
                eng.dma_start(weights[:, n % NW, 0:src.shape[1]], src).then_inc(w_in[n % NW], 16)

            for t in GROUPS[0]:
                eng.dma_start(h[0:ROWS[t], t, :], i["x"][P * t:P * t + ROWS[t], :]).then_inc(h_in[t], 16)
            load_unit(0)
            load_unit(1)
            eng.dma_start(gains[:, :, :, :].rearrange("p a b c -> p (a b c)"), i["gains"]).then_inc(gains_in, 16)

            for s in SCHEDULE:
                if s[0] == "params":
                    l = s[1]
                    if l > 0:
                        eng.wait_ge(*routed.after(("topk", l - 1, GROUPS[1][1], H - 1)))
                    for dst, src in ((kcT[:, :, :].rearrange("p a n -> p (a n)"), i["cache_kT"][l]),
                                     (vc[:, :, :], i["cache_v"][l].rearrange("(b p) n -> p b n", p=P)),
                                     (wsT[:, :, :].rearrange("p a n -> p (a n)"), i["w_spatialT"][l]),
                                     (b_sp[:, :], i["b_spatialT"][l]),
                                     (g_av[:, :], i["g_a_v"][l:l + 1, :].to_broadcast([P, W])),
                                     (g_row[:, :], i["g_ffn"][l:l + 1, :].to_broadcast([P, D]))):
                        eng.dma_start(dst, src).then_inc(params_in, 16)
                    if l == 0:
                        for t in GROUPS[1]:
                            eng.dma_start(h[0:ROWS[t], t, :], i["x"][P * t:P * t + ROWS[t], :])\
                               .then_inc(h_in[t], 16)
                elif s[0] == "pleparams":
                    _, l, g = s
                    if (l, g) != (0, 0):
                        before = (l, 0) if g == 1 else (l - 1, 1)
                        eng.wait_ge(*products_done.after(("gate", before[0], GROUPS[before[1]][-1], 1)))
                    n = GCOLS[g]
                    eng.dma_start(pT[:, :, 0:n], i["pT"][l][:, :, P * GROUPS[g][0]:P * GROUPS[g][0] + n])\
                       .then_inc(ple_in, 16)
                    here = SCHEDULE.index(s)
                    eng.wait_ge(*routed.after([x for x in SCHEDULE[:here] if x[0] == "topk"][-1]))
                    eng.dma_start(b_gate[:, :], i["b_ple_gate"][l:l + 1, :]).then_inc(ple_in, 16)
                elif s[0] == "finalparams":
                    eng.wait_ge(*routed.after(("topk", L - 1, GROUPS[1][1], H - 1)))
                    eng.dma_start(g_row[:, :], i["g_final"].to_broadcast([P, D])).then_inc(final_in, 16)
                elif s[0] == "k":
                    _, l, t = s
                    eng.wait_ge(*act_read.after(s))
                    eng.dma_start(o["k"][l, P * t:P * t + ROWS[t], :], ktok[0:ROWS[t], K_NUMBER[s] % 2, :])\
                       .then_inc(k_out[K_NUMBER[s] % 2], 16)
                elif s[0] == "v":
                    _, l, t = s
                    eng.wait_ge(*act_read.after(s))
                    eng.dma_start(o["v"][l, P * t:P * t + ROWS[t], :], v[0:ROWS[t], t, :]).then_inc(v_out, 16)
                elif s[0] == "va" and s[2] == SAMPLE:
                    eng.wait_ge(*va_normed.after(s))
                    eng.dma_start(o["va"][s[1]], mlp[0:DEC, place(SAMPLE)[0], 0:W]).then_inc(va_out, 16)
                elif s[0] == "pack":
                    l = s[1]
                    eng.wait_ge(*routed.after(("topk", l, SAMPLE, H - 1)))
                    for b in range(4):
                        lo, hi = 32 * b, 32 * b + 32
                        eng.dma_start(idx_sam[lo:hi, :], idx[0:DEC, SAMPLE, lo:hi]).then_inc(packed, 16)
                        eng.dma_start(gate_sam[lo:hi, :], gate[0:DEC, SAMPLE, lo:hi]).then_inc(packed, 16)
                        if b:
                            eng.dma_start(xn2[lo:hi, SAMPLE, :], xn2[0:DEC, SAMPLE, :]).then_inc(packed, 16)
                elif s[0] == "final":
                    t = s[1]
                    eng.wait_ge(*normed.after(s))
                    eng.dma_start(o["y"][P * t:P * t + ROWS[t], :], xs[0:ROWS[t], NORM_NUMBER[s] % 2, :])\
                       .then_inc(y_out[NORM_NUMBER[s] % 2], 16)
                u = weight_unit(s)
                if u is not None and LAST_STAGE[u] == s and UNIT_NUMBER[u] + NW < len(UNITS):
                    load_unit(UNIT_NUMBER[u] + NW)
            for n in range(2):
                eng.wait_ge(k_out[n], 16 * len([s for s in KS if K_NUMBER[s] % 2 == n]))
                eng.wait_ge(y_out[n], 16 * len([s for s in NORMS if s[0] == "final" and NORM_NUMBER[s] % 2 == n]))
            eng.wait_ge(v_out, 16 * L * NT)
            eng.wait_ge(va_out, 16 * L)


        @block.gpsimd
        def _(pool):
            def select(out, pattern, op, fill, base=0, mult=1):
                pool.affine_select(out=out, in_=out, pattern=pattern, compare_op=op, fill=fill,
                                   base=base, channel_multiplier=mult).then_inc(pool_chain, 1)
                chain[0] += 1

            chain = [0]
            for buf, value in ((ident, 0.0), (spread, 0.0), (neg_tri, -1.0), (neg_ones, -1.0),
                               (mask, 0.0), (ones_row, 1.0)):
                pool.memset(buf[:, :], value).then_inc(pool_chain, 1)
                chain[0] += 1
            pool.wait_ge(pool_chain, chain[0])
            select(ident[:, :], [[-1, P]], ALU.not_equal, 1.0)
            select(neg_tri[:, :], [[-1, P]], ALU.is_ge, 0.0)
            select(mask[:, :], [[1, P]], ALU.is_gt, MASKED, mult=-1)
            for b in range(4):
                if b:
                    pool.wait_ge(pool_chain, chain[0])
                select(spread[:, :], [[-1, DEC]], ALU.not_equal, 1.0, base=-32 * b)
            pool.iota(iota16[:, :], [[1, TOPK]], base=0, channel_multiplier=0,
                      allow_small_or_imprecise_dtypes=True).then_inc(pool_chain, 1)
            pool.wait_ge(pool_chain, chain[0] + 1)
            pool.memset(hid[:, :, :], 0.0).then_inc(const_made, 1)

            def gather(table, rows, where, index, landed):
                pool.indirect_dma_start(out=rows[:, where, :], out_offset=None, in_=table,
                                        in_offset=bass.IndirectOffsetOnAxis(ap=index, axis=0))\
                    .then_inc(landed[where], 16)

            def column(j, s):
                _, t, e = ITEMS[j]
                c = e * TOPK + s
                return idx_sam[:, c:c + 1] if t == SAMPLE else idx[:, t, c:c + 1]

            for stage in SCHEDULE:
                if stage[0] == "params":
                    pool.wait_ge(params_in, PARAMS * (stage[1] + 1))
                    pool.affine_select(out=wsT[:, :, :], in_=wsT[:, :, :], pattern=[[0, H], [1, P]],
                                       compare_op=ALU.is_ge, fill=0.0, base=0, channel_multiplier=-1)\
                        .then_inc(tril_made, 1)
                elif stage[0] == "peer":
                    _, j, q = stage
                    for s in range(QUARTER * q, QUARTER * q + QUARTER):
                        if j < ITEM_COUNT:
                            l, t, e = ITEMS[j]
                            if s == 0:
                                if t == SAMPLE:
                                    pool.wait_ge(packed, PACKED * (l + 1))
                                else:
                                    pool.wait_ge(*routed.after(("topk", l, t, e)))
                            n = j * TOPK + s
                            if n >= NU:
                                pool.wait_ge(*dotted.after(steps[n - NU]))
                            gather(i["peer_u"], urows, n % NU, column(j, s), u_in)
                        if j > 0:
                            n = (j - 1) * TOPK + s
                            if n >= NV:
                                pool.wait_ge(*added.after(steps[n - NV]))
                            gather(i["peer_v"], vrows, n % NV, column(j - 1, s), v_in)

        @block.scalar
        def _(act):
            chain = [0]

            def mark(ins):
                chain[0] += 1
                ins.then_inc(act_chain, 1)

            def settle():
                act.wait_ge(act_chain, chain[0])

            def from_bank(use, out, func=ACT.Copy, rows=P, cols=512, **kw):
                act.wait_ge(*products_done.after(use))
                act.activation(out, banks[BANK[use]][0:rows, 0:cols], func, **kw)\
                    .then_inc(act_read.sem, 1)

            def turned(use, l, gain, k0, out):
                act.wait_ge(*products_done.after(use))
                rows = out.shape[2]
                for k in range(4):
                    last = act.activation(out[:, k, :], banks[BANK[use]][:, P * k:P * k + rows], ACT.Copy,
                                          scale=gains[:, l, gain, k0 + k:k0 + k + 1])
                last.then_inc(act_read.sem, 1)

            act.wait_ge(gains_in, 16)
            for s in SCHEDULE:
                kind = s[0]
                if kind in ("norm", "final"):
                    l, t, what = norm_source(s)
                    r, n = ROWS[t], NORM_NUMBER[s]
                    h_ready(act, l, t, what)
                    if n >= 2:
                        before = NORMS[n - 2]
                        if before[0] == "final":
                            act.wait_ge(y_out[n % 2], 16 * len([x for x in NORMS[:n] if x[0] == "final" and NORM_NUMBER[x] % 2 == n % 2]))
                        elif before[3] != "ffn":
                            act.wait_ge(*products_done.after(("tr",) + before[1:] + (1,)))
                        else:
                            act.wait_ge(*normed.after(before))
                    act.activation(xs[0:r, n % 2, :], h[0:r, t, :], ACT.Square,
                                   accum_out=ss[0:r, n % 2:n % 2 + 1]).then_inc(squares_summed.sem, 1)
                    if kind == "norm":
                        c0 = place(t)[1]
                        for half in range(2):
                            use = ("tr",) + s[1:] + (half,)
                            out = xT[:, 4 * half:4 * half + 4, c0:c0 + r]
                            if what == "ffn":
                                act.wait_ge(*products_done.after(use))
                                act.activation(out, banks[BANK[use]][:, :].rearrange("p (a n) -> p a n", a=4)[:, :, 0:r],
                                               ACT.Copy).then_inc(act_read.sem, 1)
                            else:
                                turned(use, l, 0 if what == "mix" else 2, 4 * half, out)
                elif kind == "q":
                    _, l, g, b = s
                    from_bank(s, qT[:, b, 0:GCOLS[g]], cols=GCOLS[g], scale=DH ** -0.5)
                elif kind == "k":
                    _, l, t = s
                    n = K_NUMBER[s]
                    if n >= 2:
                        act.wait_ge(k_out[n % 2], 16 * (n // 2))
                        act.wait_ge(*products_done.after(("kt",) + KS[n - 2][1:]))
                    from_bank(s, ktok[0:ROWS[t], n % 2, :], rows=ROWS[t])
                elif kind == "v":
                    _, l, t = s
                    if l > 0:
                        act.wait_ge(v_out, 16 * NT * l)
                    from_bank(s, v[0:ROWS[t], t, :], rows=ROWS[t])
                elif kind in ("ua", "va"):
                    _, l, t = s
                    at = 0 if kind == "va" else W
                    if kind == "va" and t == SAMPLE and l > 0:
                        act.wait_ge(va_out, 16 * l)
                    from_bank(s, mlp[0:ROWS[t], place(t)[0], at:at + W], ACT.Gelu, rows=ROWS[t])
                elif kind in ("attZ", "samZ"):
                    if kind == "attZ":
                        n = UNIT_OF_ATT[s]
                        cols = P * (s[2] + 1)
                        parts = [(s, sp[:, n % 2, 0:cols])]
                        if n >= 2:
                            act.wait_ge(*decay_done.after(("attE",) + list(UNIT_OF_ATT)[n - 2][1:]))
                    else:
                        parts = [(("samZ", s[1], 0), sp[:, 0, :]),
                                 (("samZ", s[1], 1), sp[0:DEC, 1, 0:H * DEC])]
                        for e in (H - 2, H - 1):
                            act.wait_ge(*decay_done.after(("attE", s[1], SAMPLE - 1, e)))
                    for use, x in parts:
                        act.wait_ge(*products_done.after(use))
                        r, cols = x.shape
                        mark(act.activation(x, banks[BANK[use]][0:r, 0:cols], ACT.Abs))
                    settle()
                    for _, x in parts:
                        mark(act.activation(x, x, ACT.Exp, scale=-1.0))
                    settle()
                    for _, x in parts:
                        last = act.activation(x, x, ACT.Ln, bias=1.0)
                        if x is not parts[-1][1]:
                            mark(last)
                    last.then_inc(log_done.sem, 1)
                elif kind == "attE":
                    z = ("attZ",) + s[1:]
                    n = UNIT_OF_ATT[z]
                    act.wait_ge(*decay_done.after(s))
                    if n >= 2:
                        earlier = [x for x in UNIT_OF_ATT][n - 2]
                        act.wait_ge(*heads_done.after(("attP",) + earlier[1:]))
                    cols = P * (s[2] + 1)
                    act.activation(att[:, n % 2, 0:cols], banks[BANK[z]][:, 0:cols], ACT.Exp)\
                        .then_inc(act_read.sem, 1)
                elif kind == "samE":
                    act.wait_ge(*exponent_done.after(s))
                    act.activation(att[:, 0, :], att[:, 0, :], ACT.Exp)
                    act.activation(att[0:DEC, 1, 0:H * DEC], att[0:DEC, 1, 0:H * DEC], ACT.Exp)\
                        .then_inc(att_done.sem, 1)
                elif kind == "attN":
                    _, l, t = s
                    r, c0 = ROWS[t], place(t)[1]
                    n = ATTNS.index(s)
                    act.wait_ge(*heads_done.after(("samP", l) if t == SAMPLE else ("attP", l, t, H - 1)))
                    if n:
                        act.wait_ge(*products_done.after(("otr",) + ATTNS[n - 1][1:]))
                    act.activation(osb[0:r, :], att_out[0:r, :], ACT.Copy).then_inc(att_moved.sem, 1)
                    turned(("otr", l, t), l, 1, 0, xT[:, 0:4, c0:c0 + r])
                elif kind == "mix":
                    _, l, t = s
                    c0 = place(t)[1]
                    turned(("mtr", l, t), l, 1, 4, xT[:, 4:8, c0:c0 + ROWS[t]])
                elif kind == "pq":
                    _, l, g, e = s
                    if e == 0:
                        for n in range(2):
                            act.wait_ge(k_out[n], 16 * len([x for x in KS if K_NUMBER[x] % 2 == n
                                                            and (x[1], group_of(x[2])) <= (l, g)]))
                    from_bank(s, qpT[:, e, 0:GCOLS[g]], cols=GCOLS[g])
                elif kind == "topk":
                    _, l, t, e = s
                    r, n = ROWS[t], TOPK_NUMBER[s]
                    if n >= 2:
                        act.wait_ge(*routed.after(TOPKS[n - 2]))
                    from_bank(s, st[0:r, n % 2, :], rows=r, cols=2 * NKEYS)
                    act.wait_ge(*best_found.after(s))
                    act.activation(ex[0:r, :], best[0:r, :], ACT.Exp, bias=negm[0:r, 0:1],
                                   accum_out=esum[0:r, 0:1]).then_inc(exps_done.sem, 1)
                elif kind == "ple":
                    _, l, t, c = s
                    from_bank(s, mlp[0:ROWS[t], place(t)[0], 512 * c:512 * c + 512], rows=ROWS[t])
                elif kind == "gate":
                    _, l, t, c = s
                    n = GATE_NUMBER[s]
                    if n >= 2:
                        act.wait_ge(*gated.after(GATES[n - 2]))
                    from_bank(s, sp[0:ROWS[t], n % 2, :], ACT.Sigmoid, rows=ROWS[t])
                elif kind == "peer":
                    _, j, q = s
                    if q == 0 and j > 0:
                        act.wait_ge(*dotted.after((j - 1, TOPK - 1)))
                        act.activation(act_hid[:, (j - 1) % 2, :], hid[:, (j - 1) % 2, :], ACT.Gelu)\
                            .then_inc(gelu_done.sem, 1)

        @block.vector
        def _(dve):
            chain = [0]

            def mark(ins):
                chain[0] += 1
                ins.then_inc(dve_chain, 1)

            def settle():
                dve.wait_ge(dve_chain, chain[0])

            def link(ins):
                mark(ins)
                settle()

            def root(out, x, scale):
                r, n = x.shape
                y, half = newton[0:r, 0, 0:n], newton[0:r, 1, 0:n]
                link(dve.tensor_scalar(x, x, scale, EPS, ALU.mult, ALU.add))
                link(dve.tensor_scalar(half.bitcast(U32), x.bitcast(U32), 1, None, ALU.logical_shift_right))
                link(dve.tensor_scalar(y.bitcast(U32), half.bitcast(U32), -1.0, float(RSQRT_SEED),
                                       ALU.mult, ALU.add))
                for step in range(NEWTON_STEPS):
                    link(dve.tensor_tensor(half, y, y, ALU.mult))
                    link(dve.tensor_tensor(half, half, x, ALU.mult))
                    link(dve.tensor_scalar(half, half, -0.5, 1.5, ALU.mult, ALU.add))
                    link(dve.tensor_tensor(out if step == NEWTON_STEPS - 1 else y, y, half, ALU.mult))

            def head_norm(x, r):
                link(dve.tensor_tensor(sq[0:r, :], x, x, ALU.mult))
                link(dve.tensor_reduce(ss8[0:r, :], sq[0:r, :].rearrange("p (a n) -> p a n", a=H), AX_X, ALU.add))
                root(ss8[0:r, :], ss8[0:r, :], 1.0 / DH)
                x3 = x.rearrange("p (a n) -> p a n", a=H)
                return dve.tensor_tensor(x3, x3, ss8[0:r, :].unsqueeze(2).to_broadcast([r, H, DH]), ALU.mult)

            def top16(out, where, x, scratch):
                for a, w, b, _ in zip(out, where, x, scratch):
                    mark(dve.max(a[:, 0:8], b))
                settle()
                for a, w, b, c in zip(out, where, x, scratch):
                    mark(dve.max_index(w[:, 0:8], a[:, 0:8], b))
                    mark(dve.match_replace(c, a[:, 0:8], b, BELOW))
                settle()
                for a, w, b, c in zip(out, where, x, scratch):
                    mark(dve.max(a[:, 8:16], c))
                settle()
                for a, w, b, c in zip(out, where, x, scratch):
                    mark(dve.max_index(w[:, 8:16], a[:, 8:16], c))
                settle()

            def topk(s):
                _, l, t, e = s
                r, n = ROWS[t], TOPK_NUMBER[s]
                dve.wait_ge(*act_read.after(s))
                keys = [st[0:r, n % 2, NKEYS * p:NKEYS * p + NKEYS] for p in range(2)]
                top16([top[0:r, p, :] for p in range(2)], [topi[0:r, p, :] for p in range(2)], keys,
                      [rep[0:r, p, :] for p in range(2)])
                full = [r, TOPK, TOPK]
                link(dve.tensor_tensor(cand[0:r], top[0:r, 0, :].unsqueeze(2).to_broadcast(full),
                                       top[0:r, 1, :].unsqueeze(1).to_broadcast(full), ALU.add))
                flat = [x[0:r].rearrange("p a b -> p (a b)") for x in (cand, cand2)]
                top16([best[0:r, :]], [pos[0:r, :]], [flat[0]], [flat[1]])
                dve.tensor_scalar(negm[0:r, :], best[0:r, 0:1], -1.0, None, ALU.mult)\
                    .then_inc(best_found.sem, 1)
                mark(dve.tensor_scalar(pos2[0:r, 0, :], pos[0:r, :], 4, None, ALU.logical_shift_right))
                mark(dve.tensor_scalar(pos2[0:r, 1, :], pos[0:r, :], TOPK - 1, None, ALU.bitwise_and))
                settle()
                hot3 = [hot[0:r, p, :].rearrange("p (a b) -> p a b", a=TOPK) for p in range(2)]
                for p in range(2):
                    mark(dve.tensor_tensor(hot3[p], iota16[0:r, :].unsqueeze(1).to_broadcast(full),
                                           pos2[0:r, p, :].unsqueeze(2).to_broadcast(full), ALU.is_equal))
                settle()
                for p in range(2):
                    mark(dve.tensor_tensor(hot3[p], hot3[p], topi[0:r, p, :].unsqueeze(1).to_broadcast(full),
                                           ALU.mult))
                settle()
                for p in range(2):
                    mark(dve.tensor_reduce(part[0:r, p, :], hot3[p], AX_X, ALU.add))
                settle()
                at = slice(e * TOPK, e * TOPK + TOPK)
                link(dve.tensor_scalar(part[0:r, 0, :], part[0:r, 0, :], float(NKEYS), float(l * EXPERTS),
                                       ALU.mult, ALU.add))
                mark(dve.tensor_tensor(idx[0:r, t, at], part[0:r, 0, :], part[0:r, 1, :], ALU.add))
                dve.wait_ge(*exps_done.after(s))
                link(dve.reciprocal(esum[0:r, 1:2], esum[0:r, 0:1]))
                dve.tensor_scalar(gate[0:r, t, at], ex[0:r, :], esum[0:r, 1:2], None, ALU.mult)\
                    .then_inc(routed.sem, 1)

            dve.wait_ge(const_made, 1)
            for s in SCHEDULE:
                kind = s[0]
                if kind in ("norm", "final"):
                    l, t, what = norm_source(s)
                    r, n = ROWS[t], NORM_NUMBER[s]
                    dve.wait_ge(*squares_summed.after(s))
                    root(rs[0:r, n % 2:n % 2 + 1], ss[0:r, n % 2:n % 2 + 1], 1.0 / D)
                    scale = rs[0:r, n % 2:n % 2 + 1]
                    if what == "ffn" or what == "final":
                        if what == "ffn":
                            dve.wait_ge(params_in, PARAMS * (l + 1))
                        else:
                            dve.wait_ge(final_in, 16)
                        out = xn2[0:r, t, :] if what == "ffn" else xs[0:r, n % 2, :]
                        dve.scalar_tensor_tensor(out=out, in0=h[0:r, t, :], scalar=scale, in1=g_row[0:r, :],
                                                 op0=ALU.mult, op1=ALU.mult).then_inc(normed.sem, 1)
                    else:
                        dve.tensor_scalar(xs[0:r, n % 2, :], h[0:r, t, :], scale, None, ALU.mult)\
                            .then_inc(normed.sem, 1)
                elif kind == "kt":
                    _, l, t = s
                    r = ROWS[t]
                    dve.wait_ge(*products_done.after(s))
                    dve.tensor_copy(kT[:, :, P * t:P * t + r],
                                    banks[BANK[s]][:, :].rearrange("p (a n) -> p a n", a=4)[:, :, 0:r])\
                        .then_inc(dve_read.sem, 1)
                elif kind == "va":
                    _, l, t = s
                    r = ROWS[t]
                    dve.wait_ge(*act_read.after(s))
                    dve.wait_ge(params_in, PARAMS * (l + 1))
                    x = mlp[0:r, place(t)[0], 0:W]
                    link(head_norm(x, r))
                    dve.tensor_tensor(x, x, g_av[0:r, :], ALU.mult).then_inc(va_normed.sem, 1)
                elif kind == "attE":
                    z = ("attZ",) + s[1:]
                    x = sp[:, UNIT_OF_ATT[z] % 2, 0:P * (s[2] + 1)]
                    dve.wait_ge(*log_done.after(z))
                    dve.scalar_tensor_tensor(out=x, in0=banks[BANK[z]][:, 0:P * (s[2] + 1)], scalar=0.0,
                                             in1=x, op0=ALU.max, op1=ALU.add).then_inc(softplus_done.sem, 1)
                elif kind == "samE":
                    l = s[1]
                    dve.wait_ge(*log_done.after(("samZ", l)))
                    for e in (H - 2, H - 1):
                        dve.wait_ge(*heads_done.after(("attP", l, SAMPLE - 1, e)))
                    shapes = [(0, P, 512), (1, DEC, H * DEC)]
                    for b, r, cols in shapes:
                        z = banks[BANK["samZ", l, b]][0:r, 0:cols]
                        x = sp[0:r, b, 0:cols]
                        mark(dve.scalar_tensor_tensor(out=x, in0=z, scalar=0.0, in1=x, op0=ALU.max, op1=ALU.add))
                    settle()
                    dve.tensor_copy(att[:, 0, :], banks[BANK["samZ", l, 0]][:, :]).then_inc(dve_read.sem, 1)
                    dve.tensor_copy(att[0:DEC, 1, 0:H * DEC], banks[BANK["samZ", l, 1]][0:DEC, 0:H * DEC])\
                        .then_inc(dve_read.sem, 1)
                    dve.wait_ge(*dve_read.after(("samZ", l, 1)))
                    dve.engine_nop().then_inc(softplus_done.sem, 1)
                    for b, r, cols in shapes:
                        use = ("samE", l, b)
                        dve.wait_ge(*products_done.after(use))
                        x = att[0:r, b, 0:cols]
                        dve.tensor_tensor(x, x, banks[BANK[use]][0:r, 0:cols], ALU.add)\
                            .then_inc(dve_read.sem, 1)
                    dve.wait_ge(*dve_read.after(("samE", l, 1)))
                    dve.engine_nop().then_inc(exponent_done.sem, 1)
                elif kind == "attN":
                    _, l, t = s
                    dve.wait_ge(*att_moved.after(s))
                    head_norm(osb[0:ROWS[t], :], ROWS[t]).then_inc(att_normed.sem, 1)
                elif kind == "mix":
                    _, l, t = s
                    r = ROWS[t]
                    dve.wait_ge(*products_done.after(s))
                    out = sq[0:r, :].rearrange("p (a n) -> p a n", a=H)
                    dve.tensor_tensor(out, banks[BANK[s]][0:r, :].rearrange("p (a n) -> p a n", a=H),
                                      b_sp[0:r, :].unsqueeze(2).to_broadcast([r, H, DH]), ALU.add)\
                        .then_inc(dve_read.sem, 1)
                    dve.wait_ge(*dve_read.after(s))
                    dve.wait_ge(*act_read.after(("ua", l, t)))
                    u = mlp[0:r, place(t)[0], W:2 * W]
                    link(dve.tensor_tensor(u, u, sq[0:r, :], ALU.mult))
                    head_norm(u, r).then_inc(mix_done.sem, 1)
                elif kind == "wout":
                    _, l, t, c = s
                    r = ROWS[t]
                    if l == 0 and c == 0:
                        dve.wait_ge(h_in[t], 16)
                    dve.wait_ge(*products_done.after(s))
                    x = h[0:r, t, 512 * c:512 * c + 512]
                    dve.tensor_tensor(x, x, banks[BANK[s]][0:r, :], ALU.add).then_inc(dve_read.sem, 1)
                elif kind == "topk":
                    topk(s)
                elif kind == "gate":
                    _, l, t, c = s
                    r = ROWS[t]
                    dve.wait_ge(*act_read.after(s))
                    dve.wait_ge(*act_read.after(("ple", l, t, c)))
                    x = sp[0:r, GATE_NUMBER[s] % 2, :]
                    link(dve.tensor_tensor(x, x, mlp[0:r, place(t)[0], 512 * c:512 * c + 512], ALU.mult))
                    y = h[0:r, t, 512 * c:512 * c + 512]
                    dve.tensor_tensor(y, y, x, ALU.add).then_inc(gated.sem, 1)
                elif kind == "peer":
                    _, j, q = s
                    if j < ITEM_COUNT:
                        l, t, e = ITEMS[j]
                        if q == 0 and t == SAMPLE:
                            dve.wait_ge(packed, PACKED * (l + 1))
                        if q == 0 and j >= 2:
                            dve.wait_ge(*gelu_done.after(j - 2))
                        for k in range(QUARTER * q, QUARTER * q + QUARTER):
                            n = j * TOPK + k
                            dve.wait_ge(u_in[n % NU], 16 * (n // NU + 1))
                            row = urows[:, n % NU, :]
                            dve.tensor_tensor_reduce(row, row, xn2[:, t, :], 1.0, 0.0, ALU.mult, ALU.add,
                                                     hid[:, j % 2, k:k + 1]).then_inc(dotted.sem, 1)
                    if j > 0:
                        l, t, e = ITEMS[j - 1]
                        b = (j - 1) % 2
                        if q == 0:
                            at = slice(e * TOPK, e * TOPK + TOPK)
                            g = gate_sam[:, at] if t == SAMPLE else gate[:, t, at]
                            dve.wait_ge(*gelu_done.after(j - 1))
                            dve.tensor_tensor(amount[:, b, :], act_hid[:, b, :], g, ALU.mult)\
                                .then_inc(amounts_done.sem, 1)
                            dve.wait_ge(*amounts_done.after(j - 1))
                        m = 4 * (j - 1) + q
                        if m >= 2:
                            dve.wait_ge(*added.after(steps[QUARTER * (m - 1) - 1]))
                        full = [P, QUARTER, ROWS[t]]
                        where = spread if t == SAMPLE else ident
                        dve.tensor_tensor(diag[:, m % 2, :, 0:ROWS[t]], where[:, :].unsqueeze(1).to_broadcast(full),
                                          amount[:, b, QUARTER * q:QUARTER * q + QUARTER].unsqueeze(2).to_broadcast(full),
                                          ALU.mult).then_inc(diag_made.sem, 1)
                        if q == 3 and e == items_in_tile(t) - 1:
                            r = ROWS[t]
                            dve.wait_ge(*added.after((j - 1, TOPK - 1)))
                            for c in range(2):
                                x = h[0:r, t, 512 * c:512 * c + 512]
                                last = dve.tensor_tensor(x, x, experts[c][0:r, :], ALU.add)
                                if c == 0:
                                    mark(last)
                            last.then_inc(experts_added.sem, 1)

        @block.tensor
        def _(pe):
            def take(use):
                if use in TAKEN_BEFORE:
                    before = TAKEN_BEFORE[use]
                    pe.wait_ge(*bank_read[RELEASED_BY[before]].after(before))
                return banks[BANK[use]]

            chain = [0]

            def rows_change(ins):
                chain[0] += 1
                ins.then_inc(pe_chain, 1)
                pe.wait_ge(pe_chain, chain[0])

            def unit(s):
                n = UNIT_NUMBER[weight_unit(s)]
                pe.wait_ge(w_in[n % NW], 16 * (n // NW + 1))
                return weights[:, n % NW, :].rearrange("p (k n) -> p k n", k=KD)

            def turn(use, blocks):
                b = take(use)
                for k, x in enumerate(blocks):
                    r = x.shape[0]
                    last = pe.transpose(b[:, P * k:P * k + r], x, ident[0:r, 0:r])
                last.then_inc(products_done.sem, 1)

            def turned_ready(kind, l, tiles):
                for t in tiles:
                    pe.wait_ge(*act_read.after(("tr", l, t, kind, 1)))

            def by_token(s, x_cols, r):
                w = unit(s)
                b = take(s)
                for k in range(KD):
                    last = pe.matmul(b[0:r, :], xT[:, k, x_cols:x_cols + r], w[:, k, :],
                                     start=(k == 0), stop=(k == KD - 1))
                return b, last

            def by_column(s, block, cols):
                w = unit(s)
                b = take(s)
                for k in range(KD):
                    last = pe.matmul(b[:, 0:cols], w[:, k, P * block:P * block + P], xT[:, k, 0:cols],
                                     start=(k == 0), stop=(k == KD - 1))
                last.then_inc(products_done.sem, 1)

            pe.wait_ge(const_made, 1)
            for s in SCHEDULE:
                kind = s[0]
                if kind == "norm":
                    _, l, t, what = s
                    r = ROWS[t]
                    pe.wait_ge(*normed.after(s))
                    src = xn2[0:r, t, :] if what == "ffn" else xs[0:r, NORM_NUMBER[s] % 2, :]
                    for half in range(2):
                        turn(("tr",) + s[1:] + (half,),
                             [src[:, P * k:P * k + P] for k in range(4 * half, 4 * half + 4)])
                elif kind == "q":
                    _, l, g, b = s
                    if b == 0:
                        turned_ready("mix", l, GROUPS[g])
                    by_column(s, b, GCOLS[g])
                elif kind in ("k", "v", "ua", "va"):
                    _, l, t = s
                    by_token(s, place(t)[1], ROWS[t])[1].then_inc(products_done.sem, 1)
                elif kind == "kt":
                    _, l, t = s
                    pe.wait_ge(*act_read.after(("k", l, t)))
                    n = K_NUMBER["k", l, t]
                    turn(s, [ktok[0:ROWS[t], n % 2, P * k:P * k + P] for k in range(4)])
                elif kind == "attZ":
                    _, l, t, e = s
                    c0, lo = place(t)[1], DH * (e % 2)
                    if e == 0:
                        pe.wait_ge(*act_read.after(("q", l, group_of(t), 3)))
                        pe.wait_ge(*dve_read.after(("kt", l, t)))
                    b = take(s)
                    for kb in range(t + 1):
                        pe.matmul(b[:, P * kb:P * kb + P], kT[lo:lo + DH, e // 2, P * kb:P * kb + P],
                                  qT[lo:lo + DH, e // 2, c0:c0 + P], start=(kb == 0), stop=False,
                                  skip_group_check=True)
                    pe.matmul(b[:, P * t:P * t + P], ident[:, :], mask[:, :], start=False, stop=True,
                              skip_group_check=True).then_inc(products_done.sem, 1)
                elif kind == "attE":
                    _, l, t, e = s
                    z = ("attZ", l, t, e)
                    b = banks[BANK[z]]
                    x = sp[:, UNIT_OF_ATT[z] % 2, :]
                    pe.wait_ge(*softplus_done.after(s))
                    last = pe.matmul(b[:, 0:P * (t + 1)], neg_tri[:, :], x[:, 0:P * (t + 1)], start=False,
                                     stop=(t == 0), skip_group_check=True)
                    for kb in range(1, t + 1):
                        rhs = x[:, P * kb:P * kb + P].unsqueeze(1).to_broadcast([P, kb, P])
                        last = pe.matmul(b[:, 0:P * kb].rearrange("p (a n) -> p a n", a=kb), neg_ones[:, :], rhs,
                                         start=False, stop=(kb == t), skip_group_check=True)
                    last.then_inc(decay_done.sem, 1)
                elif kind == "attP":
                    _, l, t, e = s
                    z = ("attZ", l, t, e)
                    pe.wait_ge(*act_read.after(z))
                    if e == 0:
                        pe.wait_ge(*act_read.after(("v", l, t)))
                        n = ATTNS.index(("attN", l, t))
                        if n:
                            pe.wait_ge(*att_moved.after(ATTNS[n - 1]))
                    for kb in range(t + 1):
                        last = pe.matmul(att_out[:, DH * e:DH * e + DH],
                                         att[:, UNIT_OF_ATT[z] % 2, P * kb:P * kb + P],
                                         v[:, kb, DH * e:DH * e + DH], start=(kb == 0), stop=(kb == t))
                    last.then_inc(heads_done.sem, 1)
                elif kind == "samZ":
                    l = s[1]
                    c0 = place(SAMPLE)[1]
                    pe.wait_ge(params_in, PARAMS * (l + 1))
                    pe.wait_ge(*dve_read.after(("kt", l, SAMPLE)))
                    b = take(("samZ", l, 0))
                    for half in range(2):
                        lo = DH * half
                        if half:
                            rows_change(last)
                        for kb in range(2):
                            for e in range(half, H, 2):
                                at = (kb * H + e) * DEC
                                last = pe.matmul(b[:, at:at + DEC], kcT[lo:lo + DH, e // 2, P * kb:P * kb + P],
                                                 qT[lo:lo + DH, e // 2, c0:c0 + DEC], start=True, stop=True)
                    last.then_inc(products_done.sem, 1)
                    b = take(("samZ", l, 1))
                    for half in range(2):
                        lo = DH * half
                        if half:
                            rows_change(last)
                        for e in range(half, H, 2):
                            last = pe.matmul(b[0:DEC, DEC * e:DEC * e + DEC], kT[lo:lo + DH, e // 2, SEQ:SEQ + DEC],
                                             qT[lo:lo + DH, e // 2, c0:c0 + DEC], start=(e == 0), stop=False,
                                             skip_group_check=True)
                    pe.matmul(b[0:DEC, 0:H * DEC].rearrange("p (a n) -> p a n", a=H), ident[0:DEC, 0:DEC],
                              mask[0:DEC, 0:DEC].unsqueeze(1).to_broadcast([DEC, H, DEC]), start=False, stop=True,
                              skip_group_check=True).then_inc(products_done.sem, 1)
                elif kind == "samE":
                    l = s[1]
                    pe.wait_ge(*softplus_done.after(s))
                    new = sp[0:DEC, 1, 0:H * DEC]
                    past = [sp[:, 0, 0:256], sp[:, 0, 256:512]]
                    b = take(("samE", l, 0))
                    for kb in range(2):
                        out = b[:, 256 * kb:256 * kb + 256]
                        pe.matmul(out, neg_tri[:, :], past[kb], start=True, stop=False)
                        if kb == 0:
                            pe.matmul(out, neg_ones[:, :], past[1], start=False, stop=False)
                        last = pe.matmul(out, neg_ones[0:DEC, :], new, start=False, stop=True)
                    last.then_inc(products_done.sem, 1)
                    b = take(("samE", l, 1))
                    pe.matmul(b[0:DEC, 0:H * DEC], neg_tri[0:DEC, 0:DEC], new, start=True, stop=True)\
                        .then_inc(products_done.sem, 1)
                elif kind == "samP":
                    l = s[1]
                    pe.wait_ge(*att_done.after(("samE", l)))
                    pe.wait_ge(*act_read.after(("v", l, SAMPLE)))
                    pe.wait_ge(*att_moved.after(("attN", l, SAMPLE - 1)))
                    for e in range(H):
                        out = att_out[0:DEC, DH * e:DH * e + DH]
                        for kb in range(2):
                            at = (kb * H + e) * DEC
                            pe.matmul(out, att[:, 0, at:at + DEC], vc[:, kb, DH * e:DH * e + DH],
                                      start=(kb == 0), stop=False)
                        last = pe.matmul(out, att[0:DEC, 1, DEC * e:DEC * e + DEC],
                                         v[0:DEC, SAMPLE, DH * e:DH * e + DH], start=False, stop=True)
                    last.then_inc(heads_done.sem, 1)
                elif kind == "attN":
                    _, l, t = s
                    pe.wait_ge(*att_normed.after(s))
                    turn(("otr", l, t), [osb[0:ROWS[t], P * k:P * k + P] for k in range(4)])
                elif kind == "mix":
                    _, l, t = s
                    r, at = ROWS[t], place(t)[0]
                    pe.wait_ge(*va_normed.after(("va", l, t)))
                    pe.wait_ge(tril_made, l + 1)
                    b = take(s)
                    for e in range(H):
                        last = pe.matmul(b[0:r, DH * e:DH * e + DH], wsT[0:r, e, 0:r],
                                         mlp[0:r, at, DH * e:DH * e + DH], start=True, stop=True)
                    last.then_inc(products_done.sem, 1)
                    pe.wait_ge(*mix_done.after(s))
                    turn(("mtr", l, t), [mlp[0:r, at, W + P * k:W + P * k + P] for k in range(4)])
                elif kind == "wout":
                    _, l, t, c = s
                    pe.wait_ge(*act_read.after(("otr", l, t)))
                    pe.wait_ge(*act_read.after(("mtr", l, t)))
                    by_token(s, place(t)[1], ROWS[t])[1].then_inc(products_done.sem, 1)
                elif kind == "pq":
                    _, l, g, e = s
                    if e == 0:
                        turned_ready("ffn", l, GROUPS[g])
                    by_column(s, e % 4, GCOLS[g])
                elif kind == "topk":
                    _, l, t, e = s
                    r, c0 = ROWS[t], place(t)[1]
                    if e == 0:
                        pe.wait_ge(*act_read.after(("pq", l, group_of(t), H - 1)))
                    n = UNIT_NUMBER[weight_unit(s)]
                    pe.wait_ge(w_in[n % NW], 16 * (n // NW + 1))
                    subT = weights[:, n % NW, 0:H * NKEYS].rearrange("p (a n) -> p a n", a=H)
                    b = take(s)
                    for p in range(2):
                        lo = DH * p
                        if p:
                            rows_change(last)
                        last = pe.matmul(b[0:r, NKEYS * p:NKEYS * p + NKEYS], qpT[lo:lo + DH, e, c0:c0 + r],
                                         subT[lo:lo + DH, e, :], start=True, stop=True)
                    last.then_inc(products_done.sem, 1)
                elif kind == "ple":
                    _, l, t, c = s
                    r, c0 = ROWS[t], place(t)[1]
                    n = UNIT_NUMBER[weight_unit(s)]
                    pe.wait_ge(w_in[n % NW], 16 * (n // NW + 1))
                    pe.wait_ge(ple_in, 32 * (2 * l + group_of(t) + 1))
                    w = weights[:, n % NW, 0:2 * D].rearrange("p (k n) -> p k n", k=2)
                    b = take(s)
                    for k in range(2):
                        last = pe.matmul(b[0:r, :], pT[:, k, c0:c0 + r], w[:, k, 512 * c:512 * c + 512],
                                         start=(k == 0), stop=(k == 1))
                    last.then_inc(products_done.sem, 1)
                elif kind == "gate":
                    _, l, t, c = s
                    r, c0 = ROWS[t], place(t)[1]
                    if c == 0:
                        turned_ready("ple", l, [t])
                    w = unit(s)
                    b = take(s)
                    for k in range(KD):
                        pe.matmul(b[0:r, :], xT[:, k, c0:c0 + r], w[:, k, :], start=(k == 0), stop=False)
                    pe.matmul(b[0:r, :], ones_row[0:1, 0:r], b_gate[0:1, 512 * c:512 * c + 512],
                              start=False, stop=True).then_inc(products_done.sem, 1)
                elif kind == "peer":
                    _, j, q = s
                    if j > 0:
                        l, t, e = ITEMS[j - 1]
                        m = 4 * (j - 1) + q
                        if q == 0 and e == 0 and (l, t) != tiles_in_order[0]:
                            before = tiles_in_order[tiles_in_order.index((l, t)) - 1]
                            pe.wait_ge(*experts_added.after(before))
                        pe.wait_ge(*diag_made.after((j - 1, q)))
                        for k in range(QUARTER):
                            n = (j - 1) * TOPK + QUARTER * q + k
                            pe.wait_ge(v_in[n % NV], 16 * (n // NV + 1))
                            first = e == 0 and q == 0 and k == 0
                            final = e == items_in_tile(t) - 1 and q == 3 and k == QUARTER - 1
                            for c in range(2):
                                last = pe.matmul(experts[c][0:ROWS[t], :], diag[:, m % 2, k, 0:ROWS[t]],
                                                 vrows[:, n % NV, 512 * c:512 * c + 512], start=first, stop=final)
                            last.then_inc(added.sem, 1)


GATES = [s for s in SCHEDULE if s[0] == "gate"]
GATE_NUMBER = {s: n for n, s in enumerate(GATES)}


def kernel(x_prompt, x_sample, cache_k, cache_v, p_prompt, p_sample, g_mix, w_in, g_sb_out, w_spatial,
           b_spatial, g_a_v, g_a_out, w_out, g_ffn, w_peer_q, peer_sub_keys, peer_u, peer_v, g_ple,
           w_ple_gate, b_ple_gate, w_ple, g_final):
    import concourse.bacc as bacc
    from concourse.bass_utils import run_bass_kernel_spmd

    def blocks(w, n):
        w = np.asarray(w)
        layers, k, cols = w.shape
        return w.reshape(layers, k // P, P, cols // n, n).transpose(0, 3, 2, 1, 4).reshape(layers, cols // n, P, -1)

    def by_block(g):
        return np.asarray(g).reshape(L, KD, P).transpose(2, 0, 1)

    p_all = np.concatenate([np.asarray(p_prompt)[:, 0], np.asarray(p_sample)[:, 0]], axis=1)
    g_out = np.concatenate([np.asarray(g_sb_out).reshape(L, W), np.asarray(g_a_out).reshape(L, W)], axis=1)
    arrays = {
        "x": np.concatenate([np.asarray(x_prompt)[0], np.asarray(x_sample)[0]], axis=0),
        "cache_kT": np.asarray(cache_k)[:, 0].reshape(L, PAST, 4, P).transpose(0, 3, 2, 1).reshape(L, P, -1),
        "cache_v": np.asarray(cache_v)[:, 0].reshape(L, PAST, W),
        "pT": p_all.transpose(0, 2, 1).reshape(L, 2, P, SEQ + DEC).transpose(0, 2, 1, 3),
        "gains": np.stack([by_block(g_mix), by_block(g_out), by_block(g_ple)], axis=2).reshape(P, -1),
        "w_in": blocks(w_in, 512),
        "w_out": blocks(w_out, 512),
        "w_peer_q": blocks(w_peer_q, 512),
        "w_ple_gate": blocks(w_ple_gate, 512),
        "w_ple": blocks(w_ple, D),
        "w_spatialT": np.asarray(w_spatial).transpose(0, 3, 1, 2).reshape(L, P, -1),
        "b_spatialT": np.asarray(b_spatial).transpose(0, 2, 1),
        "g_a_v": np.asarray(g_a_v).reshape(L, W),
        "g_ffn": np.asarray(g_ffn),
        "sub_keysT": np.asarray(peer_sub_keys).transpose(0, 2, 4, 1, 3).reshape(L, 1, P, -1),
        "peer_u": np.asarray(peer_u).reshape(L * EXPERTS, D),
        "peer_v": np.asarray(peer_v).reshape(L * EXPERTS, D),
        "b_ple_gate": np.asarray(b_ple_gate),
        "g_final": np.asarray(g_final).reshape(1, D),
    }
    arrays = {n: np.ascontiguousarray(a) for n, a in arrays.items()}
    nc = bacc.Bacc("TRN2", target_bir_lowering=False, num_devices=1)
    ins = {n: nc.dram_tensor(f"in_{n}", a.shape, F32, kind="ExternalInput").ap() for n, a in arrays.items()}
    shapes = {"y": (SEQ + DEC, D), "k": (L, SEQ + DEC, W), "v": (L, SEQ + DEC, W), "va": (L, DEC, W)}
    outs = {n: nc.dram_tensor(f"out_{n}", s, F32, kind="ExternalOutput").ap() for n, s in shapes.items()}
    encoder(nc, ins, outs)
    r = run_bass_kernel_spmd(nc, [{f"in_{n}": a for n, a in arrays.items()}], core_ids=[0]).results[0]
    y, k, v, va = (np.asarray(r[f"out_{n}"]) for n in shapes)
    heads = lambda a: a.reshape(L, 1, -1, H, DH)
    return (y[None, :SEQ], y[None, SEQ:], heads(k[:, :SEQ]), heads(v[:, :SEQ]), heads(k[:, SEQ:]),
            heads(v[:, SEQ:]), heads(va))
```

```python
from contextlib import ExitStack

import concourse.bass as bass
import numpy as np
from concourse import mybir

F32 = mybir.dt.float32
U32 = mybir.dt.uint32
ALU = mybir.AluOpType
ACT = mybir.ActivationFunctionType
AX_X = mybir.AxisListType.X

P = 128
D = 1024
KD = D // P
L = 2
SEQ, DEC, PAST = 512, 32, 256
NT = SEQ // P + 1
SAMPLE = NT - 1
ROWS = [P] * SAMPLE + [DEC]
GROUPS = [[0, 1], [2, 3, 4]]
GCOLS = [sum(ROWS[t] for t in g) for g in GROUPS]
H, DH = 8, 64
W = H * DH
NKEYS, EXPERTS, TOPK = 128, 128 * 128, 16
PLE = 256
EPS = 1e-6
MASKED = -1e30
BELOW = -3.0e38
RSQRT_SEED = 0x5F3759DF
NEWTON_STEPS = 3
NU, NV = 4, 4
NW = 2
ND = 2
NB = 4
QUARTER = 4
BY_DVE = 2
ADDED = 1

IN_PARTS = ["q", "k", "v", "ua", "va"]


def group_of(t):
    return 0 if t in GROUPS[0] else 1


def place(t):
    g = GROUPS[group_of(t)]
    i = g.index(t)
    return i, P * i


def in_turns(*columns):
    n = len(columns[0])
    out = []
    for i in range(n + len(columns) - 1):
        for d in reversed(range(len(columns))):
            if 0 <= i - d < n:
                out.append(columns[d][i - d])
    return out


def norm_stages(l, tiles, what):
    names = [(l, t, what) for t in tiles]
    return in_turns([("squares",) + x for x in names], [("scale",) + x for x in names],
                    [("turn",) + x for x in names])


def attention_stages(l, g):
    tiles = GROUPS[g]
    out = [("params", l)] if g == 0 else []
    out += norm_stages(l, tiles, "mix")
    out += [("q", l, g, b) for b in range(4)]
    out += in_turns(*([(k, l, t) for t in tiles] for k in ("k", "kt", "ktE")))
    out += [("v", l, t) for t in tiles]
    out += [("ua", l, t) for t in tiles]
    out += in_turns(*([(k, l, t) for t in tiles] for k in ("va", "vaN")))
    units = [(l, t, e) for t in tiles if t != SAMPLE for e in range(H)]
    n = len(units)
    for i in range(n + 3):
        if i >= 3:
            out.append(("attP",) + units[i - 3])
            if units[i - 3][2] == H - 1:
                out.append(("attM", l, units[i - 3][1]))
        if i >= 2 and i - 2 < n:
            out.append(("attE",) + units[i - 2])
        if i < n:
            out.append(("attZ",) + units[i])
        if 1 <= i <= n:
            out.append(("attS",) + units[i - 1])
        if i >= 4 and i - 4 < n and units[i - 4][2] == H - 1:
            out.append(("attN", l, units[i - 4][1]))
        if i >= 5 and i - 5 < n and units[i - 5][2] == H - 1:
            out.append(("attT", l, units[i - 5][1]))
    out += [("attN", l, units[-1][1]), ("mix", l, tiles[0]), ("attT", l, units[-1][1])]
    rest = tiles[1:]
    if SAMPLE in tiles:
        out += [("samZ", l), ("mixN", l, tiles[0]), ("samS", l), ("mix", l, rest[0]), ("mixT", l, tiles[0]),
                ("samE", l), ("samX", l), ("mixN", l, rest[0]), ("mix", l, rest[1]), ("samP", l),
                ("attM", l, SAMPLE), ("mixT", l, rest[0]), ("attN", l, SAMPLE), ("mixN", l, rest[1]),
                ("attT", l, SAMPLE), ("mixT", l, rest[1])]
    else:
        out += [("mixN", l, tiles[0]), ("mix", l, rest[0]), ("mixT", l, tiles[0]), ("mixN", l, rest[0]),
                ("mixT", l, rest[0])]
    outs = [(l, t, c) for c in range(2) for t in tiles]
    out += in_turns([("wout",) + x for x in outs], [("woutA",) + x for x in outs])
    out += norm_stages(l, tiles, "ffn")
    out += [("pq", l, g, e) for e in range(H)]
    return out


def routing_stages(l, tiles):
    names = [(l, t, e) for t in tiles for e in range(H)]
    out = in_turns(*([(k,) + x for x in names] for k in ("score", "halves", "sums", "choice")))
    if SAMPLE in tiles:
        at = out.index(("choice", l, SAMPLE, H - 1))
        out.insert(at + 1, ("pack", l))
    return out


def embedding_stages(l, g, by_tile=False):
    tiles = GROUPS[g]
    out = embedding_products(l, g)
    if by_tile:
        for t in tiles:
            out += embedding_tile(l, t)
        return out
    out += norm_stages(l, tiles, "ple")
    gates = [(l, t, c) for c in range(2) for t in tiles]
    out += in_turns([("gate",) + x for x in gates], [("gateA",) + x for x in gates])
    if l == L - 1:
        out += in_turns([("squares", L, t, "final") for t in tiles], [("scale", L, t, "final") for t in tiles])
    return out


def embedding_products(l, g):
    return [("pleparams", l, g)] + [("ple", l, t, c) for t in GROUPS[g] for c in range(2)]


def embedding_tile(l, t):
    return (norm_stages(l, [t], "ple") + [("gate", l, t, 0), ("gate", l, t, 1), ("gateA", l, t, 0),
            ("gateA", l, t, 1), ("squares", L, t, "final"), ("scale", L, t, "final")])


ITEMS = []
FIRST_ITEM = {}
for l_ in range(L):
    for g_ in range(2):
        FIRST_ITEM[l_, g_] = len(ITEMS)
        for t_ in GROUPS[g_]:
            ITEMS += [(l_, t_, h_) for h_ in range(2 if t_ == SAMPLE else H)]
ITEM_COUNT = len(ITEMS)


def items_in_tile(t):
    return 2 if t == SAMPLE else H


def beside(gathers, work):
    total = sum(COST.get(s[0], 0) for s in work)
    out, done, n = [], 0.0, 0
    for i, s in enumerate(gathers):
        out.append(s)
        while n < len(work) and done + COST.get(work[n][0], 0) / 2 <= total * (i + 1) / len(gathers):
            done += COST.get(work[n][0], 0)
            out.append(work[n])
            n += 1
    return out + work[n:]


COST = {"squares": 1, "scale": 3, "turn": 2, "q": 4, "k": 7, "kt": 1, "ktE": 1, "v": 7, "ua": 7, "va": 7,
        "vaN": 6, "attZ": 2, "attS": 1, "attE": 2, "attP": 2, "attM": 1, "attN": 5, "attT": 1, "samZ": 11,
        "samS": 4, "samE": 4, "samX": 2, "samP": 10, "mix": 4, "mixN": 7, "mixT": 1, "wout": 7, "woutA": 1,
        "pq": 4, "score": 1, "halves": 4, "sums": 4, "choice": 5, "ple": 2, "gate": 8, "gateA": 2}


def schedule():
    def gathers(item, last_item, step=0, last_step=0):
        return [("peer", j, k) for j in range(item, last_item + 1) for k in range(TOPK)
                if (item, step) <= (j, k) < (last_item, last_step)]

    def behind(item):
        return (item + 1, ADDED + 1)

    b = [FIRST_ITEM[0, 0], FIRST_ITEM[0, 1], FIRST_ITEM[1, 0], FIRST_ITEM[1, 1], ITEM_COUNT]
    out = attention_stages(0, 0)
    first = routing_stages(0, [0])
    head = first.index(("choice", 0, 0, 1)) + 1
    out += first[:head]
    out += beside(gathers(0, 5), first[head:])
    out += beside(gathers(5, b[1]), routing_stages(0, [1]) + attention_stages(0, 1) + routing_stages(0, [2]))
    for k in (1, 2):
        l = k // 2
        own, other = k % 2, 1 - k % 2
        start, step = behind(b[k])
        late = routing_stages(l, [SAMPLE, 3] if own else [1])
        out += beside(gathers(b[k], start, 0, step), late[:len(late) // 6])
        out += beside(gathers(start, b[k + 1], step), late[len(late) // 6:]
                      + embedding_stages(k - 1 and 0, other) + attention_stages((k + 1) // 2, other)
                      + routing_stages((k + 1) // 2, [2 if other else 0]))
    start, step = behind(b[3])
    late = routing_stages(1, [SAMPLE, 3])
    out += beside(gathers(b[3], start, 0, step), late[:len(late) // 6])
    two, step2 = behind(b[3] + H)
    three, step3 = behind(b[3] + 2 * H)
    end, step4 = behind(ITEM_COUNT)
    out += beside(gathers(start, two, step, step2), late[len(late) // 6:] + embedding_stages(1, 0)
                  + embedding_products(1, 1))
    out += beside(gathers(two, three, step2, step3), embedding_tile(1, 2))
    out += beside(gathers(three, end, step3, step4), embedding_tile(1, 3))
    out += embedding_tile(1, SAMPLE)
    return out


SCHEDULE = schedule()
assert len(set(SCHEDULE)) == len(SCHEDULE)


class Signal:

    def __init__(self, sem, events):
        self.sem = sem
        self.count = {e: n + 1 for n, e in enumerate(events)}

    def after(self, event):
        return self.sem, self.count[event]


def bank_uses(s):
    k = s[0]
    if k == "turn":
        return [s + (half,) for half in range(2)]
    if k in ("q", "k", "kt", "v", "ua", "va", "attZ", "attT", "mix", "mixT", "wout", "pq", "score", "ple",
             "gate"):
        return [s]
    if k in ("samZ", "samE"):
        return [s + (half,) for half in range(2)]
    return []


def releases(s):
    k = s[0]
    if k in ("turn", "q", "k", "v", "ua", "va", "attT", "mixT", "pq", "score", "ple", "gate"):
        return [("act", u) for u in bank_uses(s)]
    if k == "attE":
        return [("act", ("attZ",) + s[1:])]
    if k in ("ktE", "woutA"):
        return [("dve", (k[:-1],) + s[1:])]
    if k == "mixN":
        return [("dve", ("mix",) + s[1:])]
    if k == "samS":
        return [("dve", ("samZ", s[1], half)) for half in range(2)]
    if k == "samX":
        return [("dve", ("samE", s[1], half)) for half in range(2)]
    return []


USES = [u for s in SCHEDULE for u in bank_uses(s)]
BANK = {u: n % NB for n, u in enumerate(USES)}
TAKEN_BEFORE = {u: USES[n - NB] for n, u in enumerate(USES) if n >= NB}
RELEASES = [r for s in SCHEDULE for r in releases(s)]
RELEASED_BY = {u: who for who, u in RELEASES}


def weight_unit(s):
    k = s[0]
    if k in IN_PARTS:
        return ("in", s[1], s[2] if k == "q" else group_of(s[2]), IN_PARTS.index(k))
    if k in ("wout", "gate"):
        return (k, s[1], group_of(s[2]), s[3])
    if k == "ple":
        return (k, s[1], group_of(s[2]), 0)
    if k == "pq":
        return (k, s[1], s[2], s[3] // 4)
    if k == "score":
        return (k, s[1], group_of(s[2]), 0)
    return None


UNITS = []
LAST_STAGE = {}
for s_ in SCHEDULE:
    u_ = weight_unit(s_)
    if u_ is not None:
        if u_ not in LAST_STAGE:
            UNITS.append(u_)
        LAST_STAGE[u_] = s_
UNIT_NUMBER = {u: n for n, u in enumerate(UNITS)}
NORMS = [s[1:] for s in SCHEDULE if s[0] == "squares"]
NORM_NUMBER = {s: n for n, s in enumerate(NORMS)}
FINALS = [x for x in NORMS if x[2] == "final"]
ROUTES = [s[1:] for s in SCHEDULE if s[0] == "choice"]
ROUTE_NUMBER = {s: n for n, s in enumerate(ROUTES)}
LAST_ROUTE = {l_: [x for x in ROUTES if x[0] == l_][-1] for l_ in range(L)}
KS = [s for s in SCHEDULE if s[0] == "k"]
K_NUMBER = {s: n for n, s in enumerate(KS)}
HEADS = [s[1:] for s in SCHEDULE if s[0] == "attZ"]
HEAD_NUMBER = {s: n for n, s in enumerate(HEADS)}
MOVES = [s[1:] for s in SCHEDULE if s[0] == "attM"]
GATES = [s[1:] for s in SCHEDULE if s[0] == "gate"]
GATE_NUMBER = {s: n for n, s in enumerate(GATES)}


def adder(j, k):
    return "dve" if ITEMS[j][1] != SAMPLE and k % QUARTER == BY_DVE else "pe"


def encoder(nc, i, o):
    with ExitStack() as ctx:
        def sb(name, shape, dt=F32):
            return ctx.enter_context(nc.sbuf_tensor(name, shape, dt))

        def sem(name):
            return ctx.enter_context(nc.semaphore(name))

        h = sb("h", [P, NT, D])
        xn2 = sb("xn2", [P, NT, D])
        kT = sb("kT", [P, 4, SEQ + DEC])
        v = sb("v", [P, NT, W])
        ident = sb("ident", [P, P])
        spread = sb("spread", [P, DEC])
        neg_tri = sb("neg_tri", [P, P])
        neg_ones = sb("neg_ones", [P, P])
        mask = sb("mask", [P, P])
        ones_row = sb("ones_row", [1, P])
        iota16 = sb("iota16", [P, TOPK])
        gains = sb("gains", [P, L, 3, KD])
        kcT = sb("kcT", [P, 4, PAST])
        vc = sb("vc", [P, PAST // P, W])
        wsT = sb("wsT", [P, H, P])
        b_sp = sb("b_sp", [P, H])
        g_av = sb("g_av", [P, W])
        g_row = sb("g_row", [P, D])
        pT = sb("pT", [P, 2, GCOLS[1]])
        weights = sb("weights", [P, NW, KD * 512])
        xT = sb("xT", [P, KD, GCOLS[1]])
        xs = sb("xs", [P, 2, D])
        routing = sb("routing", [P, H * GCOLS[1]])
        qT = routing[:, 0:4 * GCOLS[1]].rearrange("p (a n) -> p a n", a=4)
        ktok = routing[:, 4 * GCOLS[1]:4 * GCOLS[1] + 2 * W].rearrange("p (a n) -> p a n", a=2)
        qpT = routing[:, :].rearrange("p (a n) -> p a n", a=H)
        mlp = sb("mlp", [P, 3, D])
        norm_work = sb("norm_work", [P, 2 * W])
        osb = norm_work[:, 0:W]
        sq = norm_work[:, W:2 * W]
        b_gate = norm_work[0:1, :]
        work = sb("work", [P, 4 * 512])
        sp = work[:, 0:1024].rearrange("p (a n) -> p a n", a=2)
        att = work[:, 1024:2048].rearrange("p (a n) -> p a n", a=2)
        ss = sb("ss", [P, 2])
        rs = sb("rs", [P, 2])
        ss8 = sb("ss8", [P, H])
        newton = sb("newton", [P, 2, H])
        square = TOPK * TOPK
        rep = work[:, 0:square].rearrange("p (a n) -> p a n", a=2)
        cand = work[:, square:2 * square].rearrange("p (a b) -> p a b", a=TOPK)
        cand2 = work[:, 2 * square:3 * square].rearrange("p (a b) -> p a b", a=TOPK)
        hot = work[:, 3 * square:5 * square].rearrange("p (a n) -> p a n", a=2)
        st = work[:, 5 * square:5 * square + 4 * NKEYS].rearrange("p (a n) -> p a n", a=2)
        top = sb("top", [P, 2, TOPK])
        topi = sb("topi", [P, 2, 2, TOPK], U32)
        best = sb("best", [P, TOPK])
        pos = sb("pos", [P, TOPK], U32)
        pos2 = sb("pos2", [P, 2, TOPK], U32)
        part = sb("part", [P, 2, TOPK])
        negm = sb("negm", [P, 1])
        ex = sb("ex", [P, TOPK])
        esum = sb("esum", [P, 2])
        idx = sb("idx", [P, NT, H * TOPK], U32)
        gate = sb("gate", [P, NT, H * TOPK])
        idx_sam = sb("idx_sam", [P, 2 * TOPK], U32)
        gate_sam = sb("gate_sam", [P, 2 * TOPK])
        urows = sb("urows", [P, NU, D])
        vrows = sb("vrows", [P, NV, D])
        hid = sb("hid", [P, 2, TOPK])
        act_hid = sb("act_hid", [P, 2, TOPK])
        amount = sb("amount", [P, 2, TOPK])
        diag = sb("diag", [P, ND, QUARTER, P])

        def bank(name):
            return ctx.enter_context(nc.psum_tensor(name, [P, 512], F32))

        experts = [bank("experts0"), bank("experts1")]
        banks = [bank(f"bank{n}") for n in range(NB)]
        att_out = bank("att_out")

        const_made = sem("const_made")
        h_in = [sem(f"h_in{t}") for t in range(NT)]
        gains_in = sem("gains_in")
        params_in = sem("params_in")
        tril_made = sem("tril_made")
        ple_in = sem("ple_in")
        final_in = sem("final_in")
        w_in = [sem(f"w_in{n}") for n in range(NW)]
        k_out = [sem("k_out0"), sem("k_out1")]
        v_out = sem("v_out")
        va_out = sem("va_out")
        y_out = [sem("y_out0"), sem("y_out1")]
        packed = sem("packed")
        u_in = [sem(f"u_in{n}") for n in range(NU)]
        v_in = [sem(f"v_in{n}") for n in range(NV)]
        dve_chain, act_chain, pool_chain, pe_chain = (sem(n) for n in ("dve_chain", "act_chain",
                                                                       "pool_chain", "pe_chain"))

        def of(*kinds):
            return [s[1:] for s in SCHEDULE if s[0] in kinds]

        products_done = Signal(sem("products_done"), USES)
        act_read = Signal(sem("act_read"), [u for who, u in RELEASES if who == "act"])
        dve_read = Signal(sem("dve_read"), [u for who, u in RELEASES if who == "dve"])
        bank_read = {"act": act_read, "dve": dve_read}
        squares_summed = Signal(sem("squares_summed"), NORMS)
        normed = Signal(sem("normed"), of("scale"))
        va_normed = Signal(sem("va_normed"), of("vaN"))
        log_done = Signal(sem("log_done"), of("attZ", "samZ"))
        softplus_done = Signal(sem("softplus_done"), of("attS", "samS"))
        decay_done = Signal(sem("decay_done"), of("attE"))
        sample_weights_done = Signal(sem("sample_weights_done"), of("samX"))
        heads_done = Signal(sem("heads_done"), of("attP", "samP"))
        att_moved = Signal(sem("att_moved"), MOVES)
        att_normed = Signal(sem("att_normed"), of("attN"))
        mix_done = Signal(sem("mix_done"), of("mixN"))
        best_found = Signal(sem("best_found"), ROUTES)
        exps_done = Signal(sem("exps_done"), ROUTES)
        halves_done = Signal(sem("halves_done"), ROUTES)
        routed = Signal(sem("routed"), ROUTES)
        gated = Signal(sem("gated"), of("gateA"))
        steps = [(j, s) for j in range(ITEM_COUNT) for s in range(TOPK)]
        dotted = Signal(sem("dotted"), steps)
        gelu_done = Signal(sem("gelu_done"), range(ITEM_COUNT))
        amounts_done = Signal(sem("amounts_done"), range(ITEM_COUNT))
        diag_made = Signal(sem("diag_made"), [(j, q) for j in range(ITEM_COUNT) for q in range(4)])
        added = {who: Signal(sem(f"added_by_{who}"), [x for x in steps if adder(*x) == who])
                 for who in ("pe", "dve")}
        tiles_in_order = [(l, t) for l, t, e in ITEMS if e == 0]
        experts_added = Signal(sem("experts_added"), tiles_in_order)

        def h_ready(eng, l, t, kind):
            if kind == "mix" and l == 0:
                eng.wait_ge(h_in[t], 16)
            elif kind == "mix" or kind == "final":
                eng.wait_ge(*gated.after((l - 1, t, 1)))
            elif kind == "ffn":
                eng.wait_ge(*dve_read.after(("wout", l, t, 1)))
            else:
                eng.wait_ge(*experts_added.after((l, t)))

        PARAMS, PACKED = 16 * 6, 16 * 11

        SAMPLE_PARTS = [(0, P, 2 * H * DEC), (1, DEC, H * DEC)]

        block = ctx.enter_context(nc.Block())

        @block.sync
        def _(sp_eng):
            eng = sp_eng

            def load_unit(n):
                kind, l, g, c = UNITS[n]
                if n >= NW:
                    eng.wait_ge(*products_done.after(LAST_STAGE[UNITS[n - NW]]))
                src = {"in": i["w_in"], "wout": i["w_out"], "pq": i["w_peer_q"],
                       "gate": i["w_ple_gate"], "ple": i["w_ple"], "score": i["sub_keysT"]}[kind][l, c]
                eng.dma_start(weights[:, n % NW, 0:src.shape[1]], src).then_inc(w_in[n % NW], 16)

            for t in GROUPS[0]:
                eng.dma_start(h[0:ROWS[t], t, :], i["x"][P * t:P * t + ROWS[t], :]).then_inc(h_in[t], 16)
            load_unit(0)
            load_unit(1)
            eng.dma_start(gains[:, :, :, :].rearrange("p a b c -> p (a b c)"), i["gains"]).then_inc(gains_in, 16)

            for s in SCHEDULE:
                if s[0] == "params":
                    l = s[1]
                    if l > 0:
                        eng.wait_ge(*routed.after(LAST_ROUTE[l - 1]))
                    for dst, src in ((kcT[:, :, :].rearrange("p a n -> p (a n)"), i["cache_kT"][l]),
                                     (vc[:, :, :], i["cache_v"][l].rearrange("(b p) n -> p b n", p=P)),
                                     (wsT[:, :, :].rearrange("p a n -> p (a n)"), i["w_spatialT"][l]),
                                     (b_sp[:, :], i["b_spatialT"][l]),
                                     (g_av[:, :], i["g_a_v"][l:l + 1, :].to_broadcast([P, W])),
                                     (g_row[:, :], i["g_ffn"][l:l + 1, :].to_broadcast([P, D]))):
                        eng.dma_start(dst, src).then_inc(params_in, 16)
                    if l == 0:
                        for t in GROUPS[1]:
                            eng.dma_start(h[0:ROWS[t], t, :], i["x"][P * t:P * t + ROWS[t], :])\
                               .then_inc(h_in[t], 16)
                elif s[0] == "pleparams":
                    _, l, g = s
                    if (l, g) != (0, 0):
                        before = (l, 0) if g == 1 else (l - 1, 1)
                        eng.wait_ge(*gated.after((before[0], GROUPS[before[1]][-1], 1)))
                    n = GCOLS[g]
                    eng.dma_start(pT[:, :, 0:n], i["pT"][l][:, :, P * GROUPS[g][0]:P * GROUPS[g][0] + n])\
                       .then_inc(ple_in, 16)
                    here = SCHEDULE.index(s)
                    eng.wait_ge(*routed.after([x[1:] for x in SCHEDULE[:here] if x[0] == "choice"][-1]))
                    eng.dma_start(b_gate[:, :], i["b_ple_gate"][l:l + 1, :]).then_inc(ple_in, 16)
                elif s[0] == "k":
                    _, l, t = s
                    eng.wait_ge(*act_read.after(s))
                    eng.dma_start(o["k"][l, P * t:P * t + ROWS[t], :], ktok[0:ROWS[t], K_NUMBER[s] % 2, :])\
                       .then_inc(k_out[K_NUMBER[s] % 2], 16)
                elif s[0] == "v":
                    _, l, t = s
                    eng.wait_ge(*act_read.after(s))
                    eng.dma_start(o["v"][l, P * t:P * t + ROWS[t], :], v[0:ROWS[t], t, :]).then_inc(v_out, 16)
                elif s[0] == "vaN" and s[2] == SAMPLE:
                    eng.wait_ge(*va_normed.after(s[1:]))
                    eng.dma_start(o["va"][s[1]], mlp[0:DEC, place(SAMPLE)[0], 0:W]).then_inc(va_out, 16)
                elif s[0] == "pack":
                    l = s[1]
                    eng.wait_ge(*routed.after((l, SAMPLE, H - 1)))
                    for b in range(4):
                        lo, hi = 32 * b, 32 * b + 32
                        eng.dma_start(idx_sam[lo:hi, :], idx[0:DEC, SAMPLE, lo:hi]).then_inc(packed, 16)
                        eng.dma_start(gate_sam[lo:hi, :], gate[0:DEC, SAMPLE, lo:hi]).then_inc(packed, 16)
                        if b:
                            eng.dma_start(xn2[lo:hi, SAMPLE, :], xn2[0:DEC, SAMPLE, :]).then_inc(packed, 16)
                elif s[0] == "turn" and s[1:] == (L - 1, GROUPS[1][-1], "ffn"):
                    for t in GROUPS[1]:
                        eng.wait_ge(*normed.after((L - 1, t, "ffn")))
                    eng.dma_start(g_row[:, :], i["g_final"].to_broadcast([P, D])).then_inc(final_in, 16)
                elif s[0] == "scale" and s[3] == "final":
                    t, b = s[2], NORM_NUMBER[s[1:]] % 2
                    eng.wait_ge(*normed.after(s[1:]))
                    eng.dma_start(o["y"][P * t:P * t + ROWS[t], :], xs[0:ROWS[t], b, :]).then_inc(y_out[b], 16)
                u = weight_unit(s)
                if u is not None and LAST_STAGE[u] == s and UNIT_NUMBER[u] + NW < len(UNITS):
                    load_unit(UNIT_NUMBER[u] + NW)
            for n in range(2):
                eng.wait_ge(k_out[n], 16 * len([s for s in KS if K_NUMBER[s] % 2 == n]))
                eng.wait_ge(y_out[n], 16 * len([x for x in FINALS if NORM_NUMBER[x] % 2 == n]))
            eng.wait_ge(v_out, 16 * L * NT)
            eng.wait_ge(va_out, 16 * L)


        @block.gpsimd
        def _(pool):
            def select(out, pattern, op, fill, base=0, mult=1):
                pool.affine_select(out=out, in_=out, pattern=pattern, compare_op=op, fill=fill,
                                   base=base, channel_multiplier=mult).then_inc(pool_chain, 1)
                chain[0] += 1

            chain = [0]
            for buf, value in ((ident, 0.0), (spread, 0.0), (neg_tri, -1.0), (neg_ones, -1.0),
                               (mask, 0.0), (ones_row, 1.0)):
                pool.memset(buf[:, :], value).then_inc(pool_chain, 1)
                chain[0] += 1
            pool.wait_ge(pool_chain, chain[0])
            select(ident[:, :], [[-1, P]], ALU.not_equal, 1.0)
            select(neg_tri[:, :], [[-1, P]], ALU.is_ge, 0.0)
            select(mask[:, :], [[1, P]], ALU.is_gt, MASKED, mult=-1)
            for b in range(4):
                if b:
                    pool.wait_ge(pool_chain, chain[0])
                select(spread[:, :], [[-1, DEC]], ALU.not_equal, 1.0, base=-32 * b)
            pool.iota(iota16[:, :], [[1, TOPK]], base=0, channel_multiplier=0,
                      allow_small_or_imprecise_dtypes=True).then_inc(pool_chain, 1)
            pool.wait_ge(pool_chain, chain[0] + 1)
            pool.memset(hid[:, :, :], 0.0).then_inc(const_made, 1)

            def gather(table, rows, where, index, landed):
                pool.indirect_dma_start(out=rows[:, where, :], out_offset=None, in_=table,
                                        in_offset=bass.IndirectOffsetOnAxis(ap=index, axis=0))\
                    .then_inc(landed[where], 16)

            def column(j, s):
                _, t, e = ITEMS[j]
                c = e * TOPK + s
                return idx_sam[:, c:c + 1] if t == SAMPLE else idx[:, t, c:c + 1]

            for stage in SCHEDULE:
                if stage[0] == "params":
                    pool.wait_ge(params_in, PARAMS * (stage[1] + 1))
                    pool.affine_select(out=wsT[:, :, :], in_=wsT[:, :, :], pattern=[[0, H], [1, P]],
                                       compare_op=ALU.is_ge, fill=0.0, base=0, channel_multiplier=-1)\
                        .then_inc(tril_made, 1)
                elif stage[0] == "peer":
                    _, j, k = stage
                    if j < ITEM_COUNT:
                        l, t, e = ITEMS[j]
                        if k == 0:
                            if t == SAMPLE:
                                pool.wait_ge(packed, PACKED * (l + 1))
                            else:
                                pool.wait_ge(*routed.after((l, t, e)))
                        n = j * TOPK + k
                        if n >= NU:
                            pool.wait_ge(*dotted.after(steps[n - NU]))
                        gather(i["peer_u"], urows, n % NU, column(j, k), u_in)
                    if 0 < j <= ITEM_COUNT:
                        n = (j - 1) * TOPK + k
                        if n >= NV:
                            before = steps[n - NV]
                            pool.wait_ge(*added[adder(*before)].after(before))
                        gather(i["peer_v"], vrows, n % NV, column(j - 1, k), v_in)

        @block.scalar
        def _(act):
            chain = [0]

            def mark(ins):
                chain[0] += 1
                ins.then_inc(act_chain, 1)

            def settle():
                act.wait_ge(act_chain, chain[0])

            def from_bank(use, out, func=ACT.Copy, rows=P, cols=512, **kw):
                act.wait_ge(*products_done.after(use))
                act.activation(out, banks[BANK[use]][0:rows, 0:cols], func, **kw)\
                    .then_inc(act_read.sem, 1)

            def turned(use, l, gain, k0, out):
                act.wait_ge(*products_done.after(use))
                rows = out.shape[2]
                for k in range(4):
                    last = act.activation(out[:, k, :], banks[BANK[use]][:, P * k:P * k + rows], ACT.Copy,
                                          scale=gains[:, l, gain, k0 + k:k0 + k + 1])
                last.then_inc(act_read.sem, 1)

            act.wait_ge(gains_in, 16)
            for s in SCHEDULE:
                kind = s[0]
                if kind == "squares":
                    _, l, t, what = s
                    r, n = ROWS[t], NORM_NUMBER[s[1:]]
                    h_ready(act, l, t, what)
                    if n >= 2:
                        before = NORMS[n - 2]
                        if before[2] == "final":
                            act.wait_ge(y_out[n % 2], 16 * len([x for x in FINALS if NORM_NUMBER[x] < n
                                                                and NORM_NUMBER[x] % 2 == n % 2]))
                        elif before[2] != "ffn":
                            act.wait_ge(*products_done.after(("turn",) + before + (1,)))
                        else:
                            act.wait_ge(*normed.after(before))
                    act.activation(xs[0:r, n % 2, :], h[0:r, t, :], ACT.Square,
                                   accum_out=ss[0:r, n % 2:n % 2 + 1]).then_inc(squares_summed.sem, 1)
                elif kind == "turn":
                    _, l, t, what = s
                    r, c0 = ROWS[t], place(t)[1]
                    for half in range(2):
                        use = s + (half,)
                        out = xT[:, 4 * half:4 * half + 4, c0:c0 + r]
                        if what == "ffn":
                            act.wait_ge(*products_done.after(use))
                            act.activation(out, banks[BANK[use]][:, :].rearrange("p (a n) -> p a n", a=4)[:, :, 0:r],
                                           ACT.Copy).then_inc(act_read.sem, 1)
                        else:
                            turned(use, l, 0 if what == "mix" else 2, 4 * half, out)
                elif kind == "q":
                    _, l, g, b = s
                    from_bank(s, qT[:, b, 0:GCOLS[g]], cols=GCOLS[g], scale=DH ** -0.5)
                elif kind == "k":
                    _, l, t = s
                    n = K_NUMBER[s]
                    if n >= 2:
                        act.wait_ge(k_out[n % 2], 16 * (n // 2))
                        act.wait_ge(*products_done.after(("kt",) + KS[n - 2][1:]))
                    from_bank(s, ktok[0:ROWS[t], n % 2, :], rows=ROWS[t])
                elif kind == "v":
                    _, l, t = s
                    if l > 0:
                        act.wait_ge(v_out, 16 * NT * l)
                    from_bank(s, v[0:ROWS[t], t, :], rows=ROWS[t])
                elif kind in ("ua", "va"):
                    _, l, t = s
                    at = 0 if kind == "va" else W
                    if kind == "va" and t == SAMPLE and l > 0:
                        act.wait_ge(va_out, 16 * l)
                    from_bank(s, mlp[0:ROWS[t], place(t)[0], at:at + W], ACT.Gelu, rows=ROWS[t])
                elif kind in ("attZ", "samZ"):
                    if kind == "attZ":
                        n = HEAD_NUMBER[s[1:]]
                        cols = P * (s[2] + 1)
                        parts = [(s, sp[:, n % 2, 0:cols])]
                        if n >= 2:
                            act.wait_ge(*decay_done.after(HEADS[n - 2]))
                    else:
                        parts = [(("samZ", s[1], 0), sp[:, 0, :]),
                                 (("samZ", s[1], 1), sp[0:DEC, 1, 0:H * DEC])]
                        for e in (H - 2, H - 1):
                            act.wait_ge(*decay_done.after((s[1], SAMPLE - 1, e)))
                    for use, x in parts:
                        act.wait_ge(*products_done.after(use))
                        r, cols = x.shape
                        mark(act.activation(x, banks[BANK[use]][0:r, 0:cols], ACT.Abs))
                    settle()
                    for _, x in parts:
                        mark(act.activation(x, x, ACT.Exp, scale=-1.0))
                    settle()
                    for _, x in parts:
                        last = act.activation(x, x, ACT.Ln, bias=1.0)
                        if x is not parts[-1][1]:
                            mark(last)
                    last.then_inc(log_done.sem, 1)
                elif kind == "attE":
                    z, n = ("attZ",) + s[1:], HEAD_NUMBER[s[1:]]
                    act.wait_ge(*decay_done.after(s[1:]))
                    if n >= 2:
                        act.wait_ge(*heads_done.after(HEADS[n - 2]))
                    cols = P * (s[2] + 1)
                    act.activation(att[:, n % 2, 0:cols], banks[BANK[z]][:, 0:cols], ACT.Exp)\
                        .then_inc(act_read.sem, 1)
                elif kind == "samX":
                    act.wait_ge(*dve_read.after(("samE", s[1], 1)))
                    act.activation(att[:, 0, :], att[:, 0, :], ACT.Exp)
                    act.activation(att[0:DEC, 1, 0:H * DEC], att[0:DEC, 1, 0:H * DEC], ACT.Exp)\
                        .then_inc(sample_weights_done.sem, 1)
                elif kind == "attM":
                    _, l, t = s
                    n = MOVES.index(s[1:])
                    act.wait_ge(*heads_done.after((l,) if t == SAMPLE else (l, t, H - 1)))
                    if n:
                        act.wait_ge(*products_done.after(("attT",) + MOVES[n - 1]))
                    act.activation(osb[0:ROWS[t], :], att_out[0:ROWS[t], :], ACT.Copy).then_inc(att_moved.sem, 1)
                elif kind in ("attT", "mixT"):
                    _, l, t = s
                    k0, c0 = (0 if kind == "attT" else 4), place(t)[1]
                    turned(s, l, 1, k0, xT[:, k0:k0 + 4, c0:c0 + ROWS[t]])
                elif kind == "pq":
                    _, l, g, e = s
                    if e == 0:
                        for n in range(2):
                            act.wait_ge(k_out[n], 16 * len([x for x in KS if K_NUMBER[x] % 2 == n
                                                            and (x[1], group_of(x[2])) <= (l, g)]))
                    from_bank(s, qpT[:, e, 0:GCOLS[g]], cols=GCOLS[g])
                elif kind == "score":
                    _, l, t, e = s
                    r, n = ROWS[t], ROUTE_NUMBER[s[1:]]
                    if n >= 2:
                        act.wait_ge(*halves_done.after(ROUTES[n - 2]))
                    from_bank(s, st[0:r, n % 2, :], rows=r, cols=2 * NKEYS)
                elif kind == "choice":
                    r = ROWS[s[2]]
                    act.wait_ge(*best_found.after(s[1:]))
                    act.activation(ex[0:r, :], best[0:r, :], ACT.Exp, bias=negm[0:r, 0:1],
                                   accum_out=esum[0:r, 0:1]).then_inc(exps_done.sem, 1)
                elif kind == "ple":
                    _, l, t, c = s
                    from_bank(s, mlp[0:ROWS[t], place(t)[0], 512 * c:512 * c + 512], rows=ROWS[t])
                elif kind == "gate":
                    _, l, t, c = s
                    n = GATE_NUMBER[s[1:]]
                    if n >= 2:
                        act.wait_ge(*gated.after(GATES[n - 2]))
                    from_bank(s, sp[0:ROWS[t], n % 2, :], ACT.Sigmoid, rows=ROWS[t])
                elif kind == "peer":
                    _, j, k = s
                    if k == 0 and 0 < j <= ITEM_COUNT:
                        act.wait_ge(*dotted.after((j - 1, TOPK - 1)))
                        act.activation(act_hid[:, (j - 1) % 2, :], hid[:, (j - 1) % 2, :], ACT.Gelu)\
                            .then_inc(gelu_done.sem, 1)

        @block.vector
        def _(dve):
            chain = [0]

            def mark(ins):
                chain[0] += 1
                ins.then_inc(dve_chain, 1)

            def settle():
                dve.wait_ge(dve_chain, chain[0])

            def link(ins):
                mark(ins)
                settle()

            def root(out, x, scale):
                r, n = x.shape
                y, half = newton[0:r, 0, 0:n], newton[0:r, 1, 0:n]
                link(dve.tensor_scalar(x, x, scale, EPS, ALU.mult, ALU.add))
                link(dve.tensor_scalar(half.bitcast(U32), x.bitcast(U32), 1, None, ALU.logical_shift_right))
                link(dve.tensor_scalar(y.bitcast(U32), half.bitcast(U32), -1.0, float(RSQRT_SEED),
                                       ALU.mult, ALU.add))
                for step in range(NEWTON_STEPS):
                    link(dve.tensor_tensor(half, y, y, ALU.mult))
                    link(dve.tensor_tensor(half, half, x, ALU.mult))
                    link(dve.tensor_scalar(half, half, -0.5, 1.5, ALU.mult, ALU.add))
                    link(dve.tensor_tensor(out if step == NEWTON_STEPS - 1 else y, y, half, ALU.mult))

            def head_norm(x, r):
                link(dve.tensor_tensor(sq[0:r, :], x, x, ALU.mult))
                link(dve.tensor_reduce(ss8[0:r, :], sq[0:r, :].rearrange("p (a n) -> p a n", a=H), AX_X, ALU.add))
                root(ss8[0:r, :], ss8[0:r, :], 1.0 / DH)
                x3 = x.rearrange("p (a n) -> p a n", a=H)
                return dve.tensor_tensor(x3, x3, ss8[0:r, :].unsqueeze(2).to_broadcast([r, H, DH]), ALU.mult)

            def top16(out, where, x, scratch):
                for a, w, b, _ in zip(out, where, x, scratch):
                    mark(dve.max(a[:, 0:8], b))
                settle()
                for a, w, b, c in zip(out, where, x, scratch):
                    mark(dve.max_index(w[:, 0:8], a[:, 0:8], b))
                    mark(dve.match_replace(c, a[:, 0:8], b, BELOW))
                settle()
                for a, w, b, c in zip(out, where, x, scratch):
                    mark(dve.max(a[:, 8:16], c))
                settle()
                for a, w, b, c in zip(out, where, x, scratch):
                    mark(dve.max_index(w[:, 8:16], a[:, 8:16], c))
                settle()

            def best_of_halves(s):
                _, l, t, e = s
                r, n = ROWS[t], ROUTE_NUMBER[s[1:]]
                dve.wait_ge(*act_read.after(("score", l, t, e)))
                top16([top[0:r, p, :] for p in range(2)], [topi[0:r, n % 2, p, :] for p in range(2)],
                      [st[0:r, n % 2, NKEYS * p:NKEYS * p + NKEYS] for p in range(2)],
                      [rep[0:r, p, :] for p in range(2)])
                full = [r, TOPK, TOPK]
                dve.tensor_tensor(cand[0:r], top[0:r, 0, :].unsqueeze(2).to_broadcast(full),
                                  top[0:r, 1, :].unsqueeze(1).to_broadcast(full), ALU.add)\
                    .then_inc(halves_done.sem, 1)

            def best_of_sums(s):
                _, l, t, e = s
                r = ROWS[t]
                dve.wait_ge(*halves_done.after(s[1:]))
                if ROUTE_NUMBER[s[1:]]:
                    dve.wait_ge(*exps_done.after(ROUTES[ROUTE_NUMBER[s[1:]] - 1]))
                flat = [x[0:r].rearrange("p a b -> p (a b)") for x in (cand, cand2)]
                top16([best[0:r, :]], [pos[0:r, :]], [flat[0]], [flat[1]])
                dve.tensor_scalar(negm[0:r, :], best[0:r, 0:1], -1.0, None, ALU.mult)\
                    .then_inc(best_found.sem, 1)
                mark(dve.tensor_scalar(pos2[0:r, 0, :], pos[0:r, :], 4, None, ALU.logical_shift_right))
                mark(dve.tensor_scalar(pos2[0:r, 1, :], pos[0:r, :], TOPK - 1, None, ALU.bitwise_and))

            def choose(s):
                _, l, t, e = s
                r, n = ROWS[t], ROUTE_NUMBER[s[1:]]
                full = [r, TOPK, TOPK]
                settle()
                hot3 = [hot[0:r, p, :].rearrange("p (a b) -> p a b", a=TOPK) for p in range(2)]
                for p in range(2):
                    mark(dve.tensor_tensor(hot3[p], iota16[0:r, :].unsqueeze(1).to_broadcast(full),
                                           pos2[0:r, p, :].unsqueeze(2).to_broadcast(full), ALU.is_equal))
                settle()
                for p in range(2):
                    mark(dve.tensor_tensor(hot3[p], hot3[p],
                                           topi[0:r, n % 2, p, :].unsqueeze(1).to_broadcast(full), ALU.mult))
                settle()
                for p in range(2):
                    mark(dve.tensor_reduce(part[0:r, p, :], hot3[p], AX_X, ALU.add))
                settle()
                at = slice(e * TOPK, e * TOPK + TOPK)
                mark(dve.tensor_scalar(part[0:r, 0, :], part[0:r, 0, :], float(NKEYS), float(l * EXPERTS),
                                       ALU.mult, ALU.add))
                dve.wait_ge(*exps_done.after(s[1:]))
                mark(dve.reciprocal(esum[0:r, 1:2], esum[0:r, 0:1]))
                settle()
                mark(dve.tensor_tensor(idx[0:r, t, at], part[0:r, 0, :], part[0:r, 1, :], ALU.add))
                dve.tensor_scalar(gate[0:r, t, at], ex[0:r, :], esum[0:r, 1:2], None, ALU.mult)\
                    .then_inc(routed.sem, 1)

            def dot(j, k):
                if j == ITEM_COUNT:
                    return
                l, t, _ = ITEMS[j]
                if k == 0 and t == SAMPLE:
                    dve.wait_ge(packed, PACKED * (l + 1))
                if k == 0 and j >= 2:
                    dve.wait_ge(*gelu_done.after(j - 2))
                n = j * TOPK + k
                dve.wait_ge(u_in[n % NU], 16 * (n // NU + 1))
                row = urows[:, n % NU, :]
                dve.tensor_tensor_reduce(row, row, xn2[:, t, :], 1.0, 0.0, ALU.mult, ALU.add,
                                         hid[:, j % 2, k:k + 1]).then_inc(dotted.sem, 1)

            def make_amounts(j):
                if j < 0:
                    return
                _, t, e = ITEMS[j]
                at = slice(e * TOPK, e * TOPK + TOPK)
                dve.wait_ge(*gelu_done.after(j))
                dve.tensor_tensor(amount[:, j % 2, :], act_hid[:, j % 2, :],
                                  gate_sam[:, at] if t == SAMPLE else gate[:, t, at], ALU.mult)\
                    .then_inc(amounts_done.sem, 1)
                dve.wait_ge(*amounts_done.after(j))

            def make_diag(j, q):
                if j < 0:
                    return
                t = ITEMS[j][1]
                m = 4 * j + q
                if m >= ND:
                    dve.wait_ge(*added["pe"].after(steps[QUARTER * (m - ND + 1) - 1]))
                full = [P, QUARTER, ROWS[t]]
                where = spread if t == SAMPLE else ident
                dve.tensor_tensor(diag[:, m % ND, :, 0:ROWS[t]], where[:, :].unsqueeze(1).to_broadcast(full),
                                  amount[:, j % 2, QUARTER * q:QUARTER * q + QUARTER].unsqueeze(2).to_broadcast(full),
                                  ALU.mult).then_inc(diag_made.sem, 1)

            def add_row(j, k):
                t = ITEMS[j][1]
                n = j * TOPK + k
                dve.wait_ge(v_in[n % NV], 16 * (n // NV + 1))
                if (j, k) != steps[BY_DVE]:
                    dve.wait_ge(added["dve"].sem, added["dve"].count[j, k] - 1)
                dve.scalar_tensor_tensor(out=h[:, t, :], in0=vrows[:, n % NV, :], scalar=amount[:, j % 2, k:k + 1],
                                         in1=h[:, t, :], op0=ALU.mult, op1=ALU.add).then_inc(added["dve"].sem, 1)

            def add_experts(j):
                t = ITEMS[j][1]
                dve.wait_ge(*added["pe"].after((j, TOPK - 1)))
                if t != SAMPLE:
                    dve.wait_ge(*added["dve"].after((j, TOPK - QUARTER + BY_DVE)))
                for c in range(2):
                    x = h[0:ROWS[t], t, 512 * c:512 * c + 512]
                    last = dve.tensor_tensor(x, x, experts[c][0:ROWS[t], :], ALU.add)
                    if c == 0:
                        mark(last)
                last.then_inc(experts_added.sem, 1)

            dve.wait_ge(const_made, 1)
            for s in SCHEDULE:
                kind = s[0]
                if kind == "scale":
                    _, l, t, what = s
                    r, n = ROWS[t], NORM_NUMBER[s[1:]]
                    dve.wait_ge(*squares_summed.after(s[1:]))
                    scale = rs[0:r, n % 2:n % 2 + 1]
                    root(scale, ss[0:r, n % 2:n % 2 + 1], 1.0 / D)
                    if what in ("ffn", "final"):
                        if what == "ffn":
                            dve.wait_ge(params_in, PARAMS * (l + 1))
                        else:
                            dve.wait_ge(final_in, 16)
                        out = xn2[0:r, t, :] if what == "ffn" else xs[0:r, n % 2, :]
                        dve.scalar_tensor_tensor(out=out, in0=h[0:r, t, :], scalar=scale, in1=g_row[0:r, :],
                                                 op0=ALU.mult, op1=ALU.mult).then_inc(normed.sem, 1)
                    else:
                        dve.tensor_scalar(xs[0:r, n % 2, :], h[0:r, t, :], scale, None, ALU.mult)\
                            .then_inc(normed.sem, 1)
                elif kind == "ktE":
                    _, l, t = s
                    use = ("kt", l, t)
                    dve.wait_ge(*products_done.after(use))
                    dve.tensor_copy(kT[:, :, P * t:P * t + ROWS[t]],
                                    banks[BANK[use]][:, :].rearrange("p (a n) -> p a n", a=4)[:, :, 0:ROWS[t]])\
                        .then_inc(dve_read.sem, 1)
                elif kind == "vaN":
                    _, l, t = s
                    r = ROWS[t]
                    dve.wait_ge(*act_read.after(("va", l, t)))
                    dve.wait_ge(params_in, PARAMS * (l + 1))
                    x = mlp[0:r, place(t)[0], 0:W]
                    link(head_norm(x, r))
                    dve.tensor_tensor(x, x, g_av[0:r, :], ALU.mult).then_inc(va_normed.sem, 1)
                elif kind == "attS":
                    z, cols = ("attZ",) + s[1:], P * (s[2] + 1)
                    x = sp[:, HEAD_NUMBER[s[1:]] % 2, 0:cols]
                    dve.wait_ge(*log_done.after(s[1:]))
                    dve.scalar_tensor_tensor(out=x, in0=banks[BANK[z]][:, 0:cols], scalar=0.0, in1=x,
                                             op0=ALU.max, op1=ALU.add).then_inc(softplus_done.sem, 1)
                elif kind == "samS":
                    l = s[1]
                    dve.wait_ge(*log_done.after((l,)))
                    for e in (H - 2, H - 1):
                        dve.wait_ge(*heads_done.after((l, SAMPLE - 1, e)))
                    for b, r, cols in SAMPLE_PARTS:
                        x = sp[0:r, b, 0:cols]
                        last = dve.scalar_tensor_tensor(out=x, in0=banks[BANK["samZ", l, b]][0:r, 0:cols], scalar=0.0,
                                                        in1=x, op0=ALU.max, op1=ALU.add)
                        if b == 0:
                            mark(last)
                    last.then_inc(softplus_done.sem, 1)
                    for b, r, cols in SAMPLE_PARTS:
                        dve.tensor_copy(att[0:r, b, 0:cols], banks[BANK["samZ", l, b]][0:r, 0:cols])\
                            .then_inc(dve_read.sem, 1)
                elif kind == "samX":
                    l = s[1]
                    dve.wait_ge(*dve_read.after(("samZ", l, 1)))
                    for b, r, cols in SAMPLE_PARTS:
                        use = ("samE", l, b)
                        dve.wait_ge(*products_done.after(use))
                        x = att[0:r, b, 0:cols]
                        dve.tensor_tensor(x, x, banks[BANK[use]][0:r, 0:cols], ALU.add)\
                            .then_inc(dve_read.sem, 1)
                elif kind == "attN":
                    _, l, t = s
                    dve.wait_ge(*att_moved.after(s[1:]))
                    head_norm(osb[0:ROWS[t], :], ROWS[t]).then_inc(att_normed.sem, 1)
                elif kind == "mixN":
                    _, l, t = s
                    r = ROWS[t]
                    use = ("mix", l, t)
                    dve.wait_ge(*products_done.after(use))
                    out = sq[0:r, :].rearrange("p (a n) -> p a n", a=H)
                    dve.tensor_tensor(out, banks[BANK[use]][0:r, :].rearrange("p (a n) -> p a n", a=H),
                                      b_sp[0:r, :].unsqueeze(2).to_broadcast([r, H, DH]), ALU.add)\
                        .then_inc(dve_read.sem, 1)
                    dve.wait_ge(*dve_read.after(use))
                    dve.wait_ge(*act_read.after(("ua", l, t)))
                    u = mlp[0:r, place(t)[0], W:2 * W]
                    link(dve.tensor_tensor(u, u, sq[0:r, :], ALU.mult))
                    head_norm(u, r).then_inc(mix_done.sem, 1)
                elif kind == "woutA":
                    _, l, t, c = s
                    use = ("wout", l, t, c)
                    if l == 0 and c == 0:
                        dve.wait_ge(h_in[t], 16)
                    dve.wait_ge(*products_done.after(use))
                    x = h[0:ROWS[t], t, 512 * c:512 * c + 512]
                    dve.tensor_tensor(x, x, banks[BANK[use]][0:ROWS[t], :], ALU.add).then_inc(dve_read.sem, 1)
                elif kind == "halves":
                    best_of_halves(s)
                elif kind == "sums":
                    best_of_sums(s)
                elif kind == "choice":
                    choose(s)
                elif kind == "gateA":
                    _, l, t, c = s
                    r = ROWS[t]
                    dve.wait_ge(*act_read.after(("gate", l, t, c)))
                    dve.wait_ge(*act_read.after(("ple", l, t, c)))
                    x = sp[0:r, GATE_NUMBER[s[1:]] % 2, :]
                    link(dve.tensor_tensor(x, x, mlp[0:r, place(t)[0], 512 * c:512 * c + 512], ALU.mult))
                    y = h[0:r, t, 512 * c:512 * c + 512]
                    dve.tensor_tensor(y, y, x, ALU.add).then_inc(gated.sem, 1)
                elif kind == "peer":
                    _, j, k = s
                    if j < ITEM_COUNT:
                        dot(j, k)
                    if k == ADDED and j >= 2 and ITEMS[j - 2][2] == items_in_tile(ITEMS[j - 2][1]) - 1:
                        add_experts(j - 2)
                    if 0 < j <= ITEM_COUNT:
                        if k == 1:
                            make_amounts(j - 1)
                            make_diag(j - 1, 0)
                        elif k % QUARTER == 3 and k < TOPK - 1:
                            make_diag(j - 1, k // QUARTER + 1)
                        if k % QUARTER == 3 and adder(j - 1, k - 1) == "dve":
                            add_row(j - 1, k - 1)

        @block.tensor
        def _(pe):
            def take(use):
                if use in TAKEN_BEFORE:
                    before = TAKEN_BEFORE[use]
                    pe.wait_ge(*bank_read[RELEASED_BY[before]].after(before))
                return banks[BANK[use]]

            chain = [0]

            def rows_change(ins):
                chain[0] += 1
                ins.then_inc(pe_chain, 1)
                pe.wait_ge(pe_chain, chain[0])

            def unit(s):
                n = UNIT_NUMBER[weight_unit(s)]
                pe.wait_ge(w_in[n % NW], 16 * (n // NW + 1))
                return weights[:, n % NW, :].rearrange("p (k n) -> p k n", k=KD)

            def turn(use, blocks):
                b = take(use)
                for k, x in enumerate(blocks):
                    r = x.shape[0]
                    last = pe.transpose(b[:, P * k:P * k + r], x, ident[0:r, 0:r])
                last.then_inc(products_done.sem, 1)

            def turned_ready(kind, l, tiles):
                for t in tiles:
                    pe.wait_ge(*act_read.after(("turn", l, t, kind, 1)))

            def by_token(s, x_cols, r):
                w = unit(s)
                b = take(s)
                for k in range(KD):
                    last = pe.matmul(b[0:r, :], xT[:, k, x_cols:x_cols + r], w[:, k, :],
                                     start=(k == 0), stop=(k == KD - 1))
                return b, last

            def by_column(s, block, cols):
                w = unit(s)
                b = take(s)
                for k in range(KD):
                    last = pe.matmul(b[:, 0:cols], w[:, k, P * block:P * block + P], xT[:, k, 0:cols],
                                     start=(k == 0), stop=(k == KD - 1))
                last.then_inc(products_done.sem, 1)

            def add_rows(j, k):
                l, t, e = ITEMS[j]
                n, q = j * TOPK + k, k // QUARTER
                if k == 0 and e == 0 and (l, t) != tiles_in_order[0]:
                    pe.wait_ge(*experts_added.after(tiles_in_order[tiles_in_order.index((l, t)) - 1]))
                pe.wait_ge(*diag_made.after((j, q)))
                pe.wait_ge(v_in[n % NV], 16 * (n // NV + 1))
                first = e == 0 and k == 0
                final = e == items_in_tile(t) - 1 and k == TOPK - 1
                for c in range(2):
                    last = pe.matmul(experts[c][0:ROWS[t], :], diag[:, (4 * j + q) % ND, k % QUARTER, 0:ROWS[t]],
                                     vrows[:, n % NV, 512 * c:512 * c + 512], start=first, stop=final)
                last.then_inc(added["pe"].sem, 1)

            pe.wait_ge(const_made, 1)
            for s in SCHEDULE:
                kind = s[0]
                if kind == "turn":
                    _, l, t, what = s
                    r = ROWS[t]
                    pe.wait_ge(*normed.after(s[1:]))
                    src = xn2[0:r, t, :] if what == "ffn" else xs[0:r, NORM_NUMBER[s[1:]] % 2, :]
                    for half in range(2):
                        turn(s + (half,), [src[:, P * k:P * k + P] for k in range(4 * half, 4 * half + 4)])
                elif kind == "q":
                    _, l, g, b = s
                    if b == 0:
                        turned_ready("mix", l, GROUPS[g])
                    by_column(s, b, GCOLS[g])
                elif kind in ("k", "v", "ua", "va"):
                    _, l, t = s
                    by_token(s, place(t)[1], ROWS[t])[1].then_inc(products_done.sem, 1)
                elif kind == "kt":
                    _, l, t = s
                    pe.wait_ge(*act_read.after(("k", l, t)))
                    n = K_NUMBER["k", l, t]
                    turn(s, [ktok[0:ROWS[t], n % 2, P * k:P * k + P] for k in range(4)])
                elif kind == "attZ":
                    _, l, t, e = s
                    c0, lo = place(t)[1], DH * (e % 2)
                    if e == 0:
                        pe.wait_ge(*act_read.after(("q", l, group_of(t), 3)))
                        pe.wait_ge(*dve_read.after(("kt", l, t)))
                    b = take(s)
                    for kb in range(t + 1):
                        pe.matmul(b[:, P * kb:P * kb + P], kT[lo:lo + DH, e // 2, P * kb:P * kb + P],
                                  qT[lo:lo + DH, e // 2, c0:c0 + P], start=(kb == 0), stop=False,
                                  skip_group_check=True)
                    pe.matmul(b[:, P * t:P * t + P], ident[:, :], mask[:, :], start=False, stop=True,
                              skip_group_check=True).then_inc(products_done.sem, 1)
                elif kind == "attE":
                    _, l, t, e = s
                    z = ("attZ", l, t, e)
                    b = banks[BANK[z]]
                    x = sp[:, HEAD_NUMBER[s[1:]] % 2, :]
                    pe.wait_ge(*softplus_done.after(s[1:]))
                    last = pe.matmul(b[:, 0:P * (t + 1)], neg_tri[:, :], x[:, 0:P * (t + 1)], start=False,
                                     stop=(t == 0), skip_group_check=True)
                    for kb in range(1, t + 1):
                        rhs = x[:, P * kb:P * kb + P].unsqueeze(1).to_broadcast([P, kb, P])
                        last = pe.matmul(b[:, 0:P * kb].rearrange("p (a n) -> p a n", a=kb), neg_ones[:, :], rhs,
                                         start=False, stop=(kb == t), skip_group_check=True)
                    last.then_inc(decay_done.sem, 1)
                elif kind == "attP":
                    _, l, t, e = s
                    z = ("attZ", l, t, e)
                    pe.wait_ge(*act_read.after(z))
                    if e == 0:
                        pe.wait_ge(*act_read.after(("v", l, t)))
                        n = MOVES.index((l, t))
                        if n:
                            pe.wait_ge(*att_moved.after(MOVES[n - 1]))
                    for kb in range(t + 1):
                        last = pe.matmul(att_out[:, DH * e:DH * e + DH],
                                         att[:, HEAD_NUMBER[s[1:]] % 2, P * kb:P * kb + P],
                                         v[:, kb, DH * e:DH * e + DH], start=(kb == 0), stop=(kb == t))
                    last.then_inc(heads_done.sem, 1)
                elif kind == "samZ":
                    l = s[1]
                    c0 = place(SAMPLE)[1]
                    pe.wait_ge(params_in, PARAMS * (l + 1))
                    pe.wait_ge(*dve_read.after(("kt", l, SAMPLE)))
                    b = take(("samZ", l, 0))
                    for half in range(2):
                        lo = DH * half
                        if half:
                            rows_change(last)
                        for kb in range(2):
                            for e in range(half, H, 2):
                                at = (kb * H + e) * DEC
                                last = pe.matmul(b[:, at:at + DEC], kcT[lo:lo + DH, e // 2, P * kb:P * kb + P],
                                                 qT[lo:lo + DH, e // 2, c0:c0 + DEC], start=True, stop=True)
                    last.then_inc(products_done.sem, 1)
                    b = take(("samZ", l, 1))
                    for half in range(2):
                        lo = DH * half
                        if half:
                            rows_change(last)
                        for e in range(half, H, 2):
                            last = pe.matmul(b[0:DEC, DEC * e:DEC * e + DEC], kT[lo:lo + DH, e // 2, SEQ:SEQ + DEC],
                                             qT[lo:lo + DH, e // 2, c0:c0 + DEC], start=(e == 0), stop=False,
                                             skip_group_check=True)
                    pe.matmul(b[0:DEC, 0:H * DEC].rearrange("p (a n) -> p a n", a=H), ident[0:DEC, 0:DEC],
                              mask[0:DEC, 0:DEC].unsqueeze(1).to_broadcast([DEC, H, DEC]), start=False, stop=True,
                              skip_group_check=True).then_inc(products_done.sem, 1)
                elif kind == "samE":
                    l = s[1]
                    pe.wait_ge(*softplus_done.after(s[1:]))
                    new = sp[0:DEC, 1, 0:H * DEC]
                    past = [sp[:, 0, 0:256], sp[:, 0, 256:512]]
                    b = take(("samE", l, 0))
                    for kb in range(2):
                        out = b[:, 256 * kb:256 * kb + 256]
                        pe.matmul(out, neg_tri[:, :], past[kb], start=True, stop=False)
                        if kb == 0:
                            pe.matmul(out, neg_ones[:, :], past[1], start=False, stop=False)
                        last = pe.matmul(out, neg_ones[0:DEC, :], new, start=False, stop=True)
                    last.then_inc(products_done.sem, 1)
                    b = take(("samE", l, 1))
                    pe.matmul(b[0:DEC, 0:H * DEC], neg_tri[0:DEC, 0:DEC], new, start=True, stop=True)\
                        .then_inc(products_done.sem, 1)
                elif kind == "samP":
                    l = s[1]
                    pe.wait_ge(*sample_weights_done.after((l,)))
                    pe.wait_ge(*act_read.after(("v", l, SAMPLE)))
                    pe.wait_ge(*att_moved.after((l, SAMPLE - 1)))
                    for e in range(H):
                        out = att_out[0:DEC, DH * e:DH * e + DH]
                        for kb in range(2):
                            at = (kb * H + e) * DEC
                            pe.matmul(out, att[:, 0, at:at + DEC], vc[:, kb, DH * e:DH * e + DH],
                                      start=(kb == 0), stop=False)
                        last = pe.matmul(out, att[0:DEC, 1, DEC * e:DEC * e + DEC],
                                         v[0:DEC, SAMPLE, DH * e:DH * e + DH], start=False, stop=True)
                    last.then_inc(heads_done.sem, 1)
                elif kind == "attT":
                    _, l, t = s
                    pe.wait_ge(*att_normed.after(s[1:]))
                    turn(s, [osb[0:ROWS[t], P * k:P * k + P] for k in range(4)])
                elif kind == "mix":
                    _, l, t = s
                    r, at = ROWS[t], place(t)[0]
                    pe.wait_ge(*va_normed.after(s[1:]))
                    pe.wait_ge(tril_made, l + 1)
                    b = take(s)
                    for e in range(H):
                        last = pe.matmul(b[0:r, DH * e:DH * e + DH], wsT[0:r, e, 0:r],
                                         mlp[0:r, at, DH * e:DH * e + DH], start=True, stop=True)
                    last.then_inc(products_done.sem, 1)
                elif kind == "mixT":
                    _, l, t = s
                    pe.wait_ge(*mix_done.after(s[1:]))
                    turn(s, [mlp[0:ROWS[t], place(t)[0], W + P * k:W + P * k + P] for k in range(4)])
                elif kind == "wout":
                    _, l, t, c = s
                    pe.wait_ge(*act_read.after(("attT", l, t)))
                    pe.wait_ge(*act_read.after(("mixT", l, t)))
                    by_token(s, place(t)[1], ROWS[t])[1].then_inc(products_done.sem, 1)
                elif kind == "pq":
                    _, l, g, e = s
                    if e == 0:
                        turned_ready("ffn", l, GROUPS[g])
                    by_column(s, e % 4, GCOLS[g])
                elif kind == "score":
                    _, l, t, e = s
                    r, c0 = ROWS[t], place(t)[1]
                    if e == 0:
                        pe.wait_ge(*act_read.after(("pq", l, group_of(t), H - 1)))
                    n = UNIT_NUMBER[weight_unit(s)]
                    pe.wait_ge(w_in[n % NW], 16 * (n // NW + 1))
                    subT = weights[:, n % NW, 0:H * NKEYS].rearrange("p (a n) -> p a n", a=H)
                    b = take(s)
                    for p in range(2):
                        lo = DH * p
                        if p:
                            rows_change(last)
                        last = pe.matmul(b[0:r, NKEYS * p:NKEYS * p + NKEYS], qpT[lo:lo + DH, e, c0:c0 + r],
                                         subT[lo:lo + DH, e, :], start=True, stop=True)
                    last.then_inc(products_done.sem, 1)
                elif kind == "ple":
                    _, l, t, c = s
                    r, c0 = ROWS[t], place(t)[1]
                    n = UNIT_NUMBER[weight_unit(s)]
                    pe.wait_ge(w_in[n % NW], 16 * (n // NW + 1))
                    pe.wait_ge(ple_in, 32 * (2 * l + group_of(t) + 1))
                    w = weights[:, n % NW, 0:2 * D].rearrange("p (k n) -> p k n", k=2)
                    b = take(s)
                    for k in range(2):
                        last = pe.matmul(b[0:r, :], pT[:, k, c0:c0 + r], w[:, k, 512 * c:512 * c + 512],
                                         start=(k == 0), stop=(k == 1))
                    last.then_inc(products_done.sem, 1)
                elif kind == "gate":
                    _, l, t, c = s
                    r, c0 = ROWS[t], place(t)[1]
                    if c == 0:
                        turned_ready("ple", l, [t])
                    w = unit(s)
                    b = take(s)
                    for k in range(KD):
                        pe.matmul(b[0:r, :], xT[:, k, c0:c0 + r], w[:, k, :], start=(k == 0), stop=False)
                    pe.matmul(b[0:r, :], ones_row[0:1, 0:r], b_gate[0:1, 512 * c:512 * c + 512],
                              start=False, stop=True).then_inc(products_done.sem, 1)
                elif kind == "peer":
                    _, j, k = s
                    for k in {0: [], 1: [0, 1]}.get(k, [k]):
                        if 0 < j <= ITEM_COUNT and adder(j - 1, k) == "pe":
                            add_rows(j - 1, k)


def kernel(x_prompt, x_sample, cache_k, cache_v, p_prompt, p_sample, g_mix, w_in, g_sb_out, w_spatial,
           b_spatial, g_a_v, g_a_out, w_out, g_ffn, w_peer_q, peer_sub_keys, peer_u, peer_v, g_ple,
           w_ple_gate, b_ple_gate, w_ple, g_final):
    import concourse.bacc as bacc
    from concourse.bass_utils import run_bass_kernel_spmd

    def blocks(w, n):
        w = np.asarray(w)
        layers, k, cols = w.shape
        return w.reshape(layers, k // P, P, cols // n, n).transpose(0, 3, 2, 1, 4).reshape(layers, cols // n, P, -1)

    def by_block(g):
        return np.asarray(g).reshape(L, KD, P).transpose(2, 0, 1)

    p_all = np.concatenate([np.asarray(p_prompt)[:, 0], np.asarray(p_sample)[:, 0]], axis=1)
    g_out = np.concatenate([np.asarray(g_sb_out).reshape(L, W), np.asarray(g_a_out).reshape(L, W)], axis=1)
    arrays = {
        "x": np.concatenate([np.asarray(x_prompt)[0], np.asarray(x_sample)[0]], axis=0),
        "cache_kT": np.asarray(cache_k)[:, 0].reshape(L, PAST, 4, P).transpose(0, 3, 2, 1).reshape(L, P, -1),
        "cache_v": np.asarray(cache_v)[:, 0].reshape(L, PAST, W),
        "pT": p_all.transpose(0, 2, 1).reshape(L, 2, P, SEQ + DEC).transpose(0, 2, 1, 3),
        "gains": np.stack([by_block(g_mix), by_block(g_out), by_block(g_ple)], axis=2).reshape(P, -1),
        "w_in": blocks(w_in, 512),
        "w_out": blocks(w_out, 512),
        "w_peer_q": blocks(w_peer_q, 512),
        "w_ple_gate": blocks(w_ple_gate, 512),
        "w_ple": blocks(w_ple, D),
        "w_spatialT": np.asarray(w_spatial).transpose(0, 3, 1, 2).reshape(L, P, -1),
        "b_spatialT": np.asarray(b_spatial).transpose(0, 2, 1),
        "g_a_v": np.asarray(g_a_v).reshape(L, W),
        "g_ffn": np.asarray(g_ffn),
        "sub_keysT": np.asarray(peer_sub_keys).transpose(0, 2, 4, 1, 3).reshape(L, 1, P, -1),
        "peer_u": np.asarray(peer_u).reshape(L * EXPERTS, D),
        "peer_v": np.asarray(peer_v).reshape(L * EXPERTS, D),
        "b_ple_gate": np.asarray(b_ple_gate),
        "g_final": np.asarray(g_final).reshape(1, D),
    }
    arrays = {n: np.ascontiguousarray(a) for n, a in arrays.items()}
    nc = bacc.Bacc("TRN2", target_bir_lowering=False, num_devices=1)
    ins = {n: nc.dram_tensor(f"in_{n}", a.shape, F32, kind="ExternalInput").ap() for n, a in arrays.items()}
    shapes = {"y": (SEQ + DEC, D), "k": (L, SEQ + DEC, W), "v": (L, SEQ + DEC, W), "va": (L, DEC, W)}
    outs = {n: nc.dram_tensor(f"out_{n}", s, F32, kind="ExternalOutput").ap() for n, s in shapes.items()}
    encoder(nc, ins, outs)
    r = run_bass_kernel_spmd(nc, [{f"in_{n}": a for n, a in arrays.items()}], core_ids=[0]).results[0]
    y, k, v, va = (np.asarray(r[f"out_{n}"]) for n in shapes)
    heads = lambda a: a.reshape(L, 1, -1, H, DH)
    return (y[None, :SEQ], y[None, SEQ:], heads(k[:, :SEQ]), heads(v[:, :SEQ]), heads(k[:, SEQ:]),
            heads(v[:, SEQ:]), heads(va))
```

```python
from contextlib import ExitStack

import concourse.bass as bass
import numpy as np
from concourse import mybir

F32 = mybir.dt.float32
U32 = mybir.dt.uint32
ALU = mybir.AluOpType
ACT = mybir.ActivationFunctionType
AX_X = mybir.AxisListType.X

P = 128
D = 1024
KD = D // P
L = 2
SEQ, DEC, PAST = 512, 32, 256
NT = SEQ // P + 1
SAMPLE = NT - 1
ROWS = [P] * SAMPLE + [DEC]
GROUPS = [[0, 1], [2, 3, 4]]
GCOLS = [sum(ROWS[t] for t in g) for g in GROUPS]
H, DH = 8, 64
W = H * DH
NKEYS, EXPERTS, TOPK = 128, 128 * 128, 16
PLE = 256
EPS = 1e-6
MASKED = -1e30
BELOW = -3.0e38
NU, NV = 4, 5
NW = 2
ND = 2
NB = 5
QUARTER = 4
ADDED = 1

IN_PARTS = ["q", "k", "v", "ua", "va"]


LAGS = {"norm": [1, 1], "k": [1, 2], "va": [1, 3], "wout": [2], "gate": [2]}

STEPS = {"halves": 4, "sums": 3, "choice": 4}


def group_of(t):
    return 0 if t in GROUPS[0] else 1


def place(t):
    g = GROUPS[group_of(t)]
    i = g.index(t)
    return i, P * i


def in_turns(*columns, behind=None):
    n = len(columns[0])
    starts = [sum((behind or [1] * len(columns))[:d]) for d in range(len(columns))]
    out = []
    for i in range(n + starts[-1]):
        for start, column in reversed(list(zip(starts, columns))):
            if 0 <= i - start < n:
                out.append(column[i - start])
    return out


def norm_stages(l, tiles, what):
    names = [(l, t, what) for t in tiles]
    return in_turns([("squares",) + x for x in names], [("scale",) + x for x in names],
                    [("turn",) + x for x in names], behind=LAGS["norm"])


def projection_stages(l, g):
    tiles = GROUPS[g]
    out = [("params", l)] if g == 0 else []
    out += norm_stages(l, tiles, "mix")
    out += [("q", l, g, b) for b in range(4)]
    out += in_turns(*([(k, l, t) for t in tiles] for k in ("k", "kt", "ktE")), behind=LAGS["k"])
    out += [("v", l, t) for t in tiles]
    return out + ([("tril", l)] if g == 0 else [])


def mlp_stages(l, tiles):
    out = [("ua", l, t) for t in tiles]
    return out + in_turns(*([(k, l, t) for t in tiles] for k in ("va", "vaQ", "vaN")), behind=LAGS["va"])


def mix_stages(l, tiles):
    return in_turns(*([(k, l, t) for t in tiles] for k in ("mix", "mixQ", "mixN", "mixT")))


def attention_stages(l, tiles, others, rounds, tail_others=()):
    out = []
    units = [(l, t, e) for t in tiles if t != SAMPLE for e in range(H)]
    n = len(units)
    for i in range(n + 3):
        out += others[len(others) * i // rounds:len(others) * (i + 1) // rounds]
        if i >= 3:
            out.append(("attP",) + units[i - 3])
            if units[i - 3][2] == H - 1:
                out.append(("attM", l, units[i - 3][1]))
        if i >= 2 and i - 2 < n:
            out.append(("attE",) + units[i - 2])
        if i < n:
            out.append(("attZ",) + units[i])
        if 1 <= i <= n:
            out.append(("attS",) + units[i - 1])
        for late, k in ((4, "attQ"), (5, "attN"), (6, "attT")):
            if i >= late and i - late < n and units[i - late][2] == H - 1:
                out.append((k, l, units[i - late][1]))
    last = units[-1][1]
    if SAMPLE not in tiles:
        return out + list(tail_others) + [("attQ", l, last), ("attN", l, last), ("attT", l, last)]
    tail = [("attQ", l, last), ("samZ", l), ("attN", l, last), ("samS", l), ("attT", l, last), ("samE", l),
            ("samX", l), ("samP", l), ("attM", l, SAMPLE), ("attQ", l, SAMPLE), ("attN", l, SAMPLE),
            ("attT", l, SAMPLE)]
    n = len(tail_others)
    for i in range(len(tail)):
        out += tail_others[n * i // len(tail):n * (i + 1) // len(tail)] + [tail[i]]
    return out


def output_stages(l, tiles):
    outs = [(l, t, c) for c in range(2) for t in tiles]
    out = in_turns([("wout",) + x for x in outs], [("woutA",) + x for x in outs], behind=LAGS["wout"])
    return out + norm_stages(l, tiles, "ffn")


def mixer_stages(l, g):
    tiles = GROUPS[g]
    if SAMPLE in tiles:
        att = attention_stages(l, tiles, mlp_stages(l, tiles), H + 5, mix_stages(l, tiles))
    else:
        att = attention_stages(l, tiles, mlp_stages(l, tiles) + mix_stages(l, tiles), H + 5)
    return projection_stages(l, g) + att + output_stages(l, tiles) + query_stages(l, g)


def query_stages(l, g, heads=range(H)):
    return [("pq", l, g, e) for e in heads]


PASSES = {(l_, g_): GROUPS[g_] for l_ in range(L) for g_ in range(2)}
FIRST_PASS, SECOND_PASS = 0, 2
PASSES[0, FIRST_PASS] = GROUPS[0][:1]
PASSES[0, SECOND_PASS] = GROUPS[0][1:]


def pass_of(l, t):
    return next(p for (l1, p), tiles in PASSES.items() if l1 == l and t in tiles)


def routing_stages(l, tiles, alone=0):
    names = [(l, t, e) for t in tiles for e in range(H)]
    out = [("score",) + x for x in names[:alone]]
    for x in names[:alone]:
        out += [(kind,) + x + (k,) for kind in STEPS for k in range(STEPS[kind])]
    names = names[alone:]
    n = len(names)
    for i in range(n + 3):
        if i < n:
            out.append(("score",) + names[i])
        for k in range(STEPS["choice"]):
            for kind, j in (("choice", i - 3), ("halves", i - 1), ("sums", i - 2)):
                if 0 <= j < n and k < STEPS[kind]:
                    out.append((kind,) + names[j] + (k,))
    if SAMPLE in tiles:
        at = out.index(("choice", l, SAMPLE, H - 1, STEPS["choice"] - 1))
        out.insert(at + 1, ("pack", l))
    return out


def embedding_stages(l, g):
    tiles = GROUPS[g]
    out = embedding_products(l, g)
    out += norm_stages(l, tiles, "ple")
    gates = [(l, t, c) for c in range(2) for t in tiles]
    out += in_turns([("gate",) + x for x in gates], [("gateA",) + x for x in gates], behind=LAGS["gate"])
    if l == L - 1:
        out += in_turns([("squares", L, t, "final") for t in tiles], [("scale", L, t, "final") for t in tiles])
    return out


def embedding_products(l, g):
    return [("pleparams", l, g)] + [("ple", l, t, c) for t in GROUPS[g] for c in range(2)]


def embedding_tile(l, t):
    return (norm_stages(l, [t], "ple") + [("gate", l, t, 0), ("gate", l, t, 1), ("gateA", l, t, 0),
            ("gateA", l, t, 1), ("squares", L, t, "final"), ("scale", L, t, "final")])


ITEMS = []
FIRST_ITEM = {}
for l_ in range(L):
    for g_ in range(2):
        FIRST_ITEM[l_, g_] = len(ITEMS)
        for t_ in GROUPS[g_]:
            ITEMS += [(l_, t_, h_) for h_ in range(2 if t_ == SAMPLE else H)]
ITEM_COUNT = len(ITEMS)


def items_in_tile(t):
    return 2 if t == SAMPLE else H


def load(s):
    if s[0] == "part" or s[0] in IN_TWO:
        e = LOAD[s[1] if s[0] == "part" else s[0]]
        return e[0] / 2, e[1] / 2
    if s[0] in ("attZ", "attS", "attE", "attP"):
        return tuple(x * (s[2] + 1) / 2.5 for x in LOAD[s[0]])
    return LOAD.get(s[0], (0, 0))


def cost(s):
    return PE_WEIGHT * load(s)[0] + DVE_WEIGHT * load(s)[1] + STAGE_WEIGHT


def in_parts(work):
    out = []
    for s in work:
        out += [("part",) + s, s] if s[0] in IN_TWO else [s]
    return out


def beside(gathers, work):
    work = in_parts(work)
    total = sum(cost(s) for s in work)
    out, done, n = [], 0.0, 0
    for i, s in enumerate(gathers):
        out.append(s)
        while n < len(work) and done + cost(work[n]) / 2 <= total * (i + 1) / len(gathers):
            done += cost(work[n])
            out.append(work[n])
            n += 1
    return out + work[n:]


LOAD = {"squares": (0, 0.3), "scale": (0, 2), "turn": (1, 0),
        "q": (3.9, 0), "k": (6.8, 0), "kt": (0.4, 0), "ktE": (0, 0.7), "v": (6.8, 0),
        "ua": (6.8, 0), "va": (7.1, 0), "vaQ": (0, 2), "vaN": (0, 2.3),
        "attZ": (0.8, 0), "attS": (0, 0.5), "attE": (1.1, 0), "attP": (0.3, 0),
        "attQ": (0, 2), "attN": (0, 1.8), "attT": (0.5, 0),
        "samZ": (2.1, 0), "samS": (0, 2.4), "samE": (2.6, 0), "samX": (0, 1.2), "samP": (3.2, 0),
        "mix": (1, 0), "mixQ": (0, 3.4), "mixN": (0, 1.8), "mixT": (0.5, 0),
        "wout": (7.1, 0), "woutA": (0, 0.7), "pq": (3.7, 0),
        "score": (0.5, 0), "halves": (0, 0.6), "sums": (0, 0.6), "choice": (0, 0.6),
        "ple": (2.1, 0), "gate": (7.8, 0), "gateA": (0, 1.5)}
IN_TWO = ("q", "k", "v", "ua", "va", "wout", "pq", "gate")
STAGE_WEIGHT = 1.44
PE_WEIGHT = 1.0
DVE_WEIGHT = 1.17
LATE = 0.15
START = 3


def schedule():
    def gathers(item, last_item, step=0, last_step=0):
        return [("peer", j, k) for j in range(item, last_item + 1) for k in range(TOPK)
                if (item, step) <= (j, k) < (last_item, last_step)]

    def behind(item):
        return (item + 1, ADDED + 1)

    b = [FIRST_ITEM[0, 0], FIRST_ITEM[0, 1], FIRST_ITEM[1, 0], FIRST_ITEM[1, 1], ITEM_COUNT]
    first, later = PASSES[0, FIRST_PASS], PASSES[0, SECOND_PASS]
    out = projection_stages(0, 0)
    out += attention_stages(0, first, mlp_stages(0, GROUPS[0]) + mix_stages(0, first), H + 3)
    out += output_stages(0, first) + query_stages(0, FIRST_PASS, range(H // 2))
    route = routing_stages(0, first, alone=1)
    at = route.index(("score", 0, 0, H // 2))
    route[at:at] = query_stages(0, FIRST_PASS, range(H // 2, H))
    one, two = (route.index(("choice", 0, 0, e, STEPS["choice"] - 1)) + 1 for e in range(2))
    out += route[:one]
    out += beside(gathers(0, 1), route[one:two])
    out += beside(gathers(1, START), route[two:])
    out += beside(gathers(START, b[1]), attention_stages(0, later, mix_stages(0, later), H + 3)
                  + output_stages(0, later) + query_stages(0, SECOND_PASS) + routing_stages(0, later)
                  + mixer_stages(0, 1) + routing_stages(0, [2]))
    for k in (1, 2):
        l = k // 2
        own, other = k % 2, 1 - k % 2
        start, step = behind(b[k])
        late = routing_stages(l, [SAMPLE, 3] if own else [1])
        out += beside(gathers(b[k], start, 0, step), late[:int(len(late) * LATE)])
        out += beside(gathers(start, b[k + 1], step), late[int(len(late) * LATE):]
                      + embedding_stages(0, other) + mixer_stages((k + 1) // 2, other)
                      + routing_stages((k + 1) // 2, [2 if other else 0]))
    start, step = behind(b[3])
    late = routing_stages(1, [SAMPLE, 3])
    out += beside(gathers(b[3], start, 0, step), late[:int(len(late) * LATE)])
    two, step2 = behind(b[3] + H)
    three, step3 = behind(b[3] + 2 * H)
    end, step4 = behind(ITEM_COUNT)
    out += beside(gathers(start, two, step, step2), late[int(len(late) * LATE):] + embedding_stages(1, 0)
                  + embedding_products(1, 1))
    out += beside(gathers(two, three, step2, step3), embedding_tile(1, 2))
    out += beside(gathers(three, end, step3, step4), embedding_tile(1, 3))
    out += embedding_tile(1, SAMPLE)
    return out


SCHEDULE = schedule()
assert len(set(SCHEDULE)) == len(SCHEDULE)


class Signal:

    def __init__(self, sem, events):
        self.sem = sem
        self.count = {e: n + 1 for n, e in enumerate(events)}

    def after(self, event):
        return self.sem, self.count[event]


def bank_uses(s):
    k = s[0]
    if k == "turn":
        return [s + (half,) for half in range(2)]
    if k in ("q", "k", "kt", "v", "ua", "va", "attZ", "attT", "mix", "mixT", "wout", "pq", "score", "ple",
             "gate"):
        return [s]
    if k in ("samZ", "samE"):
        return [s + (half,) for half in range(2)]
    return []


def releases(s):
    k = s[0]
    if k in ("turn", "q", "k", "v", "ua", "va", "attT", "mixT", "pq", "score", "ple", "gate"):
        return [("act", u) for u in bank_uses(s)]
    if k == "attE":
        return [("act", ("attZ",) + s[1:])]
    if k in ("ktE", "woutA"):
        return [("dve", (k[:-1],) + s[1:])]
    if k == "mixQ":
        return [("dve", ("mix",) + s[1:])]
    if k == "samS":
        return [("dve", ("samZ", s[1], half)) for half in range(2)]
    if k == "samX":
        return [("dve", ("samE", s[1], half)) for half in range(2)]
    return []


USES = [u for s in SCHEDULE for u in bank_uses(s)]
BANK = {u: n % NB for n, u in enumerate(USES)}
TAKEN_BEFORE = {u: USES[n - NB] for n, u in enumerate(USES) if n >= NB}
RELEASES = [r for s in SCHEDULE for r in releases(s)]
RELEASED_BY = {u: who for who, u in RELEASES}
RELEASED_IN = {u: n for n, s in enumerate(SCHEDULE) for who, u in releases(s)}
assert all(RELEASED_IN[TAKEN_BEFORE[u]] < n for n, s in enumerate(SCHEDULE) for u in bank_uses(s)
           if u in TAKEN_BEFORE and TAKEN_BEFORE[u][:len(s)] != s)


def weight_unit(s):
    k = s[0]
    if k in IN_PARTS:
        return ("in", s[1], s[2] if k == "q" else group_of(s[2]), IN_PARTS.index(k))
    if k == "wout":
        return (k, s[1], pass_of(s[1], s[2]), s[3])
    if k == "gate":
        return (k, s[1], group_of(s[2]), s[3])
    if k == "ple":
        return (k, s[1], group_of(s[2]), 0)
    if k == "pq":
        return (k, s[1], s[2], s[3] // 4)
    if k == "score":
        return (k, s[1], pass_of(s[1], s[2]), 0)
    return None


UNITS = []
LAST_STAGE = {}
for s_ in SCHEDULE:
    u_ = weight_unit(s_)
    if u_ is not None:
        if u_ not in LAST_STAGE:
            UNITS.append(u_)
        LAST_STAGE[u_] = s_
UNIT_NUMBER = {u: n for n, u in enumerate(UNITS)}
NORMS = [s[1:] for s in SCHEDULE if s[0] == "squares"]
NORM_NUMBER = {s: n for n, s in enumerate(NORMS)}
FINALS = [x for x in NORMS if x[2] == "final"]
ROUTES = [s[1:4] for s in SCHEDULE if s[0] == "choice" and s[4] == 0]
ROUTE_NUMBER = {s: n for n, s in enumerate(ROUTES)}
LAST_ROUTE = {l_: [x for x in ROUTES if x[0] == l_][-1] for l_ in range(L)}
HEAD_NORMS = [s for s in SCHEDULE if s[0] in ("vaQ", "attQ", "mixQ")]
HEAD_NORM_NUMBER = {s: n for n, s in enumerate(HEAD_NORMS)}
assert all(SCHEDULE.index((a[0][:-1] + "N",) + a[1:]) < SCHEDULE.index(b) for a, b in zip(HEAD_NORMS, HEAD_NORMS[4:]))
KS = [s for s in SCHEDULE if s[0] == "k"]
K_NUMBER = {s: n for n, s in enumerate(KS)}
HEADS = [s[1:] for s in SCHEDULE if s[0] == "attZ"]
HEAD_NUMBER = {s: n for n, s in enumerate(HEADS)}
MOVES = [s[1:] for s in SCHEDULE if s[0] == "attM"]
GATES = [s[1:] for s in SCHEDULE if s[0] == "gate"]
GATE_NUMBER = {s: n for n, s in enumerate(GATES)}


DVE_ROWS = [(), (2,), (1, 2), (0, 1, 2)]
PE_ROW = 1.75
DVE_ROW = 0.43
DVE_STEP = 1.0
WINDOW = 5


def shares():
    at = [n for n, s in enumerate(SCHEDULE) if s[0] == "peer"]
    between = [[sum(load(s)[e] for s in SCHEDULE[a:b]) for e in range(2)]
               for a, b in zip(at, at[1:] + [len(SCHEDULE)])]
    out = {}
    for j in range(ITEM_COUNT):
        for q in range(4):
            if ITEMS[j][1] == SAMPLE:
                out[j, q] = 0
                continue
            here = (j + 1) * TOPK + QUARTER * q + 2
            near = between[max(0, here - WINDOW):here + WINDOW]
            pe, dve = (QUARTER * sum(x[e] for x in near) / len(near) for e in range(2))
            most = len(DVE_ROWS) - (ITEMS[j][2] == 0 and q == 0)
            out[j, q] = min(range(most),
                            key=lambda n: max(pe + PE_ROW * (QUARTER - n), dve + DVE_STEP * QUARTER + DVE_ROW * n))
    return out


SHARES = shares()


def adder(j, k):
    return "dve" if k % QUARTER in DVE_ROWS[SHARES[j, k // QUARTER]] else "pe"


def encoder(nc, i, o):
    with ExitStack() as ctx:
        def sb(name, shape, dt=F32):
            return ctx.enter_context(nc.sbuf_tensor(name, shape, dt))

        def sem(name):
            return ctx.enter_context(nc.semaphore(name))

        h = sb("h", [P, NT, D])
        xn2 = sb("xn2", [P, NT, D])
        kT = sb("kT", [P, 4, SEQ + DEC])
        v = sb("v", [P, NT, W])
        ident = sb("ident", [P, P])
        spread = sb("spread", [P, DEC])
        neg_tri = sb("neg_tri", [P, P])
        neg_ones = sb("neg_ones", [P, P])
        mask = sb("mask", [P, P])
        ones_row = sb("ones_row", [1, P])
        iota16 = sb("iota16", [P, TOPK])
        gains = sb("gains", [P, L, 3, KD])
        kcT = sb("kcT", [P, 4, PAST])
        vc = sb("vc", [P, PAST // P, W])
        wsT = sb("wsT", [P, H, P])
        b_sp = sb("b_sp", [P, H])
        g_av = sb("g_av", [P, W])
        g_row = sb("g_row", [P, D])
        weights = sb("weights", [P, NW, KD * 512])
        xT = sb("xT", [P, KD, GCOLS[1]])
        xs = sb("xs", [P, 2, D])
        routing = sb("routing", [P, H * GCOLS[1]])
        qT = routing[:, 0:4 * GCOLS[1]].rearrange("p (a n) -> p a n", a=4)
        ktok = routing[:, 4 * GCOLS[1]:4 * GCOLS[1] + 2 * W].rearrange("p (a n) -> p a n", a=2)
        qpT = routing[:, :].rearrange("p (a n) -> p a n", a=H)
        qpT_alone = routing[:, 4 * GCOLS[1]:4 * GCOLS[1] + H * P].rearrange("p (a n) -> p a n", a=H)
        mlp = sb("mlp", [P, 3, D])
        osb = sb("osb", [P, W])
        sq = xs[:, 0, 0:W]
        b_gate = routing[0:1, 0:D]
        work = sb("work", [P, 4 * 512])
        sp = work[:, 0:1024].rearrange("p (a n) -> p a n", a=2)
        att = work[:, 1024:2048].rearrange("p (a n) -> p a n", a=2)
        ss = sb("ss", [P, 2])
        guess = sb("guess", [P, 2])
        ss8 = sb("ss8", [P, 4, H])
        guess8 = sb("guess8", [P, 4, H])
        newton = sb("newton", [P, H])
        eps_col = sb("eps_col", [P, 1])
        square = TOPK * TOPK
        rep = work[:, 0:square].rearrange("p (a n) -> p a n", a=2)
        cand = work[:, square:2 * square].rearrange("p (a b) -> p a b", a=TOPK)
        cand2 = work[:, 2 * square:3 * square].rearrange("p (a b) -> p a b", a=TOPK)
        hot = work[:, 3 * square:5 * square].rearrange("p (a n) -> p a n", a=2)
        st = work[:, 5 * square:5 * square + 4 * NKEYS].rearrange("p (a n) -> p a n", a=2)
        top = sb("top", [P, 2, TOPK])
        topi = sb("topi", [P, 3, 2, TOPK], U32)
        best = sb("best", [P, 2, TOPK])
        pos = sb("pos", [P, TOPK], U32)
        pos2 = sb("pos2", [P, 2, TOPK], U32)
        part = sb("part", [P, 2, TOPK])
        negm = sb("negm", [P, 2])
        ex = sb("ex", [P, 2, TOPK])
        esum = sb("esum", [P, 2, 2])
        idx = sb("idx", [P, NT, H * TOPK], U32)
        gate = sb("gate", [P, NT, H * TOPK])
        idx_sam = sb("idx_sam", [P, 2 * TOPK], U32)
        gate_sam = sb("gate_sam", [P, 2 * TOPK])
        urows = sb("urows", [P, NU, D])
        vrows = sb("vrows", [P, NV, D])
        hid = sb("hid", [P, 2, TOPK])
        act_hid = sb("act_hid", [P, 2, TOPK])
        amount = sb("amount", [P, 2, TOPK])
        diag = sb("diag", [P, ND, QUARTER, P])

        def bank(name):
            return ctx.enter_context(nc.psum_tensor(name, [P, 512], F32))

        experts = [bank("experts0"), bank("experts1")]
        banks = [bank(f"bank{n}") for n in range(NB)]
        att_out = bank("att_out")

        const_made = sem("const_made")
        h_in = [sem(f"h_in{t}") for t in range(NT)]
        gains_in = sem("gains_in")
        params_in = sem("params_in")
        tril_made = sem("tril_made")
        p_in, bias_in = sem("p_in"), sem("bias_in")
        final_in = sem("final_in")
        w_in = [sem(f"w_in{n}") for n in range(NW)]
        k_out = [sem("k_out0"), sem("k_out1")]
        v_out = sem("v_out")
        va_out = sem("va_out")
        y_out = [sem("y_out0"), sem("y_out1")]
        packed = sem("packed")
        u_in = [sem(f"u_in{n}") for n in range(NU)]
        v_in = [sem(f"v_in{n}") for n in range(NV)]
        dve_chain, act_chain, pool_chain, pe_chain = (sem(n) for n in ("dve_chain", "act_chain",
                                                                       "pool_chain", "pe_chain"))

        def of(*kinds):
            return [s[1:] for s in SCHEDULE if s[0] in kinds]

        products_done = Signal(sem("products_done"), USES)
        act_read = Signal(sem("act_read"), [u for who, u in RELEASES if who == "act"])
        dve_read = Signal(sem("dve_read"), [u for who, u in RELEASES if who == "dve"])
        bank_read = {"act": act_read, "dve": dve_read}
        squares_summed = Signal(sem("squares_summed"), NORMS)
        normed = Signal(sem("normed"), of("scale"))
        heads_summed = Signal(sem("heads_summed"), HEAD_NORMS)
        heads_guessed = Signal(sem("heads_guessed"), HEAD_NORMS)
        va_normed = Signal(sem("va_normed"), of("vaN"))
        log_done = Signal(sem("log_done"), of("attZ", "samZ"))
        softplus_done = Signal(sem("softplus_done"), of("attS", "samS"))
        decay_done = Signal(sem("decay_done"), of("attE"))
        sample_weights_done = Signal(sem("sample_weights_done"), of("samX"))
        heads_done = Signal(sem("heads_done"), of("attP", "samP"))
        att_moved = Signal(sem("att_moved"), MOVES)
        att_normed = Signal(sem("att_normed"), of("attN"))
        mix_done = Signal(sem("mix_done"), of("mixN"))
        best_found = Signal(sem("best_found"), ROUTES)
        exps_done = Signal(sem("exps_done"), ROUTES)
        halves_done = Signal(sem("halves_done"), ROUTES)
        routed = Signal(sem("routed"), ROUTES)
        gated = Signal(sem("gated"), of("gateA"))
        steps = [(j, s) for j in range(ITEM_COUNT) for s in range(TOPK)]
        dotted = Signal(sem("dotted"), steps)
        gelu_done = Signal(sem("gelu_done"), range(ITEM_COUNT))
        amounts_done = Signal(sem("amounts_done"), range(ITEM_COUNT))
        diag_made = Signal(sem("diag_made"), [(j, q) for j in range(ITEM_COUNT) for q in range(4)])
        added = {who: Signal(sem(f"added_by_{who}"), [x for x in steps if adder(*x) == who])
                 for who in ("pe", "dve")}
        tiles_in_order = [(l, t) for l, t, e in ITEMS if e == 0]
        experts_added = Signal(sem("experts_added"), tiles_in_order)

        def h_ready(eng, l, t, kind):
            if kind == "mix" and l == 0:
                eng.wait_ge(h_in[t], 16)
            elif kind == "mix" or kind == "final":
                eng.wait_ge(*gated.after((l - 1, t, 1)))
            elif kind == "ffn":
                eng.wait_ge(*dve_read.after(("wout", l, t, 1)))
            else:
                eng.wait_ge(*experts_added.after((l, t)))

        def tokens_p(n, g):
            return weights[:, n % NW, 2 * D:2 * D + 2 * GCOLS[g]].rearrange("p (k n) -> p k n", k=2)

        def peer_queries(l, p, e, tiles):
            if len(PASSES[l, p]) == 1:
                return qpT_alone[:, e, 0:ROWS[tiles[0]]]
            c0 = place(tiles[0])[1]
            return qpT[:, e, c0:c0 + sum(ROWS[t] for t in tiles)]

        PARAMS, PACKED = 16 * 6, 16 * 11

        SAMPLE_PARTS = [(0, P, 2 * H * DEC), (1, DEC, H * DEC)]

        block = ctx.enter_context(nc.Block())

        @block.sync
        def _(sp_eng):
            eng = sp_eng

            def load_unit(n):
                kind, l, g, c = UNITS[n]
                if n >= NW:
                    eng.wait_ge(*products_done.after(LAST_STAGE[UNITS[n - NW]]))
                src = {"in": i["w_in"], "wout": i["w_out"], "pq": i["w_peer_q"],
                       "gate": i["w_ple_gate"], "ple": i["w_ple"], "score": i["sub_keysT"]}[kind][l, c]
                eng.dma_start(weights[:, n % NW, 0:src.shape[1]], src).then_inc(w_in[n % NW], 16)
                if kind == "ple":
                    eng.dma_start(tokens_p(n, g), i["pT"][l][:, :, P * GROUPS[g][0]:P * GROUPS[g][0] + GCOLS[g]])\
                       .then_inc(p_in, 16)

            eng.dma_start(gains[:, :, :, :].rearrange("p a b c -> p (a b c)"), i["gains"]).then_inc(gains_in, 16)
            for t in GROUPS[0]:
                eng.dma_start(h[0:ROWS[t], t, :], i["x"][P * t:P * t + ROWS[t], :]).then_inc(h_in[t], 16)
            load_unit(0)
            load_unit(1)

            for s in SCHEDULE:
                if s[0] == "params":
                    l = s[1]
                    if l > 0:
                        eng.wait_ge(*routed.after(LAST_ROUTE[l - 1]))
                    for dst, src in ((kcT[:, :, :].rearrange("p a n -> p (a n)"), i["cache_kT"][l]),
                                     (vc[:, :, :], i["cache_v"][l].rearrange("(b p) n -> p b n", p=P)),
                                     (wsT[:, :, :].rearrange("p a n -> p (a n)"), i["w_spatialT"][l]),
                                     (b_sp[:, :], i["b_spatialT"][l]),
                                     (g_av[:, :], i["g_a_v"][l:l + 1, :].to_broadcast([P, W])),
                                     (g_row[:, :], i["g_ffn"][l:l + 1, :].to_broadcast([P, D]))):
                        eng.dma_start(dst, src).then_inc(params_in, 16)
                    if l == 0:
                        for t in GROUPS[1]:
                            eng.dma_start(h[0:ROWS[t], t, :], i["x"][P * t:P * t + ROWS[t], :])\
                               .then_inc(h_in[t], 16)
                elif s[0] == "pleparams":
                    _, l, g = s
                    if (l, g) != (0, 0):
                        before = (l, 0) if g == 1 else (l - 1, 1)
                        eng.wait_ge(*gated.after((before[0], GROUPS[before[1]][-1], 1)))
                    here = SCHEDULE.index(s)
                    eng.wait_ge(*routed.after([x[1:4] for x in SCHEDULE[:here] if x[0] == "choice"][-1]))
                    eng.dma_start(b_gate[:, :], i["b_ple_gate"][l:l + 1, :]).then_inc(bias_in, 16)
                elif s[0] == "k":
                    _, l, t = s
                    eng.wait_ge(*act_read.after(s))
                    eng.dma_start(o["k"][l, P * t:P * t + ROWS[t], :], ktok[0:ROWS[t], K_NUMBER[s] % 2, :])\
                       .then_inc(k_out[K_NUMBER[s] % 2], 16)
                elif s[0] == "v":
                    _, l, t = s
                    eng.wait_ge(*act_read.after(s))
                    eng.dma_start(o["v"][l, P * t:P * t + ROWS[t], :], v[0:ROWS[t], t, :]).then_inc(v_out, 16)
                elif s[0] == "vaN" and s[2] == SAMPLE:
                    eng.wait_ge(*va_normed.after(s[1:]))
                    eng.dma_start(o["va"][s[1]], mlp[0:DEC, place(SAMPLE)[0], 0:W]).then_inc(va_out, 16)
                elif s[0] == "pack":
                    l = s[1]
                    eng.wait_ge(*routed.after((l, SAMPLE, H - 1)))
                    for b in range(4):
                        lo, hi = 32 * b, 32 * b + 32
                        eng.dma_start(idx_sam[lo:hi, :], idx[0:DEC, SAMPLE, lo:hi]).then_inc(packed, 16)
                        eng.dma_start(gate_sam[lo:hi, :], gate[0:DEC, SAMPLE, lo:hi]).then_inc(packed, 16)
                        if b:
                            eng.dma_start(xn2[lo:hi, SAMPLE, :], xn2[0:DEC, SAMPLE, :]).then_inc(packed, 16)
                elif s[0] == "turn" and s[1:] == (L - 1, GROUPS[1][-1], "ffn"):
                    for t in GROUPS[1]:
                        eng.wait_ge(*normed.after((L - 1, t, "ffn")))
                    eng.dma_start(g_row[:, :], i["g_final"].to_broadcast([P, D])).then_inc(final_in, 16)
                elif s[0] == "scale" and s[3] == "final":
                    t, b = s[2], NORM_NUMBER[s[1:]] % 2
                    eng.wait_ge(*normed.after(s[1:]))
                    eng.dma_start(o["y"][P * t:P * t + ROWS[t], :], xs[0:ROWS[t], b, :]).then_inc(y_out[b], 16)
                u = weight_unit(s)
                if u is not None and LAST_STAGE[u] == s and UNIT_NUMBER[u] + NW < len(UNITS):
                    load_unit(UNIT_NUMBER[u] + NW)
            for n in range(2):
                eng.wait_ge(k_out[n], 16 * len([s for s in KS if K_NUMBER[s] % 2 == n]))
                eng.wait_ge(y_out[n], 16 * len([x for x in FINALS if NORM_NUMBER[x] % 2 == n]))
            eng.wait_ge(v_out, 16 * L * NT)
            eng.wait_ge(va_out, 16 * L)


        @block.gpsimd
        def _(pool):
            def select(out, pattern, op, fill, base=0, mult=1):
                pool.affine_select(out=out, in_=out, pattern=pattern, compare_op=op, fill=fill,
                                   base=base, channel_multiplier=mult).then_inc(pool_chain, 1)
                chain[0] += 1

            chain = [0]
            for buf, value in ((ident, 0.0), (spread, 0.0), (neg_tri, -1.0), (neg_ones, -1.0),
                               (mask, 0.0), (ones_row, 1.0), (eps_col, EPS)):
                pool.memset(buf[:, :], value).then_inc(pool_chain, 1)
                chain[0] += 1
            pool.wait_ge(pool_chain, chain[0])
            select(ident[:, :], [[-1, P]], ALU.not_equal, 1.0)
            select(neg_tri[:, :], [[-1, P]], ALU.is_ge, 0.0)
            select(mask[:, :], [[1, P]], ALU.is_gt, MASKED, mult=-1)
            for b in range(4):
                if b:
                    pool.wait_ge(pool_chain, chain[0])
                select(spread[:, :], [[-1, DEC]], ALU.not_equal, 1.0, base=-32 * b)
            pool.iota(iota16[:, :], [[1, TOPK]], base=0, channel_multiplier=0,
                      allow_small_or_imprecise_dtypes=True).then_inc(pool_chain, 1)
            pool.wait_ge(pool_chain, chain[0] + 1)
            pool.memset(hid[:, :, :], 0.0).then_inc(const_made, 1)

            def gather(table, rows, where, index, landed):
                pool.indirect_dma_start(out=rows[:, where, :], out_offset=None, in_=table,
                                        in_offset=bass.IndirectOffsetOnAxis(ap=index, axis=0))\
                    .then_inc(landed[where], 16)

            def column(j, s):
                _, t, e = ITEMS[j]
                c = e * TOPK + s
                return idx_sam[:, c:c + 1] if t == SAMPLE else idx[:, t, c:c + 1]

            for stage in SCHEDULE:
                if stage[0] == "tril":
                    pool.wait_ge(params_in, PARAMS * (stage[1] + 1))
                    pool.affine_select(out=wsT[:, :, :], in_=wsT[:, :, :], pattern=[[0, H], [1, P]],
                                       compare_op=ALU.is_ge, fill=0.0, base=0, channel_multiplier=-1)\
                        .then_inc(tril_made, 1)
                elif stage[0] == "peer":
                    _, j, k = stage
                    if j < ITEM_COUNT:
                        l, t, e = ITEMS[j]
                        if k == 0:
                            if t == SAMPLE:
                                pool.wait_ge(packed, PACKED * (l + 1))
                            else:
                                pool.wait_ge(*routed.after((l, t, e)))
                        n = j * TOPK + k
                        if n >= NU:
                            pool.wait_ge(*dotted.after(steps[n - NU]))
                        gather(i["peer_u"], urows, n % NU, column(j, k), u_in)
                    if 0 < j <= ITEM_COUNT:
                        n = (j - 1) * TOPK + k
                        if n >= NV:
                            before = steps[n - NV]
                            pool.wait_ge(*added[adder(*before)].after(before))
                        gather(i["peer_v"], vrows, n % NV, column(j - 1, k), v_in)

        @block.scalar
        def _(act):
            chain = [0]

            def mark(ins):
                chain[0] += 1
                ins.then_inc(act_chain, 1)

            def settle():
                act.wait_ge(act_chain, chain[0])

            def from_bank(use, out, func=ACT.Copy, rows=P, cols=512, **kw):
                act.wait_ge(*products_done.after(use))
                act.activation(out, banks[BANK[use]][0:rows, 0:cols], func, **kw)\
                    .then_inc(act_read.sem, 1)

            def turned(use, l, gain, k0, out):
                act.wait_ge(*products_done.after(use))
                act.wait_ge(gains_in, 16)
                rows = out.shape[2]
                for k in range(4):
                    last = act.activation(out[:, k, :], banks[BANK[use]][:, P * k:P * k + rows], ACT.Copy,
                                          scale=gains[:, l, gain, k0 + k:k0 + k + 1])
                last.then_inc(act_read.sem, 1)

            def guess_root(out, x, scale):
                settle()
                mark(act.activation(out, x, ACT.Ln, bias=eps_col[0:x.shape[0], 0:1], scale=scale))
                settle()
                return act.activation(out, out, ACT.Exp, scale=-0.5)

            act.wait_ge(const_made, 1)
            for s in SCHEDULE:
                kind = s[0]
                if kind == "squares":
                    _, l, t, what = s
                    r, n = ROWS[t], NORM_NUMBER[s[1:]]
                    h_ready(act, l, t, what)
                    if n >= 2:
                        before = NORMS[n - 2]
                        if before[2] == "final":
                            act.wait_ge(y_out[n % 2], 16 * len([x for x in FINALS if NORM_NUMBER[x] < n
                                                                and NORM_NUMBER[x] % 2 == n % 2]))
                        elif before[2] != "ffn":
                            act.wait_ge(*products_done.after(("turn",) + before + (1,)))
                        else:
                            act.wait_ge(*normed.after(before))
                    mark(act.activation(xs[0:r, n % 2, :], h[0:r, t, :], ACT.Square,
                                        accum_out=ss[0:r, n % 2:n % 2 + 1]))
                    guess_root(guess[0:r, n % 2:n % 2 + 1], ss[0:r, n % 2:n % 2 + 1], 1.0 / D)\
                        .then_inc(squares_summed.sem, 1)
                elif kind in ("vaQ", "attQ", "mixQ"):
                    r, n = ROWS[s[2]], HEAD_NORM_NUMBER[s]
                    act.wait_ge(*heads_summed.after(s))
                    guess_root(guess8[0:r, n % 4, :], ss8[0:r, n % 4, :], 1.0 / DH).then_inc(heads_guessed.sem, 1)
                elif kind == "turn":
                    _, l, t, what = s
                    r, c0 = ROWS[t], place(t)[1]
                    for half in range(2):
                        use = s + (half,)
                        out = xT[:, 4 * half:4 * half + 4, c0:c0 + r]
                        if what == "ffn":
                            act.wait_ge(*products_done.after(use))
                            act.activation(out, banks[BANK[use]][:, :].rearrange("p (a n) -> p a n", a=4)[:, :, 0:r],
                                           ACT.Copy).then_inc(act_read.sem, 1)
                        else:
                            turned(use, l, 0 if what == "mix" else 2, 4 * half, out)
                elif kind == "q":
                    _, l, g, b = s
                    from_bank(s, qT[:, b, 0:GCOLS[g]], cols=GCOLS[g], scale=DH ** -0.5)
                elif kind == "k":
                    _, l, t = s
                    n = K_NUMBER[s]
                    if n >= 2:
                        act.wait_ge(k_out[n % 2], 16 * (n // 2))
                        act.wait_ge(*products_done.after(("kt",) + KS[n - 2][1:]))
                    from_bank(s, ktok[0:ROWS[t], n % 2, :], rows=ROWS[t])
                elif kind == "v":
                    _, l, t = s
                    if l > 0:
                        act.wait_ge(v_out, 16 * NT * l)
                    from_bank(s, v[0:ROWS[t], t, :], rows=ROWS[t])
                elif kind in ("ua", "va"):
                    _, l, t = s
                    at = 0 if kind == "va" else W
                    if kind == "va" and t == SAMPLE and l > 0:
                        act.wait_ge(va_out, 16 * l)
                    from_bank(s, mlp[0:ROWS[t], place(t)[0], at:at + W], ACT.Gelu, rows=ROWS[t])
                elif kind in ("attZ", "samZ"):
                    if kind == "attZ":
                        n = HEAD_NUMBER[s[1:]]
                        cols = P * (s[2] + 1)
                        parts = [(s, sp[:, n % 2, 0:cols])]
                        if n >= 2:
                            act.wait_ge(*decay_done.after(HEADS[n - 2]))
                        routes = [x[1:4] for x in SCHEDULE[:SCHEDULE.index(s)] if x[0] == "choice"]
                        if s[3] == 0 and routes:
                            act.wait_ge(*routed.after(routes[-1]))
                    else:
                        parts = [(("samZ", s[1], 0), sp[:, 0, :]),
                                 (("samZ", s[1], 1), sp[0:DEC, 1, 0:H * DEC])]
                        for e in (H - 2, H - 1):
                            act.wait_ge(*decay_done.after((s[1], SAMPLE - 1, e)))
                    for use, x in parts:
                        act.wait_ge(*products_done.after(use))
                        r, cols = x.shape
                        mark(act.activation(x, banks[BANK[use]][0:r, 0:cols], ACT.Abs))
                    settle()
                    for _, x in parts:
                        mark(act.activation(x, x, ACT.Exp, scale=-1.0))
                    settle()
                    for _, x in parts:
                        last = act.activation(x, x, ACT.Ln, bias=1.0)
                        if x is not parts[-1][1]:
                            mark(last)
                    last.then_inc(log_done.sem, 1)
                elif kind == "attE":
                    z, n = ("attZ",) + s[1:], HEAD_NUMBER[s[1:]]
                    act.wait_ge(*decay_done.after(s[1:]))
                    if n >= 2:
                        act.wait_ge(*heads_done.after(HEADS[n - 2]))
                    cols = P * (s[2] + 1)
                    act.activation(att[:, n % 2, 0:cols], banks[BANK[z]][:, 0:cols], ACT.Exp)\
                        .then_inc(act_read.sem, 1)
                elif kind == "samX":
                    act.wait_ge(*dve_read.after(("samE", s[1], 1)))
                    act.activation(att[:, 0, :], att[:, 0, :], ACT.Exp)
                    act.activation(att[0:DEC, 1, 0:H * DEC], att[0:DEC, 1, 0:H * DEC], ACT.Exp)\
                        .then_inc(sample_weights_done.sem, 1)
                elif kind == "attM":
                    _, l, t = s
                    n = MOVES.index(s[1:])
                    act.wait_ge(*heads_done.after((l,) if t == SAMPLE else (l, t, H - 1)))
                    if n:
                        act.wait_ge(*products_done.after(("attT",) + MOVES[n - 1]))
                    act.activation(osb[0:ROWS[t], :], att_out[0:ROWS[t], :], ACT.Copy).then_inc(att_moved.sem, 1)
                elif kind in ("attT", "mixT"):
                    _, l, t = s
                    k0, c0 = (0 if kind == "attT" else 4), place(t)[1]
                    turned(s, l, 1, k0, xT[:, k0:k0 + 4, c0:c0 + ROWS[t]])
                elif kind == "pq":
                    _, l, g, e = s
                    if e == 0:
                        for n in range(2):
                            act.wait_ge(k_out[n], 16 * len([x for x in KS if K_NUMBER[x] % 2 == n
                                                            and SCHEDULE.index(x) < SCHEDULE.index(s)]))
                    out = peer_queries(l, g, e, PASSES[l, g])
                    from_bank(s, out, cols=out.shape[1])
                elif kind == "score":
                    _, l, t, e = s
                    r, n = ROWS[t], ROUTE_NUMBER[s[1:]]
                    if n >= 2:
                        act.wait_ge(*halves_done.after(ROUTES[n - 2]))
                    from_bank(s, st[0:r, n % 2, :], rows=r, cols=2 * NKEYS)
                elif kind == "choice" and s[4] == 0:
                    r, n = ROWS[s[2]], ROUTE_NUMBER[s[1:4]]
                    act.wait_ge(*best_found.after(s[1:4]))
                    if n >= 2:
                        act.wait_ge(*routed.after(ROUTES[n - 2]))
                    act.activation(ex[0:r, n % 2, :], best[0:r, n % 2, :], ACT.Exp, bias=negm[0:r, n % 2:n % 2 + 1],
                                   accum_out=esum[0:r, n % 2, 0:1]).then_inc(exps_done.sem, 1)
                elif kind == "ple":
                    _, l, t, c = s
                    from_bank(s, mlp[0:ROWS[t], place(t)[0], 512 * c:512 * c + 512], rows=ROWS[t])
                elif kind == "gate":
                    _, l, t, c = s
                    n = GATE_NUMBER[s[1:]]
                    if n >= 2:
                        act.wait_ge(*gated.after(GATES[n - 2]))
                    from_bank(s, sp[0:ROWS[t], n % 2, :], ACT.Sigmoid, rows=ROWS[t])
                elif kind == "peer":
                    _, j, k = s
                    if k == 0 and 0 < j <= ITEM_COUNT:
                        act.wait_ge(*dotted.after((j - 1, TOPK - 1)))
                        act.activation(act_hid[:, (j - 1) % 2, :], hid[:, (j - 1) % 2, :], ACT.Gelu)\
                            .then_inc(gelu_done.sem, 1)

        @block.vector
        def _(dve):
            chain = [0]

            def mark(ins):
                chain[0] += 1
                ins.then_inc(dve_chain, 1)

            def settle():
                dve.wait_ge(dve_chain, chain[0])

            def link(ins):
                mark(ins)
                settle()

            def root(y, x, scale):
                r, n = x.shape
                half = newton[0:r, 0:n]
                mark(dve.tensor_scalar(x, x, scale, EPS, ALU.mult, ALU.add))
                link(dve.scalar_tensor_tensor(out=half, in0=y, scalar=-0.5, in1=y, op0=ALU.mult, op1=ALU.mult))
                link(dve.tensor_tensor(half, half, x, ALU.mult))
                link(dve.scalar_tensor_tensor(out=y, in0=half, scalar=1.5, in1=y, op0=ALU.add, op1=ALU.mult))

            def squares_free(s):
                n = HEAD_NORM_NUMBER[s]
                if n:
                    dve.wait_ge(*heads_summed.after(HEAD_NORMS[n - 1]))

            def head_squares(s, x):
                r = x.shape[0]
                link(dve.tensor_tensor(sq[0:r, :], x, x, ALU.mult))
                dve.tensor_reduce(ss8[0:r, HEAD_NORM_NUMBER[s] % 4, :], sq[0:r, :].rearrange("p (a n) -> p a n", a=H),
                                  AX_X, ALU.add).then_inc(heads_summed.sem, 1)

            def head_norm(s, x):
                r, q = x.shape[0], (s[0][:-1] + "Q",) + s[1:]
                n = HEAD_NORM_NUMBER[q]
                dve.wait_ge(*heads_guessed.after(q))
                root(guess8[0:r, n % 4, :], ss8[0:r, n % 4, :], 1.0 / DH)
                x3 = x.rearrange("p (a n) -> p a n", a=H)
                return dve.tensor_tensor(x3, x3, guess8[0:r, n % 4, :].unsqueeze(2).to_broadcast([r, H, DH]), ALU.mult)

            def top16(step, out, where, x, scratch):
                settle()
                for a, w, b, c in zip(out, where, x, scratch):
                    if step == 0:
                        mark(dve.max(a[:, 0:8], b))
                    elif step == 1:
                        mark(dve.max_index(w[:, 0:8], a[:, 0:8], b))
                        mark(dve.match_replace(c, a[:, 0:8], b, BELOW))
                    elif step == 2:
                        mark(dve.max(a[:, 8:16], c))
                    else:
                        mark(dve.max_index(w[:, 8:16], a[:, 8:16], c))

            def best_of_halves(s):
                _, l, t, e, step = s
                r, n = ROWS[t], ROUTE_NUMBER[s[1:4]]
                if step == 0:
                    dve.wait_ge(*act_read.after(("score", l, t, e)))
                    if n:
                        dve.wait_ge(*halves_done.after(ROUTES[n - 1]))
                top16(step, [top[0:r, p, :] for p in range(2)], [topi[0:r, n % 3, p, :] for p in range(2)],
                      [st[0:r, n % 2, NKEYS * p:NKEYS * p + NKEYS] for p in range(2)],
                      [rep[0:r, p, :] for p in range(2)])
                if step == 3:
                    full = [r, TOPK, TOPK]
                    dve.tensor_tensor(cand[0:r], top[0:r, 0, :].unsqueeze(2).to_broadcast(full),
                                      top[0:r, 1, :].unsqueeze(1).to_broadcast(full), ALU.add)\
                        .then_inc(halves_done.sem, 1)

            def best_of_sums(s):
                _, l, t, e, step = s
                r, n = ROWS[t], ROUTE_NUMBER[s[1:4]]
                if step == 0:
                    dve.wait_ge(*halves_done.after(s[1:4]))
                    if n >= 2:
                        dve.wait_ge(*exps_done.after(ROUTES[n - 2]))
                flat = [x[0:r].rearrange("p a b -> p (a b)") for x in (cand, cand2)]
                top16(step, [best[0:r, n % 2, :]], [pos[0:r, :]], [flat[0]], [flat[1]])
                if step == 2:
                    dve.tensor_scalar(negm[0:r, n % 2:n % 2 + 1], best[0:r, n % 2, 0:1], -1.0, None, ALU.mult)\
                        .then_inc(best_found.sem, 1)
                    top16(3, [best[0:r, n % 2, :]], [pos[0:r, :]], [flat[0]], [flat[1]])

            def choose(s):
                _, l, t, e, step = s
                r, n = ROWS[t], ROUTE_NUMBER[s[1:4]]
                full = [r, TOPK, TOPK]
                hot3 = [hot[0:r, p, :].rearrange("p (a b) -> p a b", a=TOPK) for p in range(2)]
                settle()
                if step == 0:
                    if n:
                        dve.wait_ge(*routed.after(ROUTES[n - 1]))
                    mark(dve.tensor_scalar(pos2[0:r, 0, :], pos[0:r, :], 4, None, ALU.logical_shift_right))
                    mark(dve.tensor_scalar(pos2[0:r, 1, :], pos[0:r, :], TOPK - 1, None, ALU.bitwise_and))
                elif step == 1:
                    for p in range(2):
                        mark(dve.tensor_tensor(hot3[p], iota16[0:r, :].unsqueeze(1).to_broadcast(full),
                                               pos2[0:r, p, :].unsqueeze(2).to_broadcast(full), ALU.is_equal))
                elif step == 2:
                    for p in range(2):
                        mark(dve.tensor_tensor(hot3[p], hot3[p],
                                               topi[0:r, n % 3, p, :].unsqueeze(1).to_broadcast(full), ALU.mult))
                    dve.wait_ge(*exps_done.after(s[1:4]))
                    mark(dve.reciprocal(esum[0:r, n % 2, 1:2], esum[0:r, n % 2, 0:1]))
                else:
                    for p in range(2):
                        mark(dve.tensor_reduce(part[0:r, p, :], hot3[p], AX_X, ALU.add))
                    at = slice(e * TOPK, e * TOPK + TOPK)
                    mark(dve.tensor_scalar(gate[0:r, t, at], ex[0:r, n % 2, :], esum[0:r, n % 2, 1:2], None, ALU.mult))
                    settle()
                    mark(dve.tensor_scalar(part[0:r, 0, :], part[0:r, 0, :], float(NKEYS), float(l * EXPERTS),
                                           ALU.mult, ALU.add))
                    settle()
                    dve.tensor_tensor(idx[0:r, t, at], part[0:r, 0, :], part[0:r, 1, :], ALU.add)\
                        .then_inc(routed.sem, 1)

            def dot(j, k):
                if j == ITEM_COUNT:
                    return
                l, t, _ = ITEMS[j]
                if k == 0 and t == SAMPLE:
                    dve.wait_ge(packed, PACKED * (l + 1))
                if k == 0 and j >= 2:
                    dve.wait_ge(*gelu_done.after(j - 2))
                n = j * TOPK + k
                dve.wait_ge(u_in[n % NU], 16 * (n // NU + 1))
                row = urows[:, n % NU, :]
                dve.tensor_tensor_reduce(row, row, xn2[:, t, :], 1.0, 0.0, ALU.mult, ALU.add,
                                         hid[:, j % 2, k:k + 1]).then_inc(dotted.sem, 1)

            def make_amounts(j):
                if j < 0:
                    return
                _, t, e = ITEMS[j]
                at = slice(e * TOPK, e * TOPK + TOPK)
                dve.wait_ge(*gelu_done.after(j))
                dve.tensor_tensor(amount[:, j % 2, :], act_hid[:, j % 2, :],
                                  gate_sam[:, at] if t == SAMPLE else gate[:, t, at], ALU.mult)\
                    .then_inc(amounts_done.sem, 1)
                dve.wait_ge(*amounts_done.after(j))

            def make_diag(j, q):
                if j < 0:
                    return
                t = ITEMS[j][1]
                m = 4 * j + q
                if m >= ND:
                    dve.wait_ge(*added["pe"].after(steps[QUARTER * (m - ND + 1) - 1]))
                full = [P, QUARTER, ROWS[t]]
                where = spread if t == SAMPLE else ident
                dve.tensor_tensor(diag[:, m % ND, :, 0:ROWS[t]], where[:, :].unsqueeze(1).to_broadcast(full),
                                  amount[:, j % 2, QUARTER * q:QUARTER * q + QUARTER].unsqueeze(2).to_broadcast(full),
                                  ALU.mult).then_inc(diag_made.sem, 1)

            def add_row(j, k):
                t = ITEMS[j][1]
                n = j * TOPK + k
                dve.wait_ge(v_in[n % NV], 16 * (n // NV + 1))
                if added["dve"].count[j, k] > 1:
                    dve.wait_ge(added["dve"].sem, added["dve"].count[j, k] - 1)
                dve.scalar_tensor_tensor(out=h[:, t, :], in0=vrows[:, n % NV, :], scalar=amount[:, j % 2, k:k + 1],
                                         in1=h[:, t, :], op0=ALU.mult, op1=ALU.add).then_inc(added["dve"].sem, 1)

            def add_experts(j):
                t = ITEMS[j][1]
                dve.wait_ge(*added["pe"].after((j, TOPK - 1)))
                own = [added["dve"].count[x] for x in steps if x in added["dve"].count and x[0] <= j]
                if own:
                    dve.wait_ge(added["dve"].sem, own[-1])
                for c in range(2):
                    x = h[0:ROWS[t], t, 512 * c:512 * c + 512]
                    last = dve.tensor_tensor(x, x, experts[c][0:ROWS[t], :], ALU.add)
                    if c == 0:
                        mark(last)
                last.then_inc(experts_added.sem, 1)

            dve.wait_ge(const_made, 1)
            for s in SCHEDULE:
                kind = s[0]
                if kind == "scale":
                    _, l, t, what = s
                    r, n = ROWS[t], NORM_NUMBER[s[1:]]
                    dve.wait_ge(*squares_summed.after(s[1:]))
                    scale = guess[0:r, n % 2:n % 2 + 1]
                    root(scale, ss[0:r, n % 2:n % 2 + 1], 1.0 / D)
                    if what in ("ffn", "final"):
                        if what == "ffn":
                            dve.wait_ge(params_in, PARAMS * (l + 1))
                        else:
                            dve.wait_ge(final_in, 16)
                        out = xn2[0:r, t, :] if what == "ffn" else xs[0:r, n % 2, :]
                        dve.scalar_tensor_tensor(out=out, in0=h[0:r, t, :], scalar=scale, in1=g_row[0:r, :],
                                                 op0=ALU.mult, op1=ALU.mult).then_inc(normed.sem, 1)
                    else:
                        dve.tensor_scalar(xs[0:r, n % 2, :], h[0:r, t, :], scale, None, ALU.mult)\
                            .then_inc(normed.sem, 1)
                elif kind == "ktE":
                    _, l, t = s
                    use = ("kt", l, t)
                    dve.wait_ge(*products_done.after(use))
                    dve.tensor_copy(kT[:, :, P * t:P * t + ROWS[t]],
                                    banks[BANK[use]][:, :].rearrange("p (a n) -> p a n", a=4)[:, :, 0:ROWS[t]])\
                        .then_inc(dve_read.sem, 1)
                elif kind == "vaQ":
                    _, l, t = s
                    dve.wait_ge(*act_read.after(("va", l, t)))
                    squares_free(s)
                    head_squares(s, mlp[0:ROWS[t], place(t)[0], 0:W])
                elif kind == "vaN":
                    _, l, t = s
                    r = ROWS[t]
                    dve.wait_ge(params_in, PARAMS * (l + 1))
                    x = mlp[0:r, place(t)[0], 0:W]
                    link(head_norm(s, x))
                    dve.tensor_tensor(x, x, g_av[0:r, :], ALU.mult).then_inc(va_normed.sem, 1)
                elif kind == "attS":
                    z, cols = ("attZ",) + s[1:], P * (s[2] + 1)
                    x = sp[:, HEAD_NUMBER[s[1:]] % 2, 0:cols]
                    dve.wait_ge(*log_done.after(s[1:]))
                    dve.scalar_tensor_tensor(out=x, in0=banks[BANK[z]][:, 0:cols], scalar=0.0, in1=x,
                                             op0=ALU.max, op1=ALU.add).then_inc(softplus_done.sem, 1)
                elif kind == "samS":
                    l = s[1]
                    dve.wait_ge(*log_done.after((l,)))
                    for e in (H - 2, H - 1):
                        dve.wait_ge(*heads_done.after((l, SAMPLE - 1, e)))
                    for b, r, cols in SAMPLE_PARTS:
                        x = sp[0:r, b, 0:cols]
                        last = dve.scalar_tensor_tensor(out=x, in0=banks[BANK["samZ", l, b]][0:r, 0:cols], scalar=0.0,
                                                        in1=x, op0=ALU.max, op1=ALU.add)
                        if b == 0:
                            mark(last)
                    last.then_inc(softplus_done.sem, 1)
                    for b, r, cols in SAMPLE_PARTS:
                        dve.tensor_copy(att[0:r, b, 0:cols], banks[BANK["samZ", l, b]][0:r, 0:cols])\
                            .then_inc(dve_read.sem, 1)
                elif kind == "samX":
                    l = s[1]
                    dve.wait_ge(*dve_read.after(("samZ", l, 1)))
                    for b, r, cols in SAMPLE_PARTS:
                        use = ("samE", l, b)
                        dve.wait_ge(*products_done.after(use))
                        x = att[0:r, b, 0:cols]
                        dve.tensor_tensor(x, x, banks[BANK[use]][0:r, 0:cols], ALU.add)\
                            .then_inc(dve_read.sem, 1)
                elif kind == "attQ":
                    _, l, t = s
                    dve.wait_ge(*att_moved.after(s[1:]))
                    squares_free(s)
                    head_squares(s, osb[0:ROWS[t], :])
                elif kind == "attN":
                    _, l, t = s
                    head_norm(s, osb[0:ROWS[t], :]).then_inc(att_normed.sem, 1)
                elif kind == "mixQ":
                    _, l, t = s
                    r = ROWS[t]
                    use = ("mix", l, t)
                    dve.wait_ge(*products_done.after(use))
                    squares_free(s)
                    out = sq[0:r, :].rearrange("p (a n) -> p a n", a=H)
                    dve.tensor_tensor(out, banks[BANK[use]][0:r, :].rearrange("p (a n) -> p a n", a=H),
                                      b_sp[0:r, :].unsqueeze(2).to_broadcast([r, H, DH]), ALU.add)\
                        .then_inc(dve_read.sem, 1)
                    dve.wait_ge(*dve_read.after(use))
                    dve.wait_ge(*act_read.after(("ua", l, t)))
                    u = mlp[0:r, place(t)[0], W:2 * W]
                    link(dve.tensor_tensor(u, u, sq[0:r, :], ALU.mult))
                    head_squares(s, u)
                elif kind == "mixN":
                    _, l, t = s
                    head_norm(s, mlp[0:ROWS[t], place(t)[0], W:2 * W]).then_inc(mix_done.sem, 1)
                elif kind == "woutA":
                    _, l, t, c = s
                    use = ("wout", l, t, c)
                    if l == 0 and c == 0:
                        dve.wait_ge(h_in[t], 16)
                    dve.wait_ge(*products_done.after(use))
                    x = h[0:ROWS[t], t, 512 * c:512 * c + 512]
                    dve.tensor_tensor(x, x, banks[BANK[use]][0:ROWS[t], :], ALU.add).then_inc(dve_read.sem, 1)
                elif kind == "halves":
                    best_of_halves(s)
                elif kind == "sums":
                    best_of_sums(s)
                elif kind == "choice":
                    choose(s)
                elif kind == "gateA":
                    _, l, t, c = s
                    r = ROWS[t]
                    dve.wait_ge(*act_read.after(("gate", l, t, c)))
                    dve.wait_ge(*act_read.after(("ple", l, t, c)))
                    x = sp[0:r, GATE_NUMBER[s[1:]] % 2, :]
                    link(dve.tensor_tensor(x, x, mlp[0:r, place(t)[0], 512 * c:512 * c + 512], ALU.mult))
                    y = h[0:r, t, 512 * c:512 * c + 512]
                    dve.tensor_tensor(y, y, x, ALU.add).then_inc(gated.sem, 1)
                elif kind == "peer":
                    _, j, k = s
                    if j < ITEM_COUNT:
                        dot(j, k)
                    if k == ADDED and j >= 2 and ITEMS[j - 2][2] == items_in_tile(ITEMS[j - 2][1]) - 1:
                        add_experts(j - 2)
                    if 0 < j <= ITEM_COUNT:
                        if k == 1:
                            make_amounts(j - 1)
                            make_diag(j - 1, 0)
                        elif k % QUARTER == 3 and k < TOPK - 1:
                            make_diag(j - 1, k // QUARTER + 1)
                        if k and adder(j - 1, k - 1) == "dve":
                            add_row(j - 1, k - 1)

        @block.tensor
        def _(pe):
            def take(use):
                if use in TAKEN_BEFORE:
                    before = TAKEN_BEFORE[use]
                    pe.wait_ge(*bank_read[RELEASED_BY[before]].after(before))
                return banks[BANK[use]]

            chain = [0]

            def rows_change(ins):
                chain[0] += 1
                ins.then_inc(pe_chain, 1)
                pe.wait_ge(pe_chain, chain[0])

            def unit(s):
                n = UNIT_NUMBER[weight_unit(s)]
                pe.wait_ge(w_in[n % NW], 16 * (n // NW + 1))
                return weights[:, n % NW, :].rearrange("p (k n) -> p k n", k=KD)

            def turn(use, blocks):
                b = take(use)
                for k, x in enumerate(blocks):
                    r = x.shape[0]
                    last = pe.transpose(b[:, P * k:P * k + r], x, ident[0:r, 0:r])
                last.then_inc(products_done.sem, 1)

            def turned_ready(kind, l, tiles):
                for t in tiles:
                    pe.wait_ge(*act_read.after(("turn", l, t, kind, 1)))

            begun = set()

            def blocks_now(s, part):
                if part:
                    begun.add(s)
                    take(s)
                    return range(KD // 2)
                if s in begun:
                    return range(KD // 2, KD)
                take(s)
                return range(KD)

            def by_token(s, x_cols, r, part, stop=True):
                w = unit(s)
                b = banks[BANK[s]]
                for k in blocks_now(s, part):
                    last = pe.matmul(b[0:r, :], xT[:, k, x_cols:x_cols + r], w[:, k, :],
                                     start=(k == 0), stop=(stop and k == KD - 1))
                if not part and stop:
                    last.then_inc(products_done.sem, 1)

            def by_column(s, block, cols, part, c0=0):
                w = unit(s)
                b = banks[BANK[s]]
                for k in blocks_now(s, part):
                    last = pe.matmul(b[:, 0:cols], w[:, k, P * block:P * block + P], xT[:, k, c0:c0 + cols],
                                     start=(k == 0), stop=(k == KD - 1))
                if not part:
                    last.then_inc(products_done.sem, 1)

            def add_rows(j, k):
                l, t, e = ITEMS[j]
                n, q = j * TOPK + k, k // QUARTER
                if k == 0 and e == 0 and (l, t) != tiles_in_order[0]:
                    pe.wait_ge(*experts_added.after(tiles_in_order[tiles_in_order.index((l, t)) - 1]))
                pe.wait_ge(*diag_made.after((j, q)))
                pe.wait_ge(v_in[n % NV], 16 * (n // NV + 1))
                first = e == 0 and k == 0
                final = e == items_in_tile(t) - 1 and k == TOPK - 1
                for c in range(2):
                    last = pe.matmul(experts[c][0:ROWS[t], :], diag[:, (4 * j + q) % ND, k % QUARTER, 0:ROWS[t]],
                                     vrows[:, n % NV, 512 * c:512 * c + 512], start=first, stop=final)
                last.then_inc(added["pe"].sem, 1)

            pe.wait_ge(const_made, 1)
            for s in SCHEDULE:
                part = s[0] == "part"
                s = s[1:] if part else s
                kind = s[0]
                if kind == "turn":
                    _, l, t, what = s
                    r = ROWS[t]
                    pe.wait_ge(*normed.after(s[1:]))
                    src = xn2[0:r, t, :] if what == "ffn" else xs[0:r, NORM_NUMBER[s[1:]] % 2, :]
                    for half in range(2):
                        turn(s + (half,), [src[:, P * k:P * k + P] for k in range(4 * half, 4 * half + 4)])
                elif kind == "q":
                    _, l, g, b = s
                    if b == 0:
                        turned_ready("mix", l, GROUPS[g])
                    by_column(s, b, GCOLS[g], part)
                elif kind in ("k", "v", "ua", "va"):
                    _, l, t = s
                    by_token(s, place(t)[1], ROWS[t], part)
                elif kind == "kt":
                    _, l, t = s
                    pe.wait_ge(*act_read.after(("k", l, t)))
                    n = K_NUMBER["k", l, t]
                    turn(s, [ktok[0:ROWS[t], n % 2, P * k:P * k + P] for k in range(4)])
                elif kind == "attZ":
                    _, l, t, e = s
                    c0, lo = place(t)[1], DH * (e % 2)
                    if e == 0:
                        pe.wait_ge(*act_read.after(("q", l, group_of(t), 3)))
                        pe.wait_ge(*dve_read.after(("kt", l, t)))
                    b = take(s)
                    for kb in range(t + 1):
                        pe.matmul(b[:, P * kb:P * kb + P], kT[lo:lo + DH, e // 2, P * kb:P * kb + P],
                                  qT[lo:lo + DH, e // 2, c0:c0 + P], start=(kb == 0), stop=False,
                                  skip_group_check=True)
                    pe.matmul(b[:, P * t:P * t + P], ident[:, :], mask[:, :], start=False, stop=True,
                              skip_group_check=True).then_inc(products_done.sem, 1)
                elif kind == "attE":
                    _, l, t, e = s
                    z = ("attZ", l, t, e)
                    b = banks[BANK[z]]
                    x = sp[:, HEAD_NUMBER[s[1:]] % 2, :]
                    pe.wait_ge(*softplus_done.after(s[1:]))
                    last = pe.matmul(b[:, 0:P * (t + 1)], neg_tri[:, :], x[:, 0:P * (t + 1)], start=False,
                                     stop=(t == 0), skip_group_check=True)
                    for kb in range(1, t + 1):
                        rhs = x[:, P * kb:P * kb + P].unsqueeze(1).to_broadcast([P, kb, P])
                        last = pe.matmul(b[:, 0:P * kb].rearrange("p (a n) -> p a n", a=kb), neg_ones[:, :], rhs,
                                         start=False, stop=(kb == t), skip_group_check=True)
                    last.then_inc(decay_done.sem, 1)
                elif kind == "attP":
                    _, l, t, e = s
                    z = ("attZ", l, t, e)
                    pe.wait_ge(*act_read.after(z))
                    if e == 0:
                        pe.wait_ge(*act_read.after(("v", l, t)))
                        n = MOVES.index((l, t))
                        if n:
                            pe.wait_ge(*att_moved.after(MOVES[n - 1]))
                    for kb in range(t + 1):
                        last = pe.matmul(att_out[:, DH * e:DH * e + DH],
                                         att[:, HEAD_NUMBER[s[1:]] % 2, P * kb:P * kb + P],
                                         v[:, kb, DH * e:DH * e + DH], start=(kb == 0), stop=(kb == t))
                    last.then_inc(heads_done.sem, 1)
                elif kind == "samZ":
                    l = s[1]
                    c0 = place(SAMPLE)[1]
                    pe.wait_ge(params_in, PARAMS * (l + 1))
                    pe.wait_ge(*dve_read.after(("kt", l, SAMPLE)))
                    b = take(("samZ", l, 0))
                    for half in range(2):
                        lo = DH * half
                        if half:
                            rows_change(last)
                        for kb in range(2):
                            for e in range(half, H, 2):
                                at = (kb * H + e) * DEC
                                last = pe.matmul(b[:, at:at + DEC], kcT[lo:lo + DH, e // 2, P * kb:P * kb + P],
                                                 qT[lo:lo + DH, e // 2, c0:c0 + DEC], start=True, stop=True)
                    last.then_inc(products_done.sem, 1)
                    b = take(("samZ", l, 1))
                    for half in range(2):
                        lo = DH * half
                        if half:
                            rows_change(last)
                        for e in range(half, H, 2):
                            last = pe.matmul(b[0:DEC, DEC * e:DEC * e + DEC], kT[lo:lo + DH, e // 2, SEQ:SEQ + DEC],
                                             qT[lo:lo + DH, e // 2, c0:c0 + DEC], start=(e == 0), stop=False,
                                             skip_group_check=True)
                    pe.matmul(b[0:DEC, 0:H * DEC].rearrange("p (a n) -> p a n", a=H), ident[0:DEC, 0:DEC],
                              mask[0:DEC, 0:DEC].unsqueeze(1).to_broadcast([DEC, H, DEC]), start=False, stop=True,
                              skip_group_check=True).then_inc(products_done.sem, 1)
                elif kind == "samE":
                    l = s[1]
                    pe.wait_ge(*softplus_done.after(s[1:]))
                    new = sp[0:DEC, 1, 0:H * DEC]
                    past = [sp[:, 0, 0:256], sp[:, 0, 256:512]]
                    b = take(("samE", l, 0))
                    for kb in range(2):
                        out = b[:, 256 * kb:256 * kb + 256]
                        pe.matmul(out, neg_tri[:, :], past[kb], start=True, stop=False)
                        if kb == 0:
                            pe.matmul(out, neg_ones[:, :], past[1], start=False, stop=False)
                        last = pe.matmul(out, neg_ones[0:DEC, :], new, start=False, stop=True)
                    last.then_inc(products_done.sem, 1)
                    b = take(("samE", l, 1))
                    pe.matmul(b[0:DEC, 0:H * DEC], neg_tri[0:DEC, 0:DEC], new, start=True, stop=True)\
                        .then_inc(products_done.sem, 1)
                elif kind == "samP":
                    l = s[1]
                    pe.wait_ge(*sample_weights_done.after((l,)))
                    pe.wait_ge(*act_read.after(("v", l, SAMPLE)))
                    pe.wait_ge(*att_moved.after((l, SAMPLE - 1)))
                    for e in range(H):
                        out = att_out[0:DEC, DH * e:DH * e + DH]
                        for kb in range(2):
                            at = (kb * H + e) * DEC
                            pe.matmul(out, att[:, 0, at:at + DEC], vc[:, kb, DH * e:DH * e + DH],
                                      start=(kb == 0), stop=False)
                        last = pe.matmul(out, att[0:DEC, 1, DEC * e:DEC * e + DEC],
                                         v[0:DEC, SAMPLE, DH * e:DH * e + DH], start=False, stop=True)
                    last.then_inc(heads_done.sem, 1)
                elif kind == "attT":
                    _, l, t = s
                    pe.wait_ge(*att_normed.after(s[1:]))
                    turn(s, [osb[0:ROWS[t], P * k:P * k + P] for k in range(4)])
                elif kind == "mix":
                    _, l, t = s
                    r, at = ROWS[t], place(t)[0]
                    pe.wait_ge(*va_normed.after(s[1:]))
                    pe.wait_ge(tril_made, l + 1)
                    b = take(s)
                    for e in range(H):
                        last = pe.matmul(b[0:r, DH * e:DH * e + DH], wsT[0:r, e, 0:r],
                                         mlp[0:r, at, DH * e:DH * e + DH], start=True, stop=True)
                    last.then_inc(products_done.sem, 1)
                elif kind == "mixT":
                    _, l, t = s
                    pe.wait_ge(*mix_done.after(s[1:]))
                    turn(s, [mlp[0:ROWS[t], place(t)[0], W + P * k:W + P * k + P] for k in range(4)])
                elif kind == "wout":
                    _, l, t, c = s
                    pe.wait_ge(*act_read.after(("attT", l, t)))
                    pe.wait_ge(*act_read.after(("mixT", l, t)))
                    by_token(s, place(t)[1], ROWS[t], part)
                elif kind == "pq":
                    _, l, g, e = s
                    if e == 0:
                        turned_ready("ffn", l, PASSES[l, g])
                    tiles = PASSES[l, g]
                    by_column(s, e % 4, sum(ROWS[t] for t in tiles), part, place(tiles[0])[1])
                elif kind == "score":
                    _, l, t, e = s
                    r = ROWS[t]
                    pe.wait_ge(*act_read.after(("pq", l, pass_of(l, t), e)))
                    queries = peer_queries(l, pass_of(l, t), e, [t])
                    n = UNIT_NUMBER[weight_unit(s)]
                    pe.wait_ge(w_in[n % NW], 16 * (n // NW + 1))
                    subT = weights[:, n % NW, 0:H * NKEYS].rearrange("p (a n) -> p a n", a=H)
                    b = take(s)
                    for p in range(2):
                        lo = DH * p
                        if p:
                            rows_change(last)
                        last = pe.matmul(b[0:r, NKEYS * p:NKEYS * p + NKEYS], queries[lo:lo + DH, :],
                                         subT[lo:lo + DH, e, :], start=True, stop=True)
                    last.then_inc(products_done.sem, 1)
                elif kind == "ple":
                    _, l, t, c = s
                    r, c0 = ROWS[t], place(t)[1]
                    n = UNIT_NUMBER[weight_unit(s)]
                    pe.wait_ge(w_in[n % NW], 16 * (n // NW + 1))
                    pe.wait_ge(p_in, 16 * (2 * l + group_of(t) + 1))
                    pT = tokens_p(n, group_of(t))
                    w = weights[:, n % NW, 0:2 * D].rearrange("p (k n) -> p k n", k=2)
                    b = take(s)
                    for k in range(2):
                        last = pe.matmul(b[0:r, :], pT[:, k, c0:c0 + r], w[:, k, 512 * c:512 * c + 512],
                                         start=(k == 0), stop=(k == 1))
                    last.then_inc(products_done.sem, 1)
                elif kind == "gate":
                    _, l, t, c = s
                    r, c0 = ROWS[t], place(t)[1]
                    if c == 0:
                        turned_ready("ple", l, [t])
                    by_token(s, c0, r, part, stop=False)
                    if not part:
                        pe.wait_ge(bias_in, 16 * (2 * l + group_of(t) + 1))
                        pe.matmul(banks[BANK[s]][0:r, :], ones_row[0:1, 0:r], b_gate[0:1, 512 * c:512 * c + 512],
                                  start=False, stop=True).then_inc(products_done.sem, 1)
                elif kind == "peer":
                    _, j, k = s
                    for k in {0: [], 1: [0, 1]}.get(k, [k]):
                        if 0 < j <= ITEM_COUNT and adder(j - 1, k) == "pe":
                            add_rows(j - 1, k)


def kernel(x_prompt, x_sample, cache_k, cache_v, p_prompt, p_sample, g_mix, w_in, g_sb_out, w_spatial,
           b_spatial, g_a_v, g_a_out, w_out, g_ffn, w_peer_q, peer_sub_keys, peer_u, peer_v, g_ple,
           w_ple_gate, b_ple_gate, w_ple, g_final):
    import concourse.bacc as bacc
    from concourse.bass_utils import run_bass_kernel_spmd

    def blocks(w, n):
        w = np.asarray(w)
        layers, k, cols = w.shape
        return w.reshape(layers, k // P, P, cols // n, n).transpose(0, 3, 2, 1, 4).reshape(layers, cols // n, P, -1)

    def by_block(g):
        return np.asarray(g).reshape(L, KD, P).transpose(2, 0, 1)

    p_all = np.concatenate([np.asarray(p_prompt)[:, 0], np.asarray(p_sample)[:, 0]], axis=1)
    g_out = np.concatenate([np.asarray(g_sb_out).reshape(L, W), np.asarray(g_a_out).reshape(L, W)], axis=1)
    arrays = {
        "x": np.concatenate([np.asarray(x_prompt)[0], np.asarray(x_sample)[0]], axis=0),
        "cache_kT": np.asarray(cache_k)[:, 0].reshape(L, PAST, 4, P).transpose(0, 3, 2, 1).reshape(L, P, -1),
        "cache_v": np.asarray(cache_v)[:, 0].reshape(L, PAST, W),
        "pT": p_all.transpose(0, 2, 1).reshape(L, 2, P, SEQ + DEC).transpose(0, 2, 1, 3),
        "gains": np.stack([by_block(g_mix), by_block(g_out), by_block(g_ple)], axis=2).reshape(P, -1),
        "w_in": blocks(w_in, 512),
        "w_out": blocks(w_out, 512),
        "w_peer_q": blocks(w_peer_q, 512),
        "w_ple_gate": blocks(w_ple_gate, 512),
        "w_ple": blocks(w_ple, D),
        "w_spatialT": np.asarray(w_spatial).transpose(0, 3, 1, 2).reshape(L, P, -1),
        "b_spatialT": np.asarray(b_spatial).transpose(0, 2, 1),
        "g_a_v": np.asarray(g_a_v).reshape(L, W),
        "g_ffn": np.asarray(g_ffn),
        "sub_keysT": np.asarray(peer_sub_keys).transpose(0, 2, 4, 1, 3).reshape(L, 1, P, -1),
        "peer_u": np.asarray(peer_u).reshape(L * EXPERTS, D),
        "peer_v": np.asarray(peer_v).reshape(L * EXPERTS, D),
        "b_ple_gate": np.asarray(b_ple_gate),
        "g_final": np.asarray(g_final).reshape(1, D),
    }
    arrays = {n: np.ascontiguousarray(a) for n, a in arrays.items()}
    nc = bacc.Bacc("TRN2", target_bir_lowering=False, num_devices=1)
    ins = {n: nc.dram_tensor(f"in_{n}", a.shape, F32, kind="ExternalInput").ap() for n, a in arrays.items()}
    shapes = {"y": (SEQ + DEC, D), "k": (L, SEQ + DEC, W), "v": (L, SEQ + DEC, W), "va": (L, DEC, W)}
    outs = {n: nc.dram_tensor(f"out_{n}", s, F32, kind="ExternalOutput").ap() for n, s in shapes.items()}
    encoder(nc, ins, outs)
    r = run_bass_kernel_spmd(nc, [{f"in_{n}": a for n, a in arrays.items()}], core_ids=[0]).results[0]
    y, k, v, va = (np.asarray(r[f"out_{n}"]) for n in shapes)
    heads = lambda a: a.reshape(L, 1, -1, H, DH)
    return (y[None, :SEQ], y[None, SEQ:], heads(k[:, :SEQ]), heads(v[:, :SEQ]), heads(k[:, SEQ:]),
            heads(v[:, SEQ:]), heads(va))
```
